# Optimizing a Trainium2 kernel written in Bass

```python
import math
import jax
import jax.numpy as jnp
from jax import lax
import numpy as np

D_MODEL = 1024
BATCH = 1
SEQ = 512
DEPTH = 2

F32 = jnp.float32
EPS = 1e-6
D_MIX = 2 * D_MODEL
GROUP_WIDTH = D_MIX // 4
CONV_WIDTH = 4
CHUNK = 64
GDN_HEADS = 4
GDN_DK = 128
GDN_DV = GROUP_WIDTH // GDN_HEADS
HGRN_HEADS = 4
HGRN_DK = 128
HGRN_DV = GROUP_WIDTH // HGRN_HEADS
LRU_WIDTH = GROUP_WIDTH
LRU_BLOCKS = 4
LRU_BLOCK_W = LRU_WIDTH // LRU_BLOCKS
LRU_C = 8.0
GLA_HEADS = 4
GLA_DK = 64
GLA_DV = GROUP_WIDTH // GLA_HEADS
GLA_GATE_RANK = 16
GLA_GATE_TAU = 16.0
PEER_HEADS = 8
PEER_NKEYS = 128
PEER_EXPERTS = PEER_NKEYS * PEER_NKEYS
PEER_QDIM = 256
PEER_TOPK = 16
PEER_TOKEN_BLOCK = 128
IN_SIZES = (
    GDN_HEADS * GDN_DK, GDN_HEADS * GDN_DK, GDN_HEADS * GDN_DV, GDN_HEADS * GDN_DV, GDN_HEADS, GDN_HEADS,
    HGRN_HEADS * HGRN_DK, HGRN_HEADS * HGRN_DK, HGRN_HEADS * HGRN_DV, HGRN_HEADS * HGRN_DV,
    LRU_WIDTH, LRU_WIDTH,
    GLA_HEADS * GLA_DK, GLA_HEADS * GLA_DK, GLA_HEADS * GLA_DV, GLA_HEADS * GLA_DV, GLA_GATE_RANK,
)
D_IN = sum(IN_SIZES)

kernel_name = "hybrid_parallel_heads_peer_block"

def rmsnorm(x, w):
    xf = x.astype(F32)
    y = xf * lax.rsqrt(jnp.mean(xf * xf, axis=-1, keepdims=True) + EPS) * w.astype(F32)
    return y.astype(x.dtype)

def l2norm(t):
    return t * lax.rsqrt(jnp.sum(t * t, axis=-1, keepdims=True) + EPS)

def to_heads(t, n_heads):
    b, s, _ = t.shape
    return t.reshape(b, s, n_heads, -1).transpose(0, 2, 1, 3)

def causal_depthwise_conv(x, w):
    width, ch = w.shape
    return lax.conv_general_dilated(
        x, w[:, None, :].astype(x.dtype), window_strides=(1,), padding=[(width - 1, 0)],
        dimension_numbers=("NWC", "WIO", "NWC"), feature_group_count=ch)

def gated_head_rmsnorm(o, gate, w):
    b, h, s, d = o.shape
    o = o * lax.rsqrt(jnp.mean(o * o, axis=-1, keepdims=True) + EPS) * w.astype(F32)
    o = o.transpose(0, 2, 1, 3).reshape(b, s, h * d)
    return (o * jax.nn.silu(gate.astype(F32))).astype(gate.dtype)

def to_chunks(a):
    b, h, s = a.shape[:3]
    return jnp.moveaxis(a.reshape(b, h, s // CHUNK, CHUNK, *a.shape[3:]), 2, 0)

def from_chunks(o):
    n, b, h, c, d = o.shape
    return jnp.moveaxis(o, 0, 2).reshape(b, h, n * c, d)

def chunk_gated_delta_rule(q, k, v, g, beta):
    b, h, s, dk = q.shape
    dv = v.shape[-1]
    qc, kc, vc = to_chunks(q * dk ** -0.5), to_chunks(k), to_chunks(v)
    gc, bc = to_chunks(g), to_chunks(beta)
    gcum = jnp.cumsum(gc, axis=-1)
    causal = jnp.tril(jnp.ones((CHUNK, CHUNK), bool))
    strict = jnp.tril(jnp.ones((CHUNK, CHUNK), bool), -1)
    decay = jnp.exp(jnp.where(causal, gcum[..., :, None] - gcum[..., None, :], -jnp.inf))
    k_beta = kc * bc[..., None]
    a_low = jnp.where(strict, jnp.einsum("nbhid,nbhjd->nbhij", k_beta, kc) * decay, 0.0)
    lower = a_low + jnp.eye(CHUNK, dtype=F32)
    u = lax.linalg.triangular_solve(lower, vc * bc[..., None], left_side=True, lower=True)
    w = lax.linalg.triangular_solve(lower, k_beta * jnp.exp(gcum)[..., None], left_side=True, lower=True)
    attn_qk = jnp.einsum("nbhid,nbhjd->nbhij", qc, kc) * decay
    q_dec = qc * jnp.exp(gcum)[..., None]
    k_dec = kc * jnp.exp(gcum[..., -1:] - gcum)[..., None]
    g_last = jnp.exp(gcum[..., -1])

    def step(state, inp):
        u_i, w_i, a_i, qd_i, kd_i, gl_i = inp
        v_new = u_i - jnp.einsum("bhck,bhkv->bhcv", w_i, state)
        o_i = jnp.einsum("bhck,bhkv->bhcv", qd_i, state) + jnp.einsum("bhij,bhjv->bhiv", a_i, v_new)
        state = state * gl_i[..., None, None] + jnp.einsum("bhck,bhcv->bhkv", kd_i, v_new)
        return state, o_i

    s0 = jnp.zeros((b, h, dk, dv), F32)
    _, o = lax.scan(step, s0, (u, w, attn_qk, q_dec, k_dec, g_last))
    return from_chunks(o)

def chunk_gated_linear_attention(q, k, v, log_g, scale):
    b, h, s, dk = q.shape
    dv = v.shape[-1]
    qc, kc, vc = to_chunks(q * scale), to_chunks(k), to_chunks(v)
    bc = jnp.cumsum(to_chunks(log_g), axis=-2)
    causal = jnp.tril(jnp.ones((CHUNK, CHUNK), bool))[:, :, None]

    def step(state, inp):
        q_i, k_i, v_i, b_i = inp
        o_inter = jnp.einsum("bhck,bhkv->bhcv", q_i * jnp.exp(b_i), state)
        diff = jnp.where(causal, b_i[:, :, :, None, :] - b_i[:, :, None, :, :], -jnp.inf)
        attn = jnp.einsum("bhik,bhjk,bhijk->bhij", q_i, k_i, jnp.exp(diff))
        o_i = o_inter + jnp.einsum("bhij,bhjv->bhiv", attn, v_i)
        b_last = b_i[:, :, -1:, :]
        state = state * jnp.exp(b_last[:, :, 0, :, None]) + jnp.einsum(
            "bhck,bhcv->bhkv", k_i * jnp.exp(b_last - b_i), v_i)
        return state, o_i

    s0 = jnp.zeros((b, h, dk, dv), F32)
    _, o = lax.scan(step, s0, (qc, kc, vc, bc))
    return from_chunks(o)

def linear_recurrence_scan(a, x):
    def combine(c1, c2):
        a1, b1 = c1
        a2, b2 = c2
        return a1 * a2, a2 * b1 + b2
    _, h = lax.associative_scan(combine, (a, x), axis=1)
    return h

def gated_deltanet_group(q, k, v, z, a, bta, conv_w, a_log, dt_bias, norm_w):
    qkv = jax.nn.silu(causal_depthwise_conv(jnp.concatenate([q, k, v], axis=-1), conv_w))
    q, k, v = jnp.split(qkv, [GDN_HEADS * GDN_DK, 2 * GDN_HEADS * GDN_DK], axis=-1)
    qh = l2norm(to_heads(q, GDN_HEADS).astype(F32))
    kh = l2norm(to_heads(k, GDN_HEADS).astype(F32))
    vh = to_heads(v, GDN_HEADS).astype(F32)
    beta = jax.nn.sigmoid(bta.astype(F32)).transpose(0, 2, 1)
    g = -(jnp.exp(a_log.astype(F32)) * jax.nn.softplus(a.astype(F32) + dt_bias.astype(F32)))
    o = chunk_gated_delta_rule(qh, kh, vh, g.transpose(0, 2, 1), beta)
    return gated_head_rmsnorm(o, z, norm_w)

def hgrn2_group(q, f, i, g, lower_bound, norm_w):
    lb = lower_bound.astype(F32)
    fl = f.astype(F32)
    log_f = jnp.log(lb + (1.0 - lb) * jax.nn.sigmoid(fl))
    k = (1.0 - lb) * jax.nn.sigmoid(-fl)
    qh = to_heads(jax.nn.silu(q.astype(F32)), HGRN_HEADS)
    o = chunk_gated_linear_attention(qh, to_heads(k, HGRN_HEADS), to_heads(i.astype(F32), HGRN_HEADS),
                                     to_heads(log_f, HGRN_HEADS), HGRN_DK ** -0.5)
    return gated_head_rmsnorm(o, g, norm_w)

def rglru_group(xb, gate, conv_w, conv_b, w_a, b_a, w_x, b_x, lam):
    xb = causal_depthwise_conv(xb, conv_w) + conv_b.astype(xb.dtype)
    b, s, _ = xb.shape
    xblk = xb.reshape(b, s, LRU_BLOCKS, LRU_BLOCK_W)
    r = jax.nn.sigmoid(jnp.einsum("btgi,gij->btgj", xblk, w_a).reshape(b, s, LRU_WIDTH).astype(F32) + b_a.astype(F32))
    i = jax.nn.sigmoid(jnp.einsum("btgi,gij->btgj", xblk, w_x).reshape(b, s, LRU_WIDTH).astype(F32) + b_x.astype(F32))
    log_a = -LRU_C * r * jax.nn.softplus(-lam.astype(F32))
    mult = jnp.sqrt(-jnp.expm1(2.0 * log_a))
    h = linear_recurrence_scan(jnp.exp(log_a), mult * i * xb.astype(F32))
    return (h * jax.nn.gelu(gate.astype(F32))).astype(gate.dtype)

def gla_group(q, k, v, g, lowrank, w_gate, b_gate, norm_w):
    log_alpha = jax.nn.log_sigmoid((lowrank @ w_gate).astype(F32) + b_gate.astype(F32)) / GLA_GATE_TAU
    o = chunk_gated_linear_attention(to_heads(q.astype(F32), GLA_HEADS), to_heads(k.astype(F32), GLA_HEADS),
                                     to_heads(v.astype(F32), GLA_HEADS), to_heads(log_alpha, GLA_HEADS), GLA_DK ** -0.5)
    return gated_head_rmsnorm(o, g, norm_w)

def hybrid_mixer(h, w_in, w_out, gdn_conv_w, gdn_a_log, gdn_dt_bias, gdn_norm, hgrn_lb, hgrn_norm,
                 lru_conv_w, lru_conv_b, lru_w_a, lru_b_a, lru_w_x, lru_b_x, lru_lambda,
                 gla_w_gate, gla_b_gate, gla_norm):
    proj = h @ w_in
    splits = [int(c) for c in np.cumsum(IN_SIZES)[:-1]]
    (aq, ak, av, az, aa, ab, bq, bf, bi, bg, cx, cg, dq, dk, dv, dg, dlr) = jnp.split(proj, splits, axis=-1)
    y_a = gated_deltanet_group(aq, ak, av, az, aa, ab, gdn_conv_w, gdn_a_log, gdn_dt_bias, gdn_norm)
    y_b = hgrn2_group(bq, bf, bi, bg, hgrn_lb, hgrn_norm)
    y_c = rglru_group(cx, cg, lru_conv_w, lru_conv_b, lru_w_a, lru_b_a, lru_w_x, lru_b_x, lru_lambda)
    y_d = gla_group(dq, dk, dv, dg, dlr, gla_w_gate, gla_b_gate, gla_norm)
    y = jnp.concatenate([y_a, y_b, y_c, y_d], axis=-1)
    return y @ w_out

def peer_ffn(h, w_q, sub_keys, u, v):
    b, s, d = h.shape
    tokens = h.reshape(-1, PEER_TOKEN_BLOCK, d)

    def block(xb):
        n = xb.shape[0]
        q = (xb @ w_q).astype(F32).reshape(n, PEER_HEADS, 2, PEER_QDIM // 2)
        scores = jnp.einsum("nhpd,hpkd->nhpk", q, sub_keys.astype(F32))
        top_s, top_i = lax.top_k(scores, PEER_TOPK)
        cand_s = (top_s[:, :, 0, :, None] + top_s[:, :, 1, None, :]).reshape(n, PEER_HEADS, -1)
        cand_i = (top_i[:, :, 0, :, None] * PEER_NKEYS + top_i[:, :, 1, None, :]).reshape(n, PEER_HEADS, -1)
        best_s, best_pos = lax.top_k(cand_s, PEER_TOPK)
        experts = jnp.take_along_axis(cand_i, best_pos, axis=-1)
        gates = jax.nn.softmax(best_s, axis=-1)
        u_sel = u[experts]
        v_sel = v[experts]
        act = jax.nn.gelu(jnp.einsum("nd,nhkd->nhk", xb, u_sel).astype(F32))
        coeff = (gates * act).astype(xb.dtype)
        return jnp.einsum("nhk,nhkd->nd", coeff, v_sel)

    return lax.map(block, tokens).reshape(b, s, d)

def setup_inputs(seed: int = 0) -> dict:
    key = jax.random.key(seed)
    ks = jax.random.split(key, 26)
    L, D = DEPTH, D_MODEL

    def nrm(k, shape, scale):
        return scale * jax.random.normal(k, shape, F32)

    def gain(k, shape):
        return 1.0 + 0.02 * jax.random.normal(k, shape, F32)

    dt = jnp.exp(jax.random.uniform(ks[7], (L, GDN_HEADS), F32, math.log(1e-3), math.log(1e-1)))
    a0 = jax.random.uniform(ks[18], (L, LRU_WIDTH), F32, 0.9, 0.999)
    s_lam = a0 ** (1.0 / LRU_C)
    return {
        "x": jax.random.normal(ks[0], (BATCH, SEQ, D), F32),
        "norm_mix": gain(ks[1], (L, D)),
        "norm_ffn": gain(ks[2], (L, D)),
        "norm_final": gain(ks[3], (D,)),
        "w_in": nrm(ks[4], (L, D, D_IN), D ** -0.5),
        "w_out": nrm(ks[5], (L, D_MIX, D), D_MIX ** -0.5),
        "gdn_conv_w": nrm(ks[6], (L, CONV_WIDTH, GDN_HEADS * (2 * GDN_DK + GDN_DV)), CONV_WIDTH ** -0.5),
        "gdn_a_log": jnp.log(jax.random.uniform(ks[8], (L, GDN_HEADS), F32, 1.0, 16.0)),
        "gdn_dt_bias": dt + jnp.log(-jnp.expm1(-dt)),
        "gdn_norm": gain(ks[9], (L, GDN_DV)),
        "hgrn_lb_logits": nrm(ks[10], (L, HGRN_HEADS * HGRN_DK), 0.1),
        "hgrn_norm": gain(ks[11], (L, HGRN_DV)),
        "lru_conv_w": nrm(ks[12], (L, CONV_WIDTH, LRU_WIDTH), CONV_WIDTH ** -0.5),
        "lru_conv_b": nrm(ks[13], (L, LRU_WIDTH), 0.01),
        "lru_w_a": nrm(ks[14], (L, LRU_BLOCKS, LRU_BLOCK_W, LRU_BLOCK_W), LRU_BLOCK_W ** -0.5),
        "lru_b_a": nrm(ks[15], (L, LRU_WIDTH), 0.01),
        "lru_w_x": nrm(ks[16], (L, LRU_BLOCKS, LRU_BLOCK_W, LRU_BLOCK_W), LRU_BLOCK_W ** -0.5),
        "lru_b_x": nrm(ks[17], (L, LRU_WIDTH), 0.01),
        "lru_lambda": jnp.log(s_lam) - jnp.log1p(-s_lam),
        "gla_w_gate": nrm(ks[19], (L, GLA_GATE_RANK, GLA_HEADS * GLA_DK), GLA_GATE_RANK ** -0.5),
        "gla_b_gate": nrm(ks[20], (L, GLA_HEADS * GLA_DK), 0.01),
        "gla_norm": gain(ks[21], (L, GLA_DV)),
        "peer_w_q": nrm(ks[22], (L, D, PEER_HEADS * PEER_QDIM), D ** -0.5),
        "peer_sub_keys": nrm(ks[23], (L, PEER_HEADS, 2, PEER_NKEYS, PEER_QDIM // 2), (PEER_QDIM // 2) ** -0.5),
        "peer_u": nrm(ks[24], (L, PEER_EXPERTS, D), D ** -0.5),
        "peer_v": nrm(ks[25], (L, PEER_EXPERTS, D), PEER_HEADS ** -0.5),
    }

def reference(x, norm_mix, norm_ffn, norm_final, w_in, w_out, gdn_conv_w, gdn_a_log, gdn_dt_bias, gdn_norm,
              hgrn_lb_logits, hgrn_norm, lru_conv_w, lru_conv_b, lru_w_a, lru_b_a, lru_w_x, lru_b_x, lru_lambda,
              gla_w_gate, gla_b_gate, gla_norm, peer_w_q, peer_sub_keys, peer_u, peer_v):
    lb_all = jnp.cumsum(jax.nn.softmax(hgrn_lb_logits.astype(F32), axis=0), axis=0)
    lb_all = lb_all - lb_all[0]
    for l in range(DEPTH):
        h = rmsnorm(x, norm_mix[l])
        x = x + hybrid_mixer(h, w_in[l], w_out[l], gdn_conv_w[l], gdn_a_log[l], gdn_dt_bias[l], gdn_norm[l],
                             lb_all[l], hgrn_norm[l], lru_conv_w[l], lru_conv_b[l], lru_w_a[l], lru_b_a[l],
                             lru_w_x[l], lru_b_x[l], lru_lambda[l], gla_w_gate[l], gla_b_gate[l], gla_norm[l]).astype(x.dtype)
        h = rmsnorm(x, norm_ffn[l])
        x = x + peer_ffn(h, peer_w_q[l], peer_sub_keys[l], peer_u[l], peer_v[l]).astype(x.dtype)
    return rmsnorm(x, norm_final)


_drawn_inputs = setup_inputs


def setup_inputs(seed=0):
    import zlib

    import numpy as np

    out = dict(_drawn_inputs(seed))
    spreads = {}
    factors = {'norm_final': 8.988,
     'hgrn_lb_logits': 6.565,
     'lru_b_a': 21.051,
     'lru_b_x': 15.402,
     'gla_b_gate': 4.743}
    for name, (base, spread) in spreads.items():
        noise = np.random.default_rng([zlib.crc32(name.encode()), seed]).standard_normal(out[name].shape)
        drawn = base * np.exp(spread * noise) if base else spread * noise
        out[name] = jnp.asarray(drawn.astype(out[name].dtype))
    for name, factor in factors.items():
        out[name] = (out[name] * factor).astype(out[name].dtype)
    return out
```

```python
from contextlib import ExitStack

import numpy as np

import concourse.bass as bass
from concourse import mybir

F32 = mybir.dt.float32
BF16 = mybir.dt.bfloat16
U16 = mybir.dt.uint16
U32 = mybir.dt.uint32
ALU = mybir.AluOpType
ACT = mybir.ActivationFunctionType
AX = mybir.AxisListType

P = 128
T = 512
D = 1024
L = 2
KC = D // P
C = P
NC = T // C
NH = 4
NM = 2 * D // P
EPS = 1e-6
PH, NK, TK = 8, 128, 16
LEVELS = [1 << n for n in range(7)]
BIG = -3.0e38
LN_FLOOR = 2.0 ** -63

XT, HT, RING, YT = 0, 8, 16, 24
NPAGES = 101
RING_SLOTS = 4
C_IN, C_X, C_R, C_I, C_A, SMALL = 89, 67, 71, 75, 79, 83
A_IN, A_Q, A_K, A_V, A_ROWG, A_ROWB, A_EXPG = 40, 53, 57, 61, 65, 66, 67
A_DEC, A_ATT, A_X, A_XT, A_MS, A_R, A_P, A_KD, A_BV, A_S, A_VN = 71, 75, 40, 44, 48, 52, 67, 79, 83, 87, 88
LB_K, L_B, L_E, L_QS, L_KS, L_ATT, L_KD, L_O, L_S = 40, 44, 48, 53, 57, 61, 67, 71, 66
B_Q, B_F, B_V = 89, 93, 97
D_Q, D_K, D_F, D_V = 75, 79, 83, 85
R_Q, R_SK, R_SC, R_TMP, R_CAND, R_EQ, R_SM, R_SEL = 24, 40, 44, 48, 49, 53, 57, 61
V_BUF, GELU, IJW, G_BUF = 24, 32, 34, 37
OH_B, OH_A = 24, 28
CHUNK_I = 64
GRP = 4

PC = {}
_at = 0
for _name, _n in (("norm_mix", 8), ("norm_ffn", 8), ("conv_a", 48), ("gdn_norm", 1), ("hgrn_norm", 1), ("gla_norm", 1),
                  ("conv_c", 16), ("conv_cb", 4), ("b_a", 4), ("b_x", 4), ("lam", 4), ("gla_b", 2), ("lb", 8),
                  ("a_log", 1), ("dt", 1), ("norm_final", 8)):
    PC[_name] = (_at, _n)
    _at += _n
NPC = _at
N_IN = 44 + 8
N_STREAM = N_IN + 16 + 16 + NK


class Tally:

    def __init__(self, eng):
        self.eng, self.put, self.got = eng, {}, {}

    def tell(self, ins, sem):
        ins.then_inc(sem, 1)
        self.put[sem] = self.put.get(sem, 0) + 1

    def done(self, ins, sem):
        self.tell(ins, sem)
        self.eng.wait_ge(sem, self.put[sem])

    def take(self, sem, n=1):
        self.got[sem] = self.got.get(sem, 0) + n
        self.eng.wait_ge(sem, self.got[sem])


def build_program(nc, x, wstream, pcol, small, wgate, skeys, vexp, const_f, const_m, out):
    with ExitStack() as ctx:
        def sb(name, shape, dt=F32):
            return ctx.enter_context(nc.sbuf_tensor(name, shape, dt))

        sems = {}

        def sem(name):
            sems[name] = ctx.enter_context(nc.semaphore(name))
            return sems[name]

        arena = sb("arena", [P, NPAGES * T])
        cf = sb("cf", [P, 2 * P])
        cm = sb("cm", [P, 8 * P], BF16)
        ones = sb("ones", [P, P])
        pc = sb("pc", [P, NPC])
        wg = sb("wg", [80, 2 * P])
        cols = sb("cols", [P, 96])
        ps = ctx.enter_context(nc.psum_tensor("ps", [P, 8, T], F32))

        def pg(a, n=1):
            return arena[:, a * T:(a + n) * T]

        def pg3(a, n, w=T):
            return arena[:, a * T:a * T + n * w].rearrange("p (n t) -> p n t", t=w)

        def par(name, k=0, n=1):
            o = PC[name][0] + k
            return pc[:, o:o + n]

        ident = cf[:, 0:P]
        iota = cf[:, P:2 * P]
        m_ge = cm[:, 7 * P:8 * P]

        def m_level(n):
            return cm[:, n * P:(n + 1) * P]

        eps_c, lamc, lbc, lb1, tmpc = cols[:, 0:1], cols[:, 1:5], cols[:, 5:9], cols[:, 9:13], cols[:, 13:17]
        alog_e, one_c = cols[:, 17:18], cols[:, 18:19]
        gct, bct, kdc, glc = cols[:, 20:36], cols[:, 36:52], cols[:, 52:68], cols[:, 68:84]
        lbt = cols[:, 84:96]

        x_loaded, c_loaded, p_loaded, small_loaded, sk_loaded = map(sem, ("x_loaded", "c_loaded", "p_loaded", "small_loaded", "sk_loaded"))
        ring_loaded = [sem(f"ring_loaded{s}") for s in range(RING_SLOTS)]
        v_loaded, out_stored = sem("v_loaded"), sem("out_stored")
        act_step, dve_step, pool_step = sem("act_step"), sem("dve_step"), sem("pool_step")
        x_ready, sq_ready, norm_sum, norm_root, h_ready = map(sem, ("x_ready", "sq_ready", "norm_sum", "norm_root", "h_ready"))
        block_done, evac_done = sem("block_done"), sem("evac_done")
        par_act, par_dve, ones_ready = sem("par_act"), sem("par_dve"), sem("ones_ready")
        tm_done, tm_evac = sem("tm_done"), sem("tm_evac")
        xc_ready, cgate_done, cgate_evac, loga_ready, cexp_ready, cm_ready, csqrt_ready, c_done = map(
            sem, ("xc_ready", "cgate_done", "cgate_evac", "loga_ready", "cexp_ready", "cm_ready", "csqrt_ready", "c_done"))
        aconv_ready, silu_ready, rows_raw, rows_done = map(sem, ("aconv_ready", "silu_ready", "rows_raw", "rows_done"))
        asq_ready, asum_done, aroot_ready, qk_ready = map(sem, ("asq_ready", "asum_done", "aroot_ready", "qk_ready"))
        sp_in, sp_ln = sem("sp_in"), sem("sp_ln")
        bc_done, bc_used, expg_ready, col_done, dec_in, dec_exp, dec_ready = map(
            sem, ("bc_done", "bc_used", "expg_ready", "col_done", "dec_in", "dec_exp", "dec_ready"))
        prod_done, prod_used, tr_done, tr_used = map(sem, ("prod_done", "prod_used", "tr_done", "tr_used"))
        amat_ready, lev_masked, lev_p, lev_pc, lev_d, lev_x = map(sem, ("amat_ready", "lev_masked", "lev_p", "lev_pc", "lev_d", "lev_x"))
        rs_done, r_ready, vn_done, vn_ready, o_done, o_used, s_done, s_ready = map(
            sem, ("rs_done", "r_ready", "vn_done", "vn_ready", "o_done", "o_used", "s_done", "s_ready"))
        osq_ready, osum_done, oroot_ready, y_ready = map(sem, ("osq_ready", "osum_done", "oroot_ready", "y_ready"))
        la_sig, la_lnin, la_ln, la_b, la_diff, la_e, la_q, la_k, la_att, la_used = map(
            sem, ("la_sig", "la_lnin", "la_ln", "la_b", "la_diff", "la_e", "la_q", "la_k", "la_att", "la_used"))
        la_ready, dk_clear, dgate_done = sem("la_ready"), sem("dk_clear"), sem("dgate_done")
        op_done, op_used = sem("op_done"), sem("op_used")
        wq_evac, sc_done, sc_evac, sc_used, best_ready, best_exp, sel_ready, selt_done, selt_evac = map(
            sem, ("wq_evac", "sc_done", "sc_evac", "sc_used", "best_ready", "best_exp", "sel_ready", "selt_done", "selt_evac"))
        hot_ready, outer_done, gate_stored = sem("hot_ready"), sem("outer_done"), sem("gate_stored")
        act_done, gelu_ready, coef_ready, mix_done, acc_done = map(sem, ("act_done", "gelu_ready", "coef_ready", "mix_done", "acc_done"))

        lowrank = arena[64:80, A_ROWG * T:(A_ROWG + 1) * T]
        block = ctx.enter_context(nc.Block())

        yT = pg3(YT, NM)
        hT = pg3(HT, KC)
        xT = pg3(XT, KC)
        n_grp = NK // GRP
        g_chunk = CHUNK_I // GRP

        def slot(s, w=P):
            return arena[:, (RING + 2 * s) * T:(RING + 2 * s + 2) * T].rearrange("p (k m) -> p k m", m=w)

        gates = pg3(G_BUF, CHUNK_I)
        v_buf = arena[:, V_BUF * T:(V_BUF + 2 * GRP) * T].rearrange("p (b d) -> p b d", b=GRP)

        @block.sync
        def _(sp):
            t = Tally(sp)
            sp.dma_start(pg(XT, KC), x).then_inc(x_loaded, 16)
            sp.dma_start(cf[:, :], const_f).then_inc(c_loaded, 16)
            sp.dma_start(cm[:, :], const_m).then_inc(c_loaded, 16)
            for l in range(L):
                if l:
                    sp.wait_ge(acc_done, 4 + l * NK // GRP * 8)
                sp.dma_start(pc[:, :], pcol[l]).then_inc(p_loaded, 16)
                sp.dma_start(wg[64:80, :], wgate[l]).then_inc(p_loaded, 16)
                sp.dma_start(pg(SMALL, 4)[:, 0:1792], small[l]).then_inc(small_loaded, 16)
                base = l * N_STREAM
                for n in range(N_IN + 32):
                    k = base + n
                    if k >= RING_SLOTS:
                        sp.wait_ge(block_done, k - RING_SLOTS + 1)
                    sp.dma_start(arena[:, (RING + 2 * (n % 4)) * T:(RING + 2 * (n % 4) + 2) * T], wstream[k]).then_inc(ring_loaded[n % 4], 16)
                    if n == N_IN + 16:
                        t.take(y_ready, 4)
                        sp.dma_start(pg(R_SK, 4), skeys[l]).then_inc(sk_loaded, 16)
                k0 = base + N_IN + 32
                for ch in range(NK // CHUNK_I):
                    with sp.Fori(0, g_chunk) as g:
                        for s in range(GRP):
                            sp.wait_ge(block_done, g * GRP + (k0 + ch * CHUNK_I + s - RING_SLOTS + 1))
                            sp.dma_start(arena[:, (RING + 2 * s) * T:(RING + 2 * s + 2) * T],
                                         wstream[bass.ds(g * GRP + (k0 + ch * CHUNK_I + s), 1)].rearrange("a p n -> p (a n)")
                                         ).then_inc(ring_loaded[s], 16)
                        sp.wait_ge(mix_done, g * 8 + ((l * n_grp + ch * g_chunk) * 8 + 1))
                        sp.wait_ge(gate_stored, (l * 2 + ch + 1) * (T // 8) + 2)
                        sp.dma_start(v_buf, vexp[bass.ds(g + (l * n_grp + ch * g_chunk), 1)].rearrange("a b p d -> p (a b) d")
                                     ).then_inc(v_loaded, 16)
            sp.wait_ge(h_ready, 2 * L + 1)
            sp.dma_start(out, pg(HT, KC)).then_inc(out_stored, 16)
            sp.wait_ge(out_stored, 16)

        JOBS = 45 + 16

        @block.tensor
        def _(pe):
            t = Tally(pe)
            nblk = [0]
            jobs = [0]

            def norm():
                t.take(sq_ready, 2)
                for k in range(KC):
                    ins = pe.matmul(ps[:, 7, :], ones[:, :], pg(YT + k), start=k == 0, stop=k == KC - 1)
                t.tell(ins, norm_sum)
                t.take(h_ready)

            def bank():
                if jobs[0] >= 2:
                    t.take(evac_done)
                jobs[0] += 1
                return (jobs[0] - 1) % 2

            def next_slot():
                s = nblk[0] % RING_SLOTS
                pe.wait_ge(ring_loaded[s], 16 * (nblk[0] // RING_SLOTS + 1))
                nblk[0] += 1
                return s

            def project(n):
                for _ in range(n):
                    b, s = bank(), next_slot()
                    for k in range(KC):
                        ins = pe.matmul(ps[:, b, :], slot(s)[:, k, :], hT[:, k, :], start=k == 0, stop=k == KC - 1)
                    ins.then_inc(block_done, 1)

            def project_small():
                b = bank()
                sw = arena[:, SMALL * T:SMALL * T + 768].rearrange("p (k m) -> p k m", m=96)
                for k in range(KC):
                    ins = pe.matmul(ps[0:96, b, :], sw[:, k, :], hT[:, k, :], start=k == 0, stop=k == KC - 1)
                t.tell(ins, rows_raw)

            def project_tokens():
                for q in range(4):
                    s = next_slot()
                    for k in range(2):
                        for c in range(NC):
                            ins = pe.matmul(ps[:, 2 + c, :], hT[:, 2 * q + k, c * C:(c + 1) * C], slot(s, T)[:, k, :],
                                            start=q == 0 and k == 0, stop=q == 3 and k == 1)
                    ins.then_inc(block_done, 1)
                t.take(tm_evac)

            def group_c():
                sw = arena[:, SMALL * T + 768:SMALL * T + 1792].rearrange("p (g m) -> p g m", m=P)
                for g in range(4):
                    t.take(xc_ready)
                    if g:
                        t.take(cgate_evac)
                    pe.matmul(ps[:, 6, :], sw[:, g, :], pg(C_X + g), start=True, stop=True)
                    t.tell(pe.matmul(ps[:, 7, :], sw[:, 4 + g, :], pg(C_X + g), start=True, stop=True), cgate_done)
                t.take(cgate_evac)

            def level_systems(b):
                return [(b, c) for c in range(NC)]

            def transposes(src, use):
                for b in range(NH):
                    for c in range(NC):
                        ins = pe.transpose(ps[:, 2 + b, c * C:(c + 1) * C], src[:, b, c * C:(c + 1) * C], ident)
                    t.tell(ins, tr_done)
                t.take(tr_used, 4)

            def group_a():
                qT, kT, vT = pg3(A_Q, NH), pg3(A_K, NH), pg3(A_V, NH)
                for m in range(8):
                    t.take(asq_ready)
                    ins = pe.matmul(ps[:, 6 + m % 2, :], ones[:, :], pg(A_X + m), start=True, stop=True)
                    t.tell(ins, asum_done)
                    if m >= 1:
                        t.take(aroot_ready)
                t.take(aroot_ready)
                t.take(rows_done)
                for c in range(NC):
                    pe.transpose(ps[:, 6, c * 4:c * 4 + 4], arena[0:4, A_ROWG * T + c * C:A_ROWG * T + (c + 1) * C], ident[0:4, 0:4])
                    ins = pe.transpose(ps[:, 6, 16 + c * 4:20 + c * 4], arena[0:4, A_ROWB * T + c * C:A_ROWB * T + (c + 1) * C], ident[0:4, 0:4])
                t.tell(ins, col_done)
                for h in range(NH):
                    ins = pe.matmul(ps[:, 2 + h, :], ident[0:4, h:h + 1].broadcast_to([4, P]), arena[0:4, A_ROWG * T:(A_ROWG + 1) * T], start=True, stop=True)
                t.tell(ins, bc_done)
                t.take(bc_used)
                t.take(qk_ready, 2)
                for rhs in (qT, kT):
                    for h in range(NH):
                        for c in range(NC):
                            ins = pe.matmul(ps[:, 2 + h, c * C:(c + 1) * C], kT[:, h, c * C:(c + 1) * C], rhs[:, h, c * C:(c + 1) * C], start=True, stop=True)
                        t.tell(ins, prod_done)
                    t.take(prod_used, 4)
                transposes(kT, None)
                transposes(vT, None)
                for h in range(NH):
                    ins = pe.matmul(ps[:, 2 + h, :], ident[0:4, h:h + 1].broadcast_to([4, P]), arena[0:4, A_ROWB * T:(A_ROWB + 1) * T], start=True, stop=True)
                t.tell(ins, bc_done)
                X, XTr, MS, PP = pg3(A_X, NH), pg3(A_XT, NH), pg3(A_MS, NH), pg3(A_P, NH)
                t.take(amat_ready)
                for n in range(7):
                    for b in range(NH):
                        t.take(lev_masked)
                        for c in range(NC):
                            q = slice(c * C, (c + 1) * C)
                            ins = pe.matmul(ps[:, 2 + b, q], MS[:, b, q], X[:, b, q], start=True, stop=True)
                        t.tell(ins, lev_p)
                    for b in range(NH):
                        t.take(lev_pc)
                        for c in range(NC):
                            q = slice(c * C, (c + 1) * C)
                            pe.matmul(ps[:, 6, q], XTr[:, b, q], PP[:, b, q], start=True, stop=True)
                        for c in range(NC):
                            q = slice(c * C, (c + 1) * C)
                            ins = pe.matmul(ps[:, 7, q], PP[:, b, q], XTr[:, b, q], start=True, stop=True)
                        t.tell(ins, lev_d)
                        t.take(lev_x)
                S, VN, R, ATT, KD = pg3(A_S, NH, C), pg3(A_VN, NH, C), pg3(A_R, NH, C), pg3(A_ATT, NH), pg3(A_KD, NH)
                t.take(s_ready)
                for c in range(NC):
                    q = slice(c * C, (c + 1) * C)
                    for h in range(NH):
                        ins = pe.matmul(ps[:, 2, h * C:(h + 1) * C], kT[:, h, q], S[:, h, :], start=True, stop=True)
                    t.tell(ins, rs_done)
                    t.take(r_ready)
                    for h in range(NH):
                        ins = pe.matmul(ps[:, 3, h * C:(h + 1) * C], XTr[:, h, q], R[:, h, :], start=True, stop=True)
                    t.tell(ins, vn_done)
                    t.take(vn_ready)
                    for h in range(NH):
                        pe.matmul(ps[:, 4, h * C:(h + 1) * C], S[:, h, :], qT[:, h, q], start=True, stop=False)
                        ins = pe.matmul(ps[:, 4, h * C:(h + 1) * C], VN[:, h, :], ATT[:, h, q], start=False, stop=True)
                    t.tell(ins, o_done)
                    for h in range(NH):
                        ins = pe.matmul(ps[:, 5, h * C:(h + 1) * C], KD[:, h, q], VN[:, h, :], start=True, stop=True)
                    t.tell(ins, s_done)
                    t.take(s_ready)
                    t.take(o_used)

            def head_norm():
                for h in range(NH):
                    t.take(osq_ready)
                    t.tell(pe.matmul(ps[:, 2 + h, :], ones[:, :], pg(L_E + h), start=True, stop=True), osum_done)
                t.take(oroot_ready, 4)

            def gate_d():
                for m in range(2):
                    ins = pe.matmul(ps[:, 2 + m, :], wg[64:80, m * P:(m + 1) * P], lowrank, start=True, stop=True)
                t.tell(ins, dgate_done)

            def linear(qa, ka, va):
                qT, kT, QS, KS = pg3(qa, NH), pg3(ka, NH), pg3(L_QS, NH), pg3(L_KS, NH)
                ATT, KD, S, V = pg3(L_ATT, NH), pg3(L_KD, NH), pg3(L_S, NH, C), pg3(va, NC)
                t.take(la_ready)
                for n in range(8):
                    a, b = (kT, qT) if n == 0 else (KS, QS)
                    if n:
                        t.take(la_q)
                        t.take(la_k)
                    for h in range(NH):
                        if n:
                            t.take(la_used)
                        for c in range(NC):
                            q = slice(c * C, (c + 1) * C)
                            ins = pe.matmul(ps[:, 2 + h, q], a[:, h, q], b[:, h, q], start=True, stop=True)
                        t.tell(ins, la_att)
                t.take(la_used, 4)
                t.take(la_q)
                t.take(la_k)
                transposes(KS, None)
                t.take(s_ready)
                for c in range(NC):
                    q = slice(c * C, (c + 1) * C)
                    for h in range(NH):
                        pe.matmul(ps[:, 4, h * C:(h + 1) * C], S[:, h, :], QS[:, h, q], start=True, stop=False)
                        ins = pe.matmul(ps[:, 4, h * C:(h + 1) * C], V[:, c, h * C:(h + 1) * C], ATT[:, h, q], start=False, stop=True)
                    t.tell(ins, o_done)
                    for h in range(NH):
                        ins = pe.matmul(ps[:, 5, h * C:(h + 1) * C], KD[:, h, q], V[:, c, h * C:(h + 1) * C], start=True, stop=True)
                    t.tell(ins, s_done)
                    t.take(s_ready)
                    t.take(o_used)

            def out_projection():
                t.take(y_ready, 4)
                for m in range(8):
                    if m >= 2:
                        t.take(op_used)
                    for half in range(2):
                        s = next_slot()
                        for k in range(8):
                            ins = pe.matmul(ps[:, 6 + m % 2, :], slot(s)[:, k, :], yT[:, 8 * half + k, :],
                                            start=half == 0 and k == 0, stop=half == 1 and k == 7)
                        ins.then_inc(block_done, 1)
                t.take(op_used, 2)

            def router(l):
                qT = pg3(R_Q, 16)
                sk = pg3(R_SK, 16, P)
                pe.wait_ge(sk_loaded, 16 * (l + 1))
                pe.wait_ge(evac_done, jobs[0])
                for tile in range(NC):
                    if tile:
                        t.take(sc_evac)
                    for hp in range(16):
                        ins = pe.matmul(ps[:, 2 + hp // 4, (hp % 4) * P:(hp % 4 + 1) * P], qT[:, hp, tile * C:(tile + 1) * C], sk[:, hp, :], start=True, stop=True)
                    t.tell(ins, sc_done)
                t.take(sc_evac)
                for tile in range(NC):
                    t.take(sel_ready)
                    if tile:
                        t.take(selt_evac)
                    for k in range(3):
                        ins = pe.transpose(ps[:, 6, k * P:(k + 1) * P], pg(R_SEL + tile)[:, k * P:(k + 1) * P], ident)
                    t.tell(ins, selt_done)
                t.take(selt_evac)

            def build_gates(l, ch):
                base = (l * 2 + ch) * (T // 8)
                hb, ha = pg3(OH_B, 16, P), pg3(OH_A, 16, CHUNK_I)
                with pe.Fori(0, T // 16) as i:
                    for half in range(2):
                        pe.wait_ge(hot_ready, i * 2 + (base + half + 1))
                        pe.wait_ge(gate_stored, i * 2 + (base + half + 1))
                        for k in range(8):
                            ins = pe.matmul(ps[:, half, k * CHUNK_I:(k + 1) * CHUNK_I], hb[:, 8 * half + k, :], ha[:, 8 * half + k, :], start=True, stop=True)
                        ins.then_inc(outer_done, 1)

            def experts(l, ch):
                g0 = l * n_grp + ch * g_chunk
                pe.wait_ge(gate_stored, (l * 2 + ch + 1) * (T // 8) + 2)
                with pe.Fori(0, g_chunk) as g:
                    for b in range(GRP):
                        pe.wait_ge(ring_loaded[b], g * 16 + 16 * ((N_STREAM * l + N_IN + 32) // 4 + ch * g_chunk + 1))
                        pe.wait_ge(gelu_ready, g * GRP + (g0 * GRP + b + 1))
                        for k in range(KC):
                            ins = pe.matmul(ps[:, b % 2, :], slot(b)[:, k, :], hT[:, k, :], start=k == 0, stop=k == KC - 1)
                        ins.then_inc(block_done, 1)
                    pe.wait_ge(v_loaded, g * 16 + 16 * (g0 + 1))
                    for m in range(8):
                        if m == 0:
                            pe.wait_ge(coef_ready, g * GRP + (g0 * GRP + GRP + 2))
                        pe.wait_ge(acc_done, g * 8 + (g0 * 8 + m + 1))
                        for b in range(GRP):
                            ins = pe.matmul(ps[:, 2 + m % 4, :], v_buf[:, b, m * P:(m + 1) * P],
                                            gates[:, bass.ds(g * GRP + b, 1), :].rearrange("p a t -> p (a t)"), start=b == 0, stop=b == GRP - 1)
                        ins.then_inc(mix_done, 1)
                pe.wait_ge(acc_done, (g0 + g_chunk) * 8 + 4)

            pe.wait_ge(c_loaded, 32)
            t.take(ones_ready)
            for k in range(3):
                pe.matmul(ps[:, 6, 0:P], ones[:, :], ones[:, :], start=True, stop=True).then_inc(mix_done if k == 2 else outer_done, 1)
            for l in range(L):
                norm()
                project(8)
                project(16)
                pe.wait_ge(small_loaded, 16 * (l + 1))
                project_small()
                group_c()
                project(12)
                project_tokens()
                group_a()
                head_norm()
                project(8)
                project_tokens()
                gate_d()
                linear(B_Q, LB_K, B_V)
                head_norm()
                linear(D_Q, D_K, D_V)
                head_norm()
                out_projection()
                norm()
                project(16)
                router(l)
                for ch in range(NK // CHUNK_I):
                    build_gates(l, ch)
                    experts(l, ch)
                nblk[0] += NK
            norm()


        @block.scalar
        def _(act):
            t = Tally(act)

            def f(out_, in_, func, sem_=None, **kw):
                t.done(act.activation(out_, in_, func, **kw), sem_ or act_step)

            def norm(l, first, scale=1.0 / D):
                if first and l == 0:
                    act.wait_ge(x_loaded, 16)
                elif first:
                    act.wait_ge(acc_done, 4 + l * n_grp * 8)
                else:
                    t.take(x_ready)
                for k in range(2):
                    f(pg(YT + 4 * k, 4), pg(XT + 4 * k, 4), ACT.Square, sq_ready)
                t.take(norm_sum)
                f(pg(YT + 8), ps[:, 7, :], ACT.Sqrt, norm_root, scale=scale, bias=eps_c)

            jobs = [0]

            def evacs(n, write):
                for m in range(n):
                    t.take(block_done)
                    write(m, ps[:, jobs[0] % 2, :])
                    jobs[0] += 1

            def softplus_tail(z, tmp, sig_):
                f(tmp, z, ACT.Abs)
                f(tmp, tmp, ACT.Exp, scale=-1.0)
                f(tmp, tmp, ACT.Ln, sig_, bias=1.0)

            def params(l):
                act.wait_ge(p_loaded, 32 * (l + 1))
                f(alog_e[0:4], par("a_log")[0:4], ACT.Exp)
                softplus_tail(par("lam", 0, 4), tmpc, par_act)
                t.take(par_dve)
                f(lbt[:, 0:8], lbt[:, 0:8], ACT.Exp, par_act)

            def tokens(dst):
                t.take(block_done, 4)
                f(pg(dst, 4), ps[:, 2:6, :], ACT.Copy, tm_evac)

            def store(dst):
                return lambda m, src: f(pg(dst + m), src, ACT.Copy, evac_done)

            def head_norm(o):
                for h in range(NH):
                    f(pg(L_E + h), pg(o + h), ACT.Square, osq_ready)
                for h in range(NH):
                    t.take(osum_done)
                    f(pg(L_QS + h), ps[:, 2 + h, :], ACT.Sqrt, oroot_ready, scale=1.0 / P, bias=eps_c)

            def recurrence(o, delta):
                for c in range(NC):
                    q = slice(c * C, (c + 1) * C)
                    if delta:
                        t.take(vn_done)
                        f(pg(A_VN), ps[:, 3, :], ACT.Copy, vn_ready)
                    t.take(o_done)
                    f(pg3(o, NH)[:, :, q], ps[:, 4, :].rearrange("p (h t) -> p h t", h=NH), ACT.Copy, o_used)

            def linear(f_page, k_page, b_page, n_level_signals):
                for n in range(1, 9):
                    t.take(la_diff)
                    f(pg(L_E, 4), pg(L_E, 4), ACT.Abs)
                    if n == 8:
                        f(pg(L_B, 4), pg(L_B, 4), ACT.Exp)
                    f(pg(L_E, 4), pg(L_E, 4), ACT.Exp, la_e, scale=-1.0)
                for h in range(NH):
                    t.take(tr_done)
                    f(pg(L_KD + h), ps[:, 2 + h, :], ACT.Copy, tr_used)
                recurrence(L_O, False)
                head_norm(L_O)

            t.take(ones_ready)
            for k in range(4):
                f(ps[:, k % 2, k:k + 1], ones[:, 0:1], ACT.Copy, gate_stored if k < 2 else gelu_ready)
            for l in range(L):
                norm(l, True)
                params(l)
                c_in = pg3(C_IN, 4, T + 3)
                evacs(4, lambda m, src: f(c_in[:, m, 3:T + 3], src, ACT.Copy, evac_done))
                evacs(4, lambda m, src: f(pg(YT + 8 + m), src, ACT.Gelu_apprx_tanh, evac_done))
                a_in = pg3(A_IN, 12, T + 3)
                evacs(12, lambda m, src: f(a_in[:, m, 3:T + 3], src, ACT.Copy, evac_done))
                evacs(4, lambda m, src: f(pg(YT + m), src, ACT.Silu, evac_done))
                t.take(rows_raw)
                src = ps[:, jobs[0] % 2, :]
                jobs[0] += 1
                row_g, row_b, row_t = (arena[0:4, a * T:(a + 1) * T] for a in (A_ROWG, A_ROWB, A_S))
                f(row_g, src[0:4], ACT.Identity, bias=par("dt")[0:4])
                f(lowrank, src[64:80], ACT.Copy)
                f(row_b, src[32:36], ACT.Sigmoid, evac_done)
                for g in range(4):
                    t.take(cgate_done)
                    f(pg(C_R + g), ps[:, 6, :], ACT.Sigmoid, bias=par("b_a", g))
                    f(pg(C_I + g), ps[:, 7, :], ACT.Sigmoid, cgate_evac, bias=par("b_x", g))
                t.take(loga_ready)
                f(pg(C_A, 4), pg(C_R, 4), ACT.Exp)
                f(pg(YT + 12, 4), pg(C_R, 4), ACT.Tanh, cexp_ready, scale=-1.0)
                t.take(cm_ready)
                f(pg(C_R, 4), pg(C_R, 4), ACT.Sqrt, csqrt_ready)
                softplus_tail(row_g, row_t, sp_ln)
                t.take(c_done)
                for m in range(12):
                    t.take(aconv_ready)
                    f(pg(A_Q + m), pg(A_Q + m), ACT.Silu)
                    t.take(block_done)
                    src = ps[:, jobs[0] % 2, :]
                    jobs[0] += 1
                    if m < 4:
                        f(pg(B_Q + m), src, ACT.Silu, evac_done)
                    elif m < 8:
                        f(pg(YT + m), src, ACT.Silu, evac_done)
                    else:
                        f(pg(B_F + m - 8), src, ACT.Copy, evac_done)
                tokens(B_V)
                for m in range(8):
                    f(pg(A_X + m), pg(A_Q + m), ACT.Square, asq_ready)
                for m in range(8):
                    t.take(asum_done)
                    if m == 4:
                        t.take(qk_ready)
                    f(pg(A_MS + m % 4), ps[:, 6 + m % 2, :], ACT.Sqrt, aroot_ready, bias=eps_c)
                t.take(qk_ready)
                t.take(bc_done)
                f(pg(A_EXPG, 4), ps[:, 2:6, :], ACT.Exp, expg_ready)
                t.take(dec_in)
                f(pg(A_DEC, 4), pg(A_DEC, 4), ACT.Exp)
                f(cols[:, 52:84], cols[:, 52:84], ACT.Exp, dec_exp)
                for dst, scale in ((A_KD, kdc), (A_BV, bct)):
                    for h in range(NH):
                        t.take(tr_done)
                        for c in range(NC):
                            col = scale[:, h * NC + c:h * NC + c + 1] if dst == A_KD else scale[:, c * NH + h:c * NH + h + 1]
                            f(pg3(dst, NH)[:, h, c * C:(c + 1) * C], ps[:, 2 + h, c * C:(c + 1) * C], ACT.Copy,
                              tr_used if c == NC - 1 else None, scale=col)
                t.take(bc_done)
                for n in range(7):
                    for b in range(NH):
                        t.take(lev_p)
                        f(pg(A_P + b), ps[:, 2 + b, :], ACT.Copy, lev_pc)
                recurrence(A_V, True)
                head_norm(A_V)
                t.take(dk_clear)
                for m in range(2):
                    t.take(block_done)
                    src = ps[:, jobs[0] % 2, :]
                    jobs[0] += 1
                    f(pg(D_Q + 2 * m), src, ACT.Copy, scale=64 ** -0.5)
                    f(pg(D_Q + 2 * m + 1), src, ACT.Copy, evac_done, scale=64 ** -0.5)
                for m in range(2):
                    t.take(block_done)
                    src = ps[:, jobs[0] % 2, :]
                    jobs[0] += 1
                    f(pg(D_K + 2 * m)[0:64], src[0:64], ACT.Copy)
                    f(pg(D_K + 2 * m + 1)[64:128], src[64:128], ACT.Copy, evac_done)
                evacs(4, lambda m, src: f(pg(YT + 12 + m), src, ACT.Silu, evac_done))
                tokens(D_V)
                t.take(sp_in)
                softplus_tail(pg(D_F, 2), pg(L_E, 2), sp_ln)
                f(pg(LB_K, 4), pg(B_F, 4), ACT.Sigmoid, scale=-1.0)
                f(pg(B_F, 4), pg(B_F, 4), ACT.Sigmoid, la_sig)
                t.take(la_lnin)
                f(pg(B_F, 4), pg(B_F, 4), ACT.Ln, la_ln)
                linear(B_F, LB_K, L_B, 9)
                linear(D_F, D_K, L_B, 9)
                norm(l, False)
                t.got[block_done] += 16
                evacs(16, store(R_Q))

                def scores(tile):
                    t.take(sc_done)
                    if tile:
                        t.take(sc_used)
                    f(pg(R_SC, 4), ps[:, 2:6, :], ACT.Copy, sc_evac)

                scores(0)
                for tile in range(NC):
                    if tile + 1 < NC:
                        scores(tile + 1)
                    t.take(best_ready)
                    best = pg(R_SM + 3)[:, 0:P]
                    f(best, best, ACT.Exp, best_exp)
                t.take(sc_used)
                for tile in range(NC):
                    t.take(selt_done)
                    f(pg3(IJW, 3)[:, :, tile * C:(tile + 1) * C], ps[:, 6, 0:3 * P].rearrange("p (k t) -> p k t", k=3), ACT.Copy, selt_evac)
                for ch in range(NK // CHUNK_I):
                    base = (l * 2 + ch) * (T // 8)
                    if ch:
                        act.wait_ge(mix_done, (l * n_grp + ch * g_chunk) * 8 + 1)
                    with act.Fori(0, T // 16) as i:
                        for half in range(2):
                            act.wait_ge(outer_done, i * 2 + (base + half + 3))
                            act.activation(gates[:, :, bass.ds(i * 16 + 8 * half, 8)],
                                           ps[:, half, :].rearrange("p (n i) -> p i n", n=8), ACT.Copy).then_inc(gate_stored, 1)
                    g0 = l * n_grp + ch * g_chunk
                    k0 = l * N_STREAM + N_IN + 32 + ch * CHUNK_I
                    with act.Fori(0, g_chunk) as g:
                        for b in range(GRP):
                            act.wait_ge(block_done, g * GRP + (k0 + b + 1))
                            act.wait_ge(coef_ready, g * GRP + (g0 * GRP + b + 1))
                            act.activation(pg(GELU + b % 2), ps[:, b % 2, :], ACT.Gelu_apprx_tanh).then_inc(gelu_ready, 1)
                t.got[block_done] = (l + 1) * N_STREAM
            norm(L, True)

        @block.vector
        def _(dve):
            t = Tally(dve)
            mul, add, sub = ALU.mult, ALU.add, ALU.subtract

            def v(ins, sem_=None):
                t.done(ins, sem_ or dve_step)

            def tt(o, a, b, op, sem_=None):
                v(dve.tensor_tensor(o, a, b, op), sem_)

            def ts(o, a, s1, s2, op0, op1=None, sem_=None):
                v(dve.tensor_scalar(o, a, s1, s2, op0, op1) if op1 is not None else dve.tensor_scalar(o, a, s1, s2, op0), sem_)

            def stt(o, a, s, b, op0, op1, sem_=None):
                v(dve.scalar_tensor_tensor(out=o, in0=a, scalar=s, in1=b, op0=op0, op1=op1), sem_)

            def norm(name):
                t.take(norm_root)
                v(dve.reciprocal(pg(YT + 8), pg(YT + 8)))
                for k in range(KC):
                    stt(pg(HT + k), pg(XT + k), par(name, k), pg(YT + 8), mul, mul, h_ready if k == KC - 1 else None)

            def conv(src, w, dst, bias, sem_):
                if bias is None:
                    ts(dst, src[:, 0:T], w(0), None, mul)
                else:
                    ts(dst, src[:, 0:T], w(0), bias, mul, add)
                for k in range(1, 4):
                    stt(dst, src[:, k:k + T], w(k), dst, mul, add, sem_ if k == 3 else None)

            def params(l):
                dve.wait_ge(p_loaded, 32 * (l + 1))
                lb = [par("lb", 4 * k, 4) for k in range(L)]
                tt(lbt[:, 8:12], lb[0], lb[1], ALU.max)
                tt(lbt[:, 0:4], lb[0], lbt[:, 8:12], sub)
                tt(lbt[:, 4:8], lb[1], lbt[:, 8:12], sub, par_dve)
                t.take(par_act)
                ts(lamc, par("lam", 0, 4), -1.0, 0.0, mul, ALU.max)
                tt(lamc, lamc, tmpc, add)
                ts(lamc, lamc, -8.0, None, mul)
                t.take(par_act)
                tt(lbt[:, 8:12], lbt[:, 0:4], lbt[:, 4:8], add)
                v(dve.reciprocal(lbt[:, 8:12], lbt[:, 8:12]))
                ts(lbc, lbt[:, 4:8], float(l), None, mul)
                tt(lbc, lbc, lbt[:, 8:12], mul)
                ts(lb1, lbc, -1.0, 1.0, mul, add)

            def heads(a, n=NH):
                return pg3(a, n)

            def chunks(a):
                return pg(a, 4).rearrange("p (s t) -> p s t", t=C)

            def head_norm(o, y, wname):
                for h in range(NH):
                    t.take(oroot_ready)
                    v(dve.reciprocal(pg(L_QS + h), pg(L_QS + h)))
                    stt(pg(o + h), pg(o + h), par(wname), pg(L_QS + h), mul, mul)
                    tt(pg(YT + y + h), pg(YT + y + h), pg(o + h), mul, y_ready if h == NH - 1 else None)

            def state_update(S, col, c):
                t.take(s_done)
                for h in range(NH):
                    stt(S[:, h, :], S[:, h, :], col(h, c), ps[:, 5, h * C:(h + 1) * C], mul, add, s_ready if h == NH - 1 else None)

            def linear(q, k, v_):
                tt_mask = ident.unsqueeze(1).broadcast_to([P, NC, C])
                v(dve.memset(pg(L_S), 0.0), la_ready)
                for n in range(9):
                    if n:
                        s2 = 2 * LEVELS[min(n, 7) - 1]
                        at = s2 // 2 - 1 if n < 8 else C - 1
                        bv = pg(L_B, 4).rearrange("p (s t) -> p s t", t=s2)
                        ev = pg(L_E, 4).rearrange("p (s t) -> p s t", t=s2)
                        if n > 1:
                            t.take(la_k)
                        tt(ev, bv, bv[:, :, at:at + 1].broadcast_to([P, 4 * T // s2, s2]), sub, la_diff)
                        t.take(la_e)
                        tt(pg(L_QS, 4), pg(q, 4), pg(L_E if n < 8 else L_B, 4), mul, la_q)
                    if n == 8:
                        break
                    for h in range(NH):
                        t.take(la_att)
                        dst = pg3(L_ATT, NH)[:, h, :].rearrange("p (c t) -> p c t", t=C)
                        src = ps[:, 2 + h, :].rearrange("p (c t) -> p c t", t=C)
                        if n == 0:
                            tt(dst, src, tt_mask, mul, la_used)
                        else:
                            v(dve.copy_predicated(dst, m_level(n - 1).bitcast(U16).unsqueeze(1).broadcast_to([P, NC, C]), src), la_used)
                t.take(la_k)
                v(dve.memset(pg(L_S), 0.0), s_ready)
                for c in range(NC):
                    state_update(pg3(L_S, NH, C), lambda h, c: pg3(L_B, NH)[:, h, (c + 1) * C - 1:(c + 1) * C], c)

            def scan_chunks(dst, src, data0):
                for c in range(NC):
                    q = slice(c * C, (c + 1) * C)
                    v(dve.tensor_tensor_scan(dst[:, q], data0, src[:, q], 0.0, mul, add))

            def router(l):
                sc, cand, eq = pg3(R_SC, 16, P), pg3(R_CAND, 8, 256), pg(R_EQ, 4)
                tmp, tmp2 = pg(R_TMP)[:, 0:P], pg(R_TMP)[:, P:P + 256]
                m0, m1, m2, m3 = (pg(R_SM + k) for k in range(4))
                top_s = m0[:, 0:256].rearrange("p (h k) -> p h k", k=TK)
                top_i = m0[:, 256:512].bitcast(U32).rearrange("p (h k) -> p h k", k=TK)
                top_f = m1[:, 0:256]
                best_s = m1[:, 256:384].rearrange("p (h k) -> p h k", k=TK)
                best_u = m1[:, 384:512].bitcast(U32)
                rank_f = [m2[:, 0:P], m2[:, P:2 * P]]
                rank_u = [m2[:, 2 * P:3 * P].bitcast(U32), m2[:, 3 * P:4 * P].bitcast(U32)]
                e, total = m3[:, 0:P], m3[:, P:P + 8]

                def top16(scores, work, s, i):
                    v(dve.max(s[:, 0:8], scores))
                    v(dve.max_index(i[:, 0:8], s[:, 0:8], scores))
                    v(dve.match_replace(work, s[:, 0:8], scores, BIG))
                    v(dve.max(s[:, 8:16], work))
                    v(dve.max_index(i[:, 8:16], s[:, 8:16], work))

                for tile in range(NC):
                    t.take(sc_evac)
                    sel = pg(R_SEL + tile)
                    for hp in range(16):
                        top16(sc[:, hp, :], tmp, top_s[:, hp, :], top_i[:, hp, :])
                    v(dve.tensor_copy(top_f, m0[:, 256:512].bitcast(U32)), sc_used)
                    ts4 = m0[:, 0:256].rearrange("p (h s k) -> p h s k", s=2, k=TK)
                    tf4 = top_f.rearrange("p (h s k) -> p h s k", s=2, k=TK)
                    tt(pg(R_CAND, 4).rearrange("p (h a b) -> p h a b", a=TK, b=TK),
                       ts4[:, :, 0, :].unsqueeze(3).broadcast_to([P, PH, TK, TK]),
                       ts4[:, :, 1, :].unsqueeze(2).broadcast_to([P, PH, TK, TK]), add)
                    bu = best_u.rearrange("p (h k) -> p h k", k=TK)
                    for h in range(PH):
                        top16(cand[:, h, :], tmp2, best_s[:, h, :], bu[:, h, :])
                    tt(e.rearrange("p (h k) -> p h k", k=TK), best_s, best_s[:, :, 0:1].broadcast_to([P, PH, TK]), sub, best_ready)
                    v(dve.tensor_scalar(rank_u[0], best_u, 4, None, ALU.logical_shift_right))
                    v(dve.tensor_scalar(rank_u[1], best_u, 15, None, ALU.bitwise_and))
                    for k in range(2):
                        v(dve.tensor_copy(rank_f[k], rank_u[k]))
                        eq3 = eq.rearrange("p (r a) -> p r a", a=TK)
                        eq4 = eq.rearrange("p (h r a) -> p h r a", r=TK, a=TK)
                        tt(eq3, iota[:, 0:TK].unsqueeze(1).broadcast_to([P, P, TK]), rank_f[k].unsqueeze(2).broadcast_to([P, P, TK]), ALU.is_equal)
                        tt(eq4, eq4, tf4[:, :, k, :].unsqueeze(2).broadcast_to([P, PH, TK, TK]), mul)
                        v(dve.tensor_reduce(sel[:, k * P:(k + 1) * P], eq3, AX.X, add))
                    t.take(best_exp)
                    e3 = e.rearrange("p (h k) -> p h k", k=TK)
                    v(dve.tensor_reduce(total, e3, AX.X, add))
                    v(dve.reciprocal(total, total))
                    tt(sel[:, 2 * P:3 * P].rearrange("p (h k) -> p h k", k=TK), e3, total.unsqueeze(2).broadcast_to([P, PH, TK]), mul, sel_ready)

            def experts(l, ch):
                base = (l * 2 + ch) * (T // 8)
                hb, ha = pg3(OH_B, 16, P), pg3(OH_A, 16, CHUNK_I)
                it, jt, wt = (pg(IJW + k) for k in range(3))
                if ch == 0:
                    dve.wait_ge(selt_evac, NC * (l + 1))
                with dve.Fori(0, T // 16) as i:
                    for half in range(2):
                        dve.wait_ge(outer_done, i * 2 + (base + half + 1))
                        for k in range(8):
                            n = i * 16 + (8 * half + k)
                            s = 8 * half + k
                            dve.tensor_scalar(hb[:, s, :], iota, jt[:, bass.ds(n, 1)], wt[:, bass.ds(n, 1)], ALU.is_equal, mul)
                            ins = dve.tensor_scalar(ha[:, s, :], iota[:, ch * CHUNK_I:(ch + 1) * CHUNK_I], it[:, bass.ds(n, 1)], None, ALU.is_equal)
                        ins.then_inc(hot_ready, 1)
                g0 = l * n_grp + ch * g_chunk
                with dve.Fori(0, g_chunk) as g:
                    for b in range(GRP):
                        dve.wait_ge(gelu_ready, g * GRP + (g0 * GRP + b + 3))
                        gb = gates[:, bass.ds(g * GRP + b, 1), :].rearrange("p a t -> p (a t)")
                        dve.tensor_tensor(gb, gb, pg(GELU + b % 2), mul).then_inc(coef_ready, 1)
                    for m in range(8):
                        dve.wait_ge(mix_done, g * 8 + (g0 * 8 + m + 2))
                        if m == 0:
                            dve.wait_ge(acc_done, g * 8 + (g0 * 8 + 4))
                        dve.tensor_tensor(pg(XT + m), pg(XT + m), ps[:, 2 + m % 4, :], add).then_inc(acc_done, 1)
                dve.wait_ge(acc_done, (g0 + g_chunk) * 8 + 4)

            v(dve.memset(cols[:, :], 0.0))
            v(dve.memset(eps_c, EPS))
            v(dve.memset(ones[:, :], 1.0), ones_ready)
            for k in range(4):
                v(dve.memset(ps[:, 2 + k, 0:1], 0.0), acc_done)
            for k in range(2):
                v(dve.memset(ps[:, 2, 0:1], 0.0), coef_ready)
            dve.wait_ge(c_loaded, 32)
            for l in range(L):
                j0 = l * JOBS
                a_in, c_in = pg3(A_IN, 12, T + 3), pg3(C_IN, 4, T + 3)
                t.take(norm_root)
                t.got[norm_root] -= 1
                v(dve.memset(a_in[:, :, 0:3], 0.0))
                v(dve.memset(c_in[:, :, 0:3], 0.0))
                params(l)
                norm("norm_mix")
                for m in range(4):
                    dve.wait_ge(evac_done, j0 + m + 1)
                    conv(c_in[:, m, :], lambda k: par("conv_c", 4 * m + k), pg(C_X + m), par("conv_cb", m), xc_ready)
                for m in range(12):
                    if m == 4:
                        dve.wait_ge(cgate_evac, 4 * (l + 1))
                        for g in range(4):
                            ts(pg(C_R + g), pg(C_R + g), lamc[:, g:g + 1], None, mul, None, loga_ready if g == 3 else None)
                        t.take(cexp_ready)
                        tt(pg(C_R, 4), pg(C_A, 4), pg(C_A, 4), mul)
                        stt(pg(C_R, 4), pg(C_R, 4), 1.0, pg(YT + 12, 4), add, mul, cm_ready)
                        tt(pg(C_I, 4), pg(C_I, 4), pg(C_X, 4), mul)
                        t.take(csqrt_ready)
                        tt(pg(C_I, 4), pg(C_I, 4), pg(C_R, 4), mul)
                        for g in range(4):
                            v(dve.tensor_tensor_scan(pg(C_X + g), pg(C_A + g), pg(C_I + g), 0.0, mul, add))
                        tt(pg(YT + 8, 4), pg(YT + 8, 4), pg(C_X, 4), mul, y_ready)
                        v(dve.memset(pg(D_K, 4), 0.0), c_done)
                    dve.wait_ge(evac_done, j0 + 8 + m + 1)
                    conv(a_in[:, m, :], lambda k: par("conv_a", 4 * m + k), pg(A_Q + m), None, aconv_ready)
                row_g, row_t = (arena[0:4, a * T:(a + 1) * T] for a in (A_ROWG, A_S))
                t.take(sp_ln)
                stt(row_g, row_g, 0.0, row_t, ALU.max, add)
                ts(row_t, row_g, alog_e[0:4], -1.0, mul, mul)
                for c in range(NC):
                    q = slice(c * C, (c + 1) * C)
                    v(dve.tensor_tensor_scan(row_g[:, q], ones[0:4, :], row_t[:, q], 0.0, mul, add), rows_done if c == NC - 1 else None)
                for m in range(8):
                    t.take(aroot_ready)
                    v(dve.reciprocal(pg(A_MS + m % 4), pg(A_MS + m % 4)))
                    stt(pg(A_Q + m), pg(A_Q + m), P ** -0.5 if m < 4 else 1.0, pg(A_MS + m % 4), mul, mul, qk_ready if m in (3, 7) else None)
                t.take(col_done)
                v(dve.tensor_copy(cols[:, 20:52], ps[:, 6, 0:32]))
                t.take(bc_done)
                t.take(expg_ready)
                for h in range(NH):
                    for c in range(NC):
                        ts(chunks(A_DEC)[:, h * NC + c, :], ps[:, 2 + h, c * C:(c + 1) * C], gct[:, c * NH + h:c * NH + h + 1], 0.0, sub, ALU.min)
                last = ps[:, 2:6, C - 1:T:C]
                tt(kdc.rearrange("p (h c) -> p h c", h=NH), last, gct.rearrange("p (c h) -> p h c", h=NH), sub)
                v(dve.tensor_copy(glc.rearrange("p (h c) -> p h c", h=NH), last), dec_in)
                v(dve.memset(tmpc, 0.0), bc_used)
                t.take(dec_exp)
                tt(chunks(A_DEC), chunks(A_DEC), m_ge.unsqueeze(1).broadcast_to([P, 16, C]), mul)
                for h in range(NH):
                    t.take(prod_done)
                    tt(pg(A_ATT + h), ps[:, 2 + h, :], pg(A_DEC + h), mul, prod_used)
                for h in range(NH):
                    t.take(prod_done)
                    tt(pg(A_DEC + h), ps[:, 2 + h, :], pg(A_DEC + h), mul, prod_used)
                t.take(bc_done)
                tt(pg(A_DEC, 4), pg(A_DEC, 4), ps[:, 2:6, :], mul)
                tt(pg(A_Q, 4), pg(A_Q, 4), pg(A_EXPG, 4), mul)
                tt(pg(A_K, 4), pg(A_K, 4), pg(A_EXPG, 4), mul)
                tt(pg(A_K, 4), pg(A_K, 4), ps[:, 2:6, :], mul)
                for a in (A_X, A_XT):
                    v(dve.tensor_copy(chunks(a), ident.unsqueeze(1).broadcast_to([P, 16, C])), amat_ready if a == A_XT else None)
                for n in range(7):
                    for b in range(NH):
                        t.take(lev_d)
                        tt(pg(A_X + b), pg(A_X + b), ps[:, 6, :], sub)
                        tt(pg(A_XT + b), pg(A_XT + b), ps[:, 7, :], sub, lev_x)
                v(dve.memset(pg(A_S), 0.0), s_ready)
                for c in range(NC):
                    t.take(rs_done)
                    tt(pg3(A_R, NH, C), pg3(A_BV, NH)[:, :, c * C:(c + 1) * C], ps[:, 2, :].rearrange("p (h t) -> p h t", h=NH), sub, r_ready)
                    state_update(pg3(A_S, NH, C), lambda h, c: glc[:, h * NC + c:h * NC + c + 1], c)
                head_norm(A_V, 0, "gdn_norm")
                v(dve.memset(pg(D_K, 4), 0.0), dk_clear)
                t.take(dgate_done)
                for m in range(2):
                    ts(pg(D_F + m), ps[:, 2 + m, :], par("gla_b", m), -1.0, add, mul, sp_in if m else None)
                t.take(sp_ln)
                stt(pg(D_F, 2), pg(D_F, 2), 0.0, pg(L_E, 2), ALU.max, add)
                ts(pg(D_F, 2), pg(D_F, 2), -1.0 / 16, None, mul)
                ts(pg(B_Q, 4), pg(B_Q, 4), P ** -0.5, None, mul)
                t.take(la_sig)
                for h in range(NH):
                    ts(pg(LB_K + h), pg(LB_K + h), lb1[:, h:h + 1], None, mul)
                    ts(pg(B_F + h), pg(B_F + h), lb1[:, h:h + 1], lbc[:, h:h + 1], mul, add)
                ts(pg(B_F, 4), pg(B_F, 4), LN_FLOOR, None, ALU.max, None, la_lnin)
                t.take(la_ln)
                for h in range(NH):
                    scan_chunks(pg(L_B + h), pg(B_F + h), ones[:, :])
                linear(B_Q, LB_K, B_V)
                head_norm(L_O, 4, "hgrn_norm")
                for h in range(NH):
                    scan_chunks(pg(L_B + h), pg(D_F + h // 2), ones[:, :])
                linear(D_Q, D_K, D_V)
                head_norm(L_O, 12, "gla_norm")
                for m in range(8):
                    dve.wait_ge(block_done, l * N_STREAM + N_IN + 2 * m + 2)
                    tt(pg(XT + m), pg(XT + m), ps[:, 6 + m % 2, :], add, op_used)
                v(dve.memset(tmpc, 0.0), x_ready)
                norm("norm_ffn")
                router(l)
                for ch in range(NK // CHUNK_I):
                    experts(l, ch)
            norm("norm_final")

        @block.gpsimd
        def _(pool):
            t = Tally(pool)
            pool.wait_ge(c_loaded, 32)

            def linear(k):
                for n in range(1, 9):
                    t.take(la_e)
                    t.take(la_att, NH)
                    t.done(pool.tensor_tensor(pg(L_KS, 4), pg(k, 4), pg(L_E, 4), ALU.mult), la_k)

            for l in range(L):
                t.take(amat_ready)
                for n in range(7):
                    for b in range(NH):
                        if n:
                            t.take(lev_p)
                        t.done(pool.tensor_tensor(pg(A_MS + b).rearrange("p (c t) -> p c t", t=C),
                                                  pg(A_DEC + b).rearrange("p (c t) -> p c t", t=C),
                                                  m_level(n).unsqueeze(1).broadcast_to([P, NC, C]), ALU.mult), lev_masked)
                t.take(lev_p, NH)
                linear(LB_K)
                linear(D_K)


def constants():
    j, i = np.arange(P)[:, None], np.arange(P)[None, :]
    f = np.concatenate([np.eye(P), np.broadcast_to(i, (P, P))], 1).astype(np.float32)
    masks = [(j // (2 * s) == i // (2 * s)) & (j // s % 2 == 0) & (i // s % 2 == 1) for s in LEVELS] + [i >= j]
    return f, np.concatenate(masks, 1).astype(mybir.dt.np(BF16))


def lay_out(a):
    def blocks(w):
        r, c = w.shape
        return w.reshape(r // P, P, c // P, P).transpose(2, 1, 0, 3).reshape(c // P, P, -1)

    def columns(p):
        return p.reshape(-1, P).T

    stream, pcol, small, wgate = [], [], [], []
    for l in range(L):
        w = a["w_in"][l]
        o = np.cumsum([0, 512, 512, 512, 512, 4, 4, 512, 512, 512, 512, 512, 512, 256, 256, 512, 512, 16])
        aq, ak, av, az, aa, ab, bq, bf, bi, bg, cx, cg, dq, dk, dv, dg, dlr = (w[:, o[k]:o[k + 1]] for k in range(17))

        def tokens(v):
            return v.reshape(4, 2, P, T).transpose(0, 2, 1, 3).reshape(4, P, -1)

        stream += [blocks(m) for m in (cx, cg, aq, ak, av, az, bq, bg, bf)] + [tokens(bi)]
        stream += [blocks(m) for m in (dq, dk, dg)] + [tokens(dv)]
        wo = blocks(a["w_out"][l]).reshape(8, P, 2, D).transpose(0, 2, 1, 3).reshape(16, P, D)
        stream += [wo, blocks(a["peer_w_q"][l])]
        stream.append(a["peer_u"][l].reshape(NK, P, KC, P).transpose(0, 3, 2, 1).reshape(NK, P, D))
        rows = np.zeros((D, 96), np.float32)
        rows[:, 0:4], rows[:, 32:36], rows[:, 64:80] = aa, ab, dlr
        small.append(np.concatenate([rows.reshape(KC, P, 96).transpose(1, 0, 2).reshape(P, -1)] +
                                    [a[k][l].transpose(1, 0, 2).reshape(P, -1) for k in ("lru_w_a", "lru_w_x")], 1))
        wgate.append(a["gla_w_gate"][l])
        c = np.zeros((P, NPC), np.float32)
        for name, val in (("norm_mix", columns(a["norm_mix"][l])), ("norm_ffn", columns(a["norm_ffn"][l])),
                          ("conv_a", a["gdn_conv_w"][l].reshape(4, 12, P).transpose(2, 1, 0).reshape(P, 48)),
                          ("gdn_norm", columns(a["gdn_norm"][l])), ("hgrn_norm", columns(a["hgrn_norm"][l])),
                          ("gla_norm", columns(a["gla_norm"][l])),
                          ("conv_c", a["lru_conv_w"][l].reshape(4, 4, P).transpose(2, 1, 0).reshape(P, 16)),
                          ("conv_cb", columns(a["lru_conv_b"][l])), ("b_a", columns(a["lru_b_a"][l])),
                          ("b_x", columns(a["lru_b_x"][l])), ("lam", columns(a["lru_lambda"][l])),
                          ("gla_b", columns(a["gla_b_gate"][l])), ("norm_final", columns(a["norm_final"]))):
            c[:, PC[name][0]:PC[name][0] + PC[name][1]] = val
        for k in range(L):
            at = PC["lb"][0] + 4 * k
            c[:, at:at + 4] = columns(a["hgrn_lb_logits"][k])
        c[0:4, PC["a_log"][0]], c[0:4, PC["dt"][0]] = a["gdn_a_log"][l], a["gdn_dt_bias"][l]
        pcol.append(c)
    const_f, const_m = constants()
    sk = a["peer_sub_keys"].reshape(L, 16, NK, P).transpose(0, 3, 1, 2).reshape(L, P, 16 * NK)
    return {
        "x": a["x"][0].T.reshape(KC, P, T).transpose(1, 0, 2).reshape(P, KC * T),
        "wstream": np.concatenate(stream, 0), "pcol": np.stack(pcol), "small": np.stack(small),
        "wgate": np.stack(wgate), "skeys": sk, "vexp": a["peer_v"].reshape(L * NK // GRP, GRP, P, D),
        "const_f": const_f, "const_m": const_m,
    }


def kernel(**inputs):
    import concourse.bacc as bacc
    from concourse.bass_utils import run_bass_kernel_spmd

    arrays = {k: np.ascontiguousarray(v) for k, v in lay_out({k: np.asarray(v) for k, v in inputs.items()}).items()}
    nc = bacc.Bacc("TRN2", target_bir_lowering=False, num_devices=1)
    aps = {k: nc.dram_tensor(f"in_{k}", v.shape, mybir.dt.from_np(v.dtype), kind="ExternalInput").ap() for k, v in arrays.items()}
    out = nc.dram_tensor("out_0", (P, KC * T), F32, kind="ExternalOutput").ap()
    build_program(nc, out=out, **aps)
    r = run_bass_kernel_spmd(nc, [{f"in_{k}": v for k, v in arrays.items()}], core_ids=[0])
    y = np.asarray(r.results[0]["out_0"])
    return y.reshape(P, KC, T).transpose(2, 1, 0).reshape(1, T, D)
```

```python
from contextlib import ExitStack

import numpy as np

import concourse.bass as bass
from concourse import mybir

F32 = mybir.dt.float32
F32R = mybir.dt.float32r
BF16 = mybir.dt.bfloat16
U16 = mybir.dt.uint16
U32 = mybir.dt.uint32
ALU = mybir.AluOpType
ACT = mybir.ActivationFunctionType
AX = mybir.AxisListType

P = 128
T = 512
D = 1024
L = 2
KC = D // P
C = P
NC = T // C
NH = 4
NM = 2 * D // P
EPS = 1e-6
PH, NK, TK = 8, 128, 16
LEVELS = [1 << n for n in range(7)]
BIG = -3.0e38
LN_FLOOR = 2.0 ** -63

XT, HT, RING, YT = 0, 8, 16, 24
NPAGES = 101
RING_SLOTS = 4
C_IN, C_X, C_R, C_I, C_A, SMALL = 89, 67, 71, 75, 79, 83
A_IN, A_Q, A_K, A_V, A_ROWG, A_ROWB, A_EXPG = 40, 53, 57, 61, 65, 66, 67
A_DEC, A_ATT, A_X, A_XT, A_MS, A_R, A_P, A_KD, A_BV, A_S, A_VN = 71, 75, 40, 44, 48, 52, 67, 79, 83, 87, 88
LB_K, L_B, L_E, L_QS, L_KS, L_ATT, L_KD, L_O, L_S = 40, 44, 48, 53, 57, 61, 67, 71, 66
B_Q, B_F, B_V = 89, 93, 97
D_Q, D_K, D_F, D_V = 75, 79, 83, 85
R_Q, R_SK, R_SC, R_CAND, R_EQ, R_SM, R_SEL, R_TMP = 24, 40, 44, 48, 52, 56, 60, 64
G_RING, V_RAW, GELU, IJW = 8, 24, 32, 34
OH_B, OH_A, STAGE = 40, 44, 48
SPLIT = 40
S_UHI, S_ULO, S_VHI, S_VLO, S_CHI, S_CLO, S_HHI, S_HLO = 0, 8, 16, 24, 32, 36, 43, 51
UNIT = 4
GRP = 4
NG = 64

PC = {}
_at = 0
for _name, _n in (("norm_mix", 8), ("norm_ffn", 8), ("conv_a", 48), ("gdn_norm", 1), ("hgrn_norm", 1), ("gla_norm", 1),
                  ("conv_c", 16), ("conv_cb", 4), ("b_a", 4), ("b_x", 4), ("lam", 4), ("gla_b", 2), ("lb", 8),
                  ("a_log", 1), ("dt", 1), ("norm_final", 8)):
    PC[_name] = (_at, _n)
    _at += _n
NPC = _at
N_IN = 44 + 8
N_STREAM = N_IN + 16 + 16 + NK


class Tally:

    def __init__(self, eng):
        self.eng, self.put, self.got = eng, {}, {}

    def tell(self, ins, sem):
        ins.then_inc(sem, 1)
        self.put[sem] = self.put.get(sem, 0) + 1

    def done(self, ins, sem):
        self.tell(ins, sem)
        self.eng.wait_ge(sem, self.put[sem])

    def take(self, sem, n=1):
        self.got[sem] = self.got.get(sem, 0) + n
        self.eng.wait_ge(sem, self.got[sem])


def build_program(nc, x, wstream, pcol, small, wgate, skeys, vexp, const_f, const_m, out):
    with ExitStack() as ctx:
        def sb(name, shape, dt=F32):
            return ctx.enter_context(nc.sbuf_tensor(name, shape, dt))

        sems = {}

        def sem(name):
            sems[name] = ctx.enter_context(nc.semaphore(name))
            return sems[name]

        front = sb("front", [P, SPLIT * T])
        with nc.sbuf_tensor("back", [P, (NPAGES - SPLIT) * T], F32) as back:
            pass
        halves = sb("halves", [P, (NPAGES - SPLIT) * T], F32R)
        cf = sb("cf", [P, 2 * P])
        cm = sb("cm", [P, 8 * P], BF16)
        ones = sb("ones", [P, P])
        pc = sb("pc", [P, NPC])
        wg = sb("wg", [80, 2 * P])
        cols = sb("cols", [P, 96])
        ps = ctx.enter_context(nc.psum_tensor("ps", [P, 8, T], F32))

        def mem(lo, hi, parts=slice(0, P)):
            at = SPLIT * T
            assert hi <= at or lo >= at
            return front[parts, lo:hi] if hi <= at else back[parts, lo - at:hi - at]

        def pg(a, n=1):
            return mem(a * T, (a + n) * T)

        def pg3(a, n, w=T):
            return mem(a * T, a * T + n * w).rearrange("p (n t) -> p n t", t=w)

        def hf(a, n=1):
            return halves[:, a * T:(a + n) * T]

        def par(name, k=0, n=1):
            o = PC[name][0] + k
            return pc[:, o:o + n]

        ident = cf[:, 0:P]
        iota = cf[:, P:2 * P]
        m_ge = cm[:, 7 * P:8 * P]

        def m_level(n):
            return cm[:, n * P:(n + 1) * P]

        eps_c, lamc, lbc, lb1, tmpc = cols[:, 0:1], cols[:, 1:5], cols[:, 5:9], cols[:, 9:13], cols[:, 13:17]
        alog_e, one_c = cols[:, 17:18], cols[:, 18:19]
        gct, bct, kdc, glc = cols[:, 20:36], cols[:, 36:52], cols[:, 52:68], cols[:, 68:84]
        lbt = cols[:, 84:96]

        x_loaded, c_loaded, p_loaded, small_loaded, sk_loaded = map(sem, ("x_loaded", "c_loaded", "p_loaded", "small_loaded", "sk_loaded"))
        ring_loaded = [sem(f"ring_loaded{s}") for s in range(RING_SLOTS)]
        v_loaded, out_stored = sem("v_loaded"), sem("out_stored")
        act_step, dve_step, pool_step = sem("act_step"), sem("dve_step"), sem("pool_step")
        x_ready, sq_ready, norm_sum, norm_root, h_ready = map(sem, ("x_ready", "sq_ready", "norm_sum", "norm_root", "h_ready"))
        block_done, evac_done = sem("block_done"), sem("evac_done")
        par_act, par_dve, ones_ready = sem("par_act"), sem("par_dve"), sem("ones_ready")
        tm_done, tm_evac = sem("tm_done"), sem("tm_evac")
        xc_ready, cgate_done, cgate_evac, loga_ready, cexp_ready, cm_ready, csqrt_ready, c_done = map(
            sem, ("xc_ready", "cgate_done", "cgate_evac", "loga_ready", "cexp_ready", "cm_ready", "csqrt_ready", "c_done"))
        aconv_ready, silu_ready, rows_raw, rows_done = map(sem, ("aconv_ready", "silu_ready", "rows_raw", "rows_done"))
        asq_ready, asum_done, aroot_ready, qk_ready = map(sem, ("asq_ready", "asum_done", "aroot_ready", "qk_ready"))
        sp_in, sp_ln = sem("sp_in"), sem("sp_ln")
        bc_done, bc_used, expg_ready, col_done, dec_in, dec_exp, dec_ready = map(
            sem, ("bc_done", "bc_used", "expg_ready", "col_done", "dec_in", "dec_exp", "dec_ready"))
        prod_done, prod_used, tr_done, tr_used = map(sem, ("prod_done", "prod_used", "tr_done", "tr_used"))
        amat_ready, lev_masked, lev_p, lev_pc, lev_d, lev_x = map(sem, ("amat_ready", "lev_masked", "lev_p", "lev_pc", "lev_d", "lev_x"))
        rs_done, r_ready, vn_done, vn_ready, o_done, o_used, s_done, s_ready = map(
            sem, ("rs_done", "r_ready", "vn_done", "vn_ready", "o_done", "o_used", "s_done", "s_ready"))
        osq_ready, osum_done, oroot_ready, y_ready = map(sem, ("osq_ready", "osum_done", "oroot_ready", "y_ready"))
        la_sig, la_lnin, la_ln, la_b, la_diff, la_e, la_q, la_k, la_att, la_used = map(
            sem, ("la_sig", "la_lnin", "la_ln", "la_b", "la_diff", "la_e", "la_q", "la_k", "la_att", "la_used"))
        la_ready, dk_clear, dgate_done = sem("la_ready"), sem("dk_clear"), sem("dgate_done")
        op_done, op_used = sem("op_done"), sem("op_used")
        wq_evac, sc_done, sc_evac, sc_used, best_ready, best_exp, sel_ready, selt_done, selt_evac = map(
            sem, ("wq_evac", "sc_done", "sc_evac", "sc_used", "best_ready", "best_exp", "sel_ready", "selt_done", "selt_evac"))
        hot_ready, outer_done, gate_staged = sem("hot_ready"), sem("outer_done"), sem("gate_staged")
        gate_stored = [sem(f"gate_stored{k}") for k in range(2)]
        gate_loaded, h_hi, h_split = sem("gate_loaded"), sem("h_hi"), sem("h_split")
        u_hi, u_split, v_hi, v_split, c_ready, c_hi = map(sem, ("u_hi", "u_split", "v_hi", "v_split", "c_ready", "c_hi"))
        gelu_ready, coef_ready, mix_done, acc_done = map(sem, ("gelu_ready", "coef_ready", "mix_done", "acc_done"))
        gates_dram = nc.dram_tensor("gates_dram", (L, T // NG, P, NK * NG), F32, kind="Internal").ap()

        lowrank = mem(A_ROWG * T, (A_ROWG + 1) * T, slice(64, 80))
        block = ctx.enter_context(nc.Block())

        yT = pg3(YT, NM)
        hT = pg3(HT, KC)
        xT = pg3(XT, KC)
        n_grp = NK // GRP
        n_gran = T // NG
        n_unit = T // UNIT

        def slot(s, w=P):
            return mem((RING + 2 * s) * T, (RING + 2 * s + 2) * T).rearrange("p (k m) -> p k m", m=w)

        def stage(k):
            return pg(STAGE + 16 * k, 16).rearrange("p (i n) -> p i n", n=NG)

        @block.sync
        def _(sp):
            t = Tally(sp)
            sp.dma_start(pg(XT, KC), x).then_inc(x_loaded, 16)
            sp.dma_start(cf[:, :], const_f).then_inc(c_loaded, 16)
            sp.dma_start(cm[:, :], const_m).then_inc(c_loaded, 16)
            for l in range(L):
                if l:
                    sp.wait_ge(acc_done, 4 + l * NK // GRP * 8)
                sp.dma_start(pc[:, :], pcol[l]).then_inc(p_loaded, 16)
                sp.dma_start(wg[64:80, :], wgate[l]).then_inc(p_loaded, 16)
                sp.dma_start(pg(SMALL, 4)[:, 0:1792], small[l]).then_inc(small_loaded, 16)
                base = l * N_STREAM
                for n in range(N_IN + 32):
                    k = base + n
                    if k >= RING_SLOTS:
                        sp.wait_ge(block_done, k - RING_SLOTS + 1)
                    sp.dma_start(mem((RING + 2 * (n % 4)) * T, (RING + 2 * (n % 4) + 2) * T), wstream[k]).then_inc(ring_loaded[n % 4], 16)
                    if n == N_IN + 16:
                        t.take(y_ready, 4)
                        sp.dma_start(pg(R_SK, 4), skeys[l]).then_inc(sk_loaded, 16)
                for q in range(n_gran):
                    sp.wait_ge(gate_staged, UNIT + l * n_unit + (q + 1) * NG // UNIT)
                    sp.dma_start(gates_dram[l, q], pg(STAGE + 16 * (q % 2), 16)).then_inc(gate_stored[q % 2], 16)

                def load_keys(g, waits):
                    for s in range(GRP):
                        waits(s)
                        sp.dma_start(mem((RING + 2 * s) * T, (RING + 2 * s + 2) * T),
                                     wstream[bass.ds(g * GRP + (base + N_IN + 32 + s), 1)].rearrange("a p n -> p (a n)")
                                     ).then_inc(ring_loaded[s], 16)

                def load_values(g):
                    sp.dma_start(pg(V_RAW, 2 * GRP).rearrange("p (b d) -> p b d", b=GRP),
                                 vexp[bass.ds(g + l * n_grp, 1)].rearrange("a b p d -> p (a b) d")).then_inc(v_loaded, 16)

                def load_gates(g):
                    src = gates_dram[l].rearrange("q j (i n) -> j i q n", n=NG)
                    for b in range(GRP):
                        sp.dma_start(pg(G_RING + b).rearrange("p (q n) -> p q n", n=NG),
                                     src[:, bass.ds(g * GRP + b, 1)].rearrange("j a q n -> j (a q) n")).then_inc(gate_loaded, 16)

                load_keys(0, lambda s: sp.wait_ge(block_done, base + N_IN + 32 + s - RING_SLOTS + 1))
                load_values(0)
                for k in range(2):
                    sp.wait_ge(gate_stored[k], 16 * (n_gran // 2) * (l + 1))
                sp.wait_ge(h_split, l + 1)
                load_gates(0)
                with sp.Fori(0, n_grp - 1) as g:
                    load_keys(g + 1, lambda s: sp.wait_ge(u_split, g * GRP + (l * NK + s + 1)))
                    sp.wait_ge(v_split, g * GRP + (l * NK + GRP))
                    load_values(g + 1)
                    sp.wait_ge(coef_ready, g * GRP + (l * NK + GRP))
                    load_gates(g + 1)
            sp.wait_ge(h_ready, 2 * L + 1)
            sp.dma_start(out, pg(HT, KC)).then_inc(out_stored, 16)
            sp.wait_ge(out_stored, 16)

        JOBS = 45 + 16

        @block.tensor
        def _(pe):
            t = Tally(pe)
            nblk = [0]
            jobs = [0]

            def norm():
                t.take(sq_ready, 2)
                for k in range(KC):
                    ins = pe.matmul(ps[:, 7, :], ones[:, :], pg(YT + k), start=k == 0, stop=k == KC - 1)
                t.tell(ins, norm_sum)
                t.take(h_ready)

            def bank():
                if jobs[0] >= 2:
                    t.take(evac_done)
                jobs[0] += 1
                return (jobs[0] - 1) % 2

            def next_slot():
                s = nblk[0] % RING_SLOTS
                pe.wait_ge(ring_loaded[s], 16 * (nblk[0] // RING_SLOTS + 1))
                nblk[0] += 1
                return s

            def project(n):
                for _ in range(n):
                    b, s = bank(), next_slot()
                    for k in range(KC):
                        ins = pe.matmul(ps[:, b, :], slot(s)[:, k, :], hT[:, k, :], start=k == 0, stop=k == KC - 1)
                    ins.then_inc(block_done, 1)

            def project_small():
                b = bank()
                sw = mem(SMALL * T, SMALL * T + 768).rearrange("p (k m) -> p k m", m=96)
                for k in range(KC):
                    ins = pe.matmul(ps[0:96, b, :], sw[:, k, :], hT[:, k, :], start=k == 0, stop=k == KC - 1)
                t.tell(ins, rows_raw)

            def project_tokens():
                for q in range(4):
                    s = next_slot()
                    for k in range(2):
                        for c in range(NC):
                            ins = pe.matmul(ps[:, 2 + c, :], hT[:, 2 * q + k, c * C:(c + 1) * C], slot(s, T)[:, k, :],
                                            start=q == 0 and k == 0, stop=q == 3 and k == 1)
                    ins.then_inc(block_done, 1)
                t.take(tm_evac)

            def group_c():
                sw = mem(SMALL * T + 768, SMALL * T + 1792).rearrange("p (g m) -> p g m", m=P)
                for g in range(4):
                    t.take(xc_ready)
                    if g:
                        t.take(cgate_evac)
                    pe.matmul(ps[:, 6, :], sw[:, g, :], pg(C_X + g), start=True, stop=True)
                    t.tell(pe.matmul(ps[:, 7, :], sw[:, 4 + g, :], pg(C_X + g), start=True, stop=True), cgate_done)
                t.take(cgate_evac)

            def level_systems(b):
                return [(b, c) for c in range(NC)]

            def transposes(src, use):
                for b in range(NH):
                    for c in range(NC):
                        ins = pe.transpose(ps[:, 2 + b, c * C:(c + 1) * C], src[:, b, c * C:(c + 1) * C], ident)
                    t.tell(ins, tr_done)
                t.take(tr_used, 4)

            def group_a():
                qT, kT, vT = pg3(A_Q, NH), pg3(A_K, NH), pg3(A_V, NH)
                for m in range(8):
                    t.take(asq_ready)
                    ins = pe.matmul(ps[:, 6 + m % 2, :], ones[:, :], pg(A_X + m), start=True, stop=True)
                    t.tell(ins, asum_done)
                    if m >= 1:
                        t.take(aroot_ready)
                t.take(aroot_ready)
                t.take(rows_done)
                for c in range(NC):
                    pe.transpose(ps[:, 6, c * 4:c * 4 + 4], mem(A_ROWG * T + c * C, A_ROWG * T + (c + 1) * C, slice(0, 4)), ident[0:4, 0:4])
                    ins = pe.transpose(ps[:, 6, 16 + c * 4:20 + c * 4], mem(A_ROWB * T + c * C, A_ROWB * T + (c + 1) * C, slice(0, 4)), ident[0:4, 0:4])
                t.tell(ins, col_done)
                for h in range(NH):
                    ins = pe.matmul(ps[:, 2 + h, :], ident[0:4, h:h + 1].broadcast_to([4, P]), mem(A_ROWG * T, (A_ROWG + 1) * T, slice(0, 4)), start=True, stop=True)
                t.tell(ins, bc_done)
                t.take(bc_used)
                t.take(qk_ready, 2)
                for rhs in (qT, kT):
                    for h in range(NH):
                        for c in range(NC):
                            ins = pe.matmul(ps[:, 2 + h, c * C:(c + 1) * C], kT[:, h, c * C:(c + 1) * C], rhs[:, h, c * C:(c + 1) * C], start=True, stop=True)
                        t.tell(ins, prod_done)
                    t.take(prod_used, 4)
                transposes(kT, None)
                transposes(vT, None)
                for h in range(NH):
                    ins = pe.matmul(ps[:, 2 + h, :], ident[0:4, h:h + 1].broadcast_to([4, P]), mem(A_ROWB * T, (A_ROWB + 1) * T, slice(0, 4)), start=True, stop=True)
                t.tell(ins, bc_done)
                X, XTr, MS, PP = pg3(A_X, NH), pg3(A_XT, NH), pg3(A_MS, NH), pg3(A_P, NH)
                t.take(amat_ready)
                for n in range(7):
                    for b in range(NH):
                        t.take(lev_masked)
                        for c in range(NC):
                            q = slice(c * C, (c + 1) * C)
                            ins = pe.matmul(ps[:, 2 + b, q], MS[:, b, q], X[:, b, q], start=True, stop=True)
                        t.tell(ins, lev_p)
                    for b in range(NH):
                        t.take(lev_pc)
                        for c in range(NC):
                            q = slice(c * C, (c + 1) * C)
                            pe.matmul(ps[:, 6, q], XTr[:, b, q], PP[:, b, q], start=True, stop=True)
                        for c in range(NC):
                            q = slice(c * C, (c + 1) * C)
                            ins = pe.matmul(ps[:, 7, q], PP[:, b, q], XTr[:, b, q], start=True, stop=True)
                        t.tell(ins, lev_d)
                        t.take(lev_x)
                S, VN, R, ATT, KD = pg3(A_S, NH, C), pg3(A_VN, NH, C), pg3(A_R, NH, C), pg3(A_ATT, NH), pg3(A_KD, NH)
                t.take(s_ready)
                for c in range(NC):
                    q = slice(c * C, (c + 1) * C)
                    for h in range(NH):
                        ins = pe.matmul(ps[:, 2, h * C:(h + 1) * C], kT[:, h, q], S[:, h, :], start=True, stop=True)
                    t.tell(ins, rs_done)
                    t.take(r_ready)
                    for h in range(NH):
                        ins = pe.matmul(ps[:, 3, h * C:(h + 1) * C], XTr[:, h, q], R[:, h, :], start=True, stop=True)
                    t.tell(ins, vn_done)
                    t.take(vn_ready)
                    for h in range(NH):
                        pe.matmul(ps[:, 4, h * C:(h + 1) * C], S[:, h, :], qT[:, h, q], start=True, stop=False)
                        ins = pe.matmul(ps[:, 4, h * C:(h + 1) * C], VN[:, h, :], ATT[:, h, q], start=False, stop=True)
                    t.tell(ins, o_done)
                    for h in range(NH):
                        ins = pe.matmul(ps[:, 5, h * C:(h + 1) * C], KD[:, h, q], VN[:, h, :], start=True, stop=True)
                    t.tell(ins, s_done)
                    t.take(s_ready)
                    t.take(o_used)

            def head_norm():
                for h in range(NH):
                    t.take(osq_ready)
                    t.tell(pe.matmul(ps[:, 2 + h, :], ones[:, :], pg(L_E + h), start=True, stop=True), osum_done)
                t.take(oroot_ready, 4)

            def gate_d():
                for m in range(2):
                    ins = pe.matmul(ps[:, 2 + m, :], wg[64:80, m * P:(m + 1) * P], lowrank, start=True, stop=True)
                t.tell(ins, dgate_done)

            def linear(qa, ka, va):
                qT, kT, QS, KS = pg3(qa, NH), pg3(ka, NH), pg3(L_QS, NH), pg3(L_KS, NH)
                ATT, KD, S, V = pg3(L_ATT, NH), pg3(L_KD, NH), pg3(L_S, NH, C), pg3(va, NC)
                t.take(la_ready)
                for n in range(8):
                    a, b = (kT, qT) if n == 0 else (KS, QS)
                    if n:
                        t.take(la_q)
                        t.take(la_k)
                    for h in range(NH):
                        if n:
                            t.take(la_used)
                        for c in range(NC):
                            q = slice(c * C, (c + 1) * C)
                            ins = pe.matmul(ps[:, 2 + h, q], a[:, h, q], b[:, h, q], start=True, stop=True)
                        t.tell(ins, la_att)
                t.take(la_used, 4)
                t.take(la_q)
                t.take(la_k)
                transposes(KS, None)
                t.take(s_ready)
                for c in range(NC):
                    q = slice(c * C, (c + 1) * C)
                    for h in range(NH):
                        pe.matmul(ps[:, 4, h * C:(h + 1) * C], S[:, h, :], QS[:, h, q], start=True, stop=False)
                        ins = pe.matmul(ps[:, 4, h * C:(h + 1) * C], V[:, c, h * C:(h + 1) * C], ATT[:, h, q], start=False, stop=True)
                    t.tell(ins, o_done)
                    for h in range(NH):
                        ins = pe.matmul(ps[:, 5, h * C:(h + 1) * C], KD[:, h, q], V[:, c, h * C:(h + 1) * C], start=True, stop=True)
                    t.tell(ins, s_done)
                    t.take(s_ready)
                    t.take(o_used)

            def out_projection():
                t.take(y_ready, 4)
                for m in range(8):
                    if m >= 2:
                        t.take(op_used)
                    for half in range(2):
                        s = next_slot()
                        for k in range(8):
                            ins = pe.matmul(ps[:, 6 + m % 2, :], slot(s)[:, k, :], yT[:, 8 * half + k, :],
                                            start=half == 0 and k == 0, stop=half == 1 and k == 7)
                        ins.then_inc(block_done, 1)
                t.take(op_used, 2)

            def router(l):
                qT = pg3(R_Q, 16)
                sk = pg3(R_SK, 16, P)
                pe.wait_ge(sk_loaded, 16 * (l + 1))
                pe.wait_ge(evac_done, jobs[0])
                for tile in range(NC):
                    if tile:
                        t.take(sc_evac)
                    for hp in range(16):
                        ins = pe.matmul(ps[:, 2 + hp // 4, (hp % 4) * P:(hp % 4 + 1) * P], qT[:, hp, tile * C:(tile + 1) * C], sk[:, hp, :], start=True, stop=True)
                    t.tell(ins, sc_done)
                t.take(sc_evac)
                for tile in range(NC):
                    t.take(sel_ready)
                    if tile:
                        t.take(selt_evac)
                    for k in range(3):
                        ins = pe.transpose(ps[:, 6, k * P:(k + 1) * P], pg(R_SEL + tile)[:, k * P:(k + 1) * P], ident)
                    t.tell(ins, selt_done)
                t.take(selt_evac)

            def build_gates(l):
                hb, ha = pg3(OH_B, 16, P), pg3(OH_A, 16, P)
                with pe.Fori(0, T // 16) as i:
                    for u in range(4):
                        pe.wait_ge(hot_ready, i * 4 + (l * n_unit + u + 1))
                        pe.wait_ge(gate_staged, i * 4 + (l * n_unit + u + 1))
                        for k in range(UNIT):
                            ins = pe.matmul(ps[:, u, k * P:(k + 1) * P], hb[:, UNIT * u + k, :], ha[:, UNIT * u + k, :], start=True, stop=True)
                        ins.then_inc(outer_done, 1)

            def halves3(w_hi, w_lo, m_hi, m_lo):
                return (w_hi, m_hi), (w_hi, m_lo), (w_lo, m_hi)

            def experts(l):
                n0, g0 = l * NK, l * n_grp
                pe.wait_ge(gate_staged, UNIT + (l + 1) * n_unit)
                pe.wait_ge(h_split, l + 1)
                with pe.Fori(0, n_grp) as g:
                    for b in range(GRP):
                        pe.wait_ge(u_split, g * GRP + (n0 + b + 1))
                        pe.wait_ge(gelu_ready, g * GRP + (n0 + b + 1))
                        for k in range(KC):
                            q = slice(k * P, (k + 1) * P)
                            terms = halves3(hf(S_UHI + 2 * b, 2)[:, q], hf(S_ULO + 2 * b, 2)[:, q], hf(S_HHI + k), hf(S_HLO + k))
                            for n, (w, m) in enumerate(terms):
                                ins = pe.matmul(ps[:, b % 2, :], w, m, start=k == 0 and n == 0, stop=k == KC - 1 and n == 2)
                        ins.then_inc(block_done, 1)
                    pe.wait_ge(v_split, g * GRP + (n0 + GRP))
                    for m0 in range(0, 8, 4):
                        for blocks in (range(GRP - 1), range(GRP - 1, GRP)):
                            if m0 == 0:
                                pe.wait_ge(coef_ready, g * GRP + (n0 + blocks[-1] + 1))
                            for m_ in range(m0, m0 + 4):
                                if blocks[0] == 0:
                                    pe.wait_ge(acc_done, g * 8 + (g0 * 8 + m_ + 1))
                                q = slice(m_ * P, (m_ + 1) * P)
                                for b in blocks:
                                    terms = halves3(hf(S_VHI + 2 * b, 2)[:, q], hf(S_VLO + 2 * b, 2)[:, q], hf(S_CHI + b), hf(S_CLO + b))
                                    for n, (w, m) in enumerate(terms):
                                        ins = pe.matmul(ps[:, 2 + m_ % 4, :], w, m, start=b == 0 and n == 0, stop=b == GRP - 1 and n == 2)
                                if blocks[-1] == GRP - 1:
                                    ins.then_inc(mix_done, 1)
                pe.wait_ge(acc_done, (g0 + n_grp) * 8 + 4)

            pe.wait_ge(c_loaded, 32)
            t.take(ones_ready)
            for k in range(5):
                pe.matmul(ps[:, 6, 0:P], ones[:, :], ones[:, :], start=True, stop=True).then_inc(mix_done if k == 4 else outer_done, 1)
            for l in range(L):
                norm()
                project(8)
                project(16)
                pe.wait_ge(small_loaded, 16 * (l + 1))
                project_small()
                group_c()
                project(12)
                project_tokens()
                group_a()
                head_norm()
                project(8)
                project_tokens()
                gate_d()
                linear(B_Q, LB_K, B_V)
                head_norm()
                linear(D_Q, D_K, D_V)
                head_norm()
                out_projection()
                norm()
                project(16)
                router(l)
                build_gates(l)
                experts(l)
                nblk[0] += NK
            norm()


        @block.scalar
        def _(act):
            t = Tally(act)

            def f(out_, in_, func, sem_=None, **kw):
                t.done(act.activation(out_, in_, func, **kw), sem_ or act_step)

            def norm(l, first, scale=1.0 / D):
                if first and l == 0:
                    act.wait_ge(x_loaded, 16)
                elif first:
                    act.wait_ge(acc_done, 4 + l * n_grp * 8)
                else:
                    t.take(x_ready)
                for k in range(2):
                    f(pg(YT + 4 * k, 4), pg(XT + 4 * k, 4), ACT.Square, sq_ready)
                t.take(norm_sum)
                f(pg(YT + 8), ps[:, 7, :], ACT.Sqrt, norm_root, scale=scale, bias=eps_c)

            jobs = [0]

            def evacs(n, write):
                for m in range(n):
                    t.take(block_done)
                    write(m, ps[:, jobs[0] % 2, :])
                    jobs[0] += 1

            def softplus_tail(z, tmp, sig_):
                f(tmp, z, ACT.Abs)
                f(tmp, tmp, ACT.Exp, scale=-1.0)
                f(tmp, tmp, ACT.Ln, sig_, bias=1.0)

            def params(l):
                act.wait_ge(p_loaded, 32 * (l + 1))
                f(alog_e[0:4], par("a_log")[0:4], ACT.Exp)
                softplus_tail(par("lam", 0, 4), tmpc, par_act)
                t.take(par_dve)
                f(lbt[:, 0:8], lbt[:, 0:8], ACT.Exp, par_act)

            def tokens(dst):
                t.take(block_done, 4)
                f(pg(dst, 4), ps[:, 2:6, :], ACT.Copy, tm_evac)

            def store(dst):
                return lambda m, src: f(pg(dst + m), src, ACT.Copy, evac_done)

            def head_norm(o):
                for h in range(NH):
                    f(pg(L_E + h), pg(o + h), ACT.Square, osq_ready)
                for h in range(NH):
                    t.take(osum_done)
                    f(pg(L_QS + h), ps[:, 2 + h, :], ACT.Sqrt, oroot_ready, scale=1.0 / P, bias=eps_c)

            def recurrence(o, delta):
                for c in range(NC):
                    q = slice(c * C, (c + 1) * C)
                    if delta:
                        t.take(vn_done)
                        f(pg(A_VN), ps[:, 3, :], ACT.Copy, vn_ready)
                    t.take(o_done)
                    f(pg3(o, NH)[:, :, q], ps[:, 4, :].rearrange("p (h t) -> p h t", h=NH), ACT.Copy, o_used)

            def linear(f_page, k_page, b_page, n_level_signals):
                for n in range(1, 9):
                    t.take(la_diff)
                    f(pg(L_E, 4), pg(L_E, 4), ACT.Abs)
                    if n == 8:
                        f(pg(L_B, 4), pg(L_B, 4), ACT.Exp)
                    f(pg(L_E, 4), pg(L_E, 4), ACT.Exp, la_e, scale=-1.0)
                for h in range(NH):
                    t.take(tr_done)
                    f(pg(L_KD + h), ps[:, 2 + h, :], ACT.Copy, tr_used)
                recurrence(L_O, False)
                head_norm(L_O)

            t.take(ones_ready)
            for k in range(6):
                f(ps[:, k % 2, k:k + 1], ones[:, 0:1], ACT.Copy, gate_staged if k < 4 else gelu_ready)
            for l in range(L):
                norm(l, True)
                params(l)
                c_in = pg3(C_IN, 4, T + 3)
                evacs(4, lambda m, src: f(c_in[:, m, 3:T + 3], src, ACT.Copy, evac_done))
                evacs(4, lambda m, src: f(pg(YT + 8 + m), src, ACT.Gelu_apprx_tanh, evac_done))
                a_in = pg3(A_IN, 12, T + 3)
                evacs(12, lambda m, src: f(a_in[:, m, 3:T + 3], src, ACT.Copy, evac_done))
                evacs(4, lambda m, src: f(pg(YT + m), src, ACT.Silu, evac_done))
                t.take(rows_raw)
                src = ps[:, jobs[0] % 2, :]
                jobs[0] += 1
                row_g, row_b, row_t = (mem(a * T, (a + 1) * T, slice(0, 4)) for a in (A_ROWG, A_ROWB, A_S))
                f(row_g, src[0:4], ACT.Identity, bias=par("dt")[0:4])
                f(lowrank, src[64:80], ACT.Copy)
                f(row_b, src[32:36], ACT.Sigmoid, evac_done)
                for g in range(4):
                    t.take(cgate_done)
                    f(pg(C_R + g), ps[:, 6, :], ACT.Sigmoid, bias=par("b_a", g))
                    f(pg(C_I + g), ps[:, 7, :], ACT.Sigmoid, cgate_evac, bias=par("b_x", g))
                t.take(loga_ready)
                f(pg(C_A, 4), pg(C_R, 4), ACT.Exp)
                f(pg(YT + 12, 4), pg(C_R, 4), ACT.Tanh, cexp_ready, scale=-1.0)
                t.take(cm_ready)
                f(pg(C_R, 4), pg(C_R, 4), ACT.Sqrt, csqrt_ready)
                softplus_tail(row_g, row_t, sp_ln)
                t.take(c_done)
                for m in range(12):
                    t.take(aconv_ready)
                    f(pg(A_Q + m), pg(A_Q + m), ACT.Silu)
                    t.take(block_done)
                    src = ps[:, jobs[0] % 2, :]
                    jobs[0] += 1
                    if m < 4:
                        f(pg(B_Q + m), src, ACT.Silu, evac_done)
                    elif m < 8:
                        f(pg(YT + m), src, ACT.Silu, evac_done)
                    else:
                        f(pg(B_F + m - 8), src, ACT.Copy, evac_done)
                tokens(B_V)
                for m in range(8):
                    f(pg(A_X + m), pg(A_Q + m), ACT.Square, asq_ready)
                for m in range(8):
                    t.take(asum_done)
                    if m == 4:
                        t.take(qk_ready)
                    f(pg(A_MS + m % 4), ps[:, 6 + m % 2, :], ACT.Sqrt, aroot_ready, bias=eps_c)
                t.take(qk_ready)
                t.take(bc_done)
                f(pg(A_EXPG, 4), ps[:, 2:6, :], ACT.Exp, expg_ready)
                t.take(dec_in)
                f(pg(A_DEC, 4), pg(A_DEC, 4), ACT.Exp)
                f(cols[:, 52:84], cols[:, 52:84], ACT.Exp, dec_exp)
                for dst, scale in ((A_KD, kdc), (A_BV, bct)):
                    for h in range(NH):
                        t.take(tr_done)
                        for c in range(NC):
                            col = scale[:, h * NC + c:h * NC + c + 1] if dst == A_KD else scale[:, c * NH + h:c * NH + h + 1]
                            f(pg3(dst, NH)[:, h, c * C:(c + 1) * C], ps[:, 2 + h, c * C:(c + 1) * C], ACT.Copy,
                              tr_used if c == NC - 1 else None, scale=col)
                t.take(bc_done)
                for n in range(7):
                    for b in range(NH):
                        t.take(lev_p)
                        f(pg(A_P + b), ps[:, 2 + b, :], ACT.Copy, lev_pc)
                recurrence(A_V, True)
                head_norm(A_V)
                t.take(dk_clear)
                for m in range(2):
                    t.take(block_done)
                    src = ps[:, jobs[0] % 2, :]
                    jobs[0] += 1
                    f(pg(D_Q + 2 * m), src, ACT.Copy, scale=64 ** -0.5)
                    f(pg(D_Q + 2 * m + 1), src, ACT.Copy, evac_done, scale=64 ** -0.5)
                for m in range(2):
                    t.take(block_done)
                    src = ps[:, jobs[0] % 2, :]
                    jobs[0] += 1
                    f(pg(D_K + 2 * m)[0:64], src[0:64], ACT.Copy)
                    f(pg(D_K + 2 * m + 1)[64:128], src[64:128], ACT.Copy, evac_done)
                evacs(4, lambda m, src: f(pg(YT + 12 + m), src, ACT.Silu, evac_done))
                tokens(D_V)
                t.take(sp_in)
                softplus_tail(pg(D_F, 2), pg(L_E, 2), sp_ln)
                f(pg(LB_K, 4), pg(B_F, 4), ACT.Sigmoid, scale=-1.0)
                f(pg(B_F, 4), pg(B_F, 4), ACT.Sigmoid, la_sig)
                t.take(la_lnin)
                f(pg(B_F, 4), pg(B_F, 4), ACT.Ln, la_ln)
                linear(B_F, LB_K, L_B, 9)
                linear(D_F, D_K, L_B, 9)
                norm(l, False)
                act.wait_ge(h_ready, 2 * l + 2)
                f(hf(S_HHI, KC), pg(HT, KC), ACT.Copy, h_hi)
                t.got[block_done] += 16
                evacs(16, store(R_Q))

                def scores(tile):
                    t.take(sc_done)
                    if tile:
                        t.take(sc_used)
                    f(pg(R_SC, 4), ps[:, 2:6, :], ACT.Copy, sc_evac)

                scores(0)
                for tile in range(NC):
                    if tile + 1 < NC:
                        scores(tile + 1)
                    t.take(best_ready)
                    best = pg(R_SM + 3)[:, 0:P]
                    f(best, best, ACT.Exp, best_exp)
                t.take(sc_used)
                for tile in range(NC):
                    t.take(selt_done)
                    f(pg3(IJW, 3)[:, :, tile * C:(tile + 1) * C], ps[:, 6, 0:3 * P].rearrange("p (k t) -> p k t", k=3), ACT.Copy, selt_evac)
                for q in range(n_gran):
                    if q >= 2 or l:
                        act.wait_ge(gate_stored[q % 2], 16 * (l * n_gran // 2 + q // 2))
                    with act.Fori(0, NG // 16) as i:
                        for u in range(4):
                            act.wait_ge(outer_done, i * 4 + (UNIT + l * n_unit + q * NG // UNIT + u + 1))
                            act.activation(stage(q % 2)[:, :, bass.ds(i * 16 + UNIT * u, UNIT)],
                                           ps[:, u, :].rearrange("p (n i) -> p i n", n=UNIT), ACT.Copy).then_inc(gate_staged, 1)
                n0, g0, k0 = l * NK, l * n_grp, l * N_STREAM + N_IN + 32

                def split_keys(g, free):
                    for s in range(GRP):
                        act.wait_ge(ring_loaded[s], g * 16 + 16 * (k0 // 4 + 1))
                        free(s)
                        act.activation(hf(S_UHI + 2 * s, 2), pg(RING + 2 * s, 2), ACT.Copy).then_inc(u_hi, 1)

                def group(g, last):
                    act.wait_ge(v_loaded, g * 16 + 16 * (g0 + 1))
                    act.wait_ge(mix_done, g * 8 + (g0 * 8 + 1))
                    for b in range(GRP):
                        act.activation(hf(S_VHI + 2 * b, 2), pg(V_RAW + 2 * b, 2), ACT.Copy).then_inc(v_hi, 1)
                        act.wait_ge(block_done, g * GRP + (k0 + b + 1))
                        act.wait_ge(c_ready, g * GRP + (n0 + b + 1))
                        act.activation(pg(GELU + b % 2), ps[:, b % 2, :], ACT.Gelu_apprx_tanh).then_inc(gelu_ready, 1)
                        act.wait_ge(c_ready, g * GRP + (n0 + b + 3))
                        act.activation(hf(S_CHI + b), pg(G_RING + b), ACT.Copy).then_inc(c_hi, 1)
                    if not last:
                        split_keys(g + 1, lambda s: act.wait_ge(block_done, g * GRP + (k0 + s + 1)))

                for k in range(2):
                    act.wait_ge(gate_stored[k], 16 * (n_gran // 2) * (l + 1))
                split_keys(0, lambda s: None)
                with act.Fori(0, n_grp - 1) as g:
                    group(g, False)
                group(n_grp - 1, True)
                t.got[block_done] = (l + 1) * N_STREAM
            norm(L, True)

        @block.vector
        def _(dve):
            t = Tally(dve)
            mul, add, sub = ALU.mult, ALU.add, ALU.subtract

            def v(ins, sem_=None):
                t.done(ins, sem_ or dve_step)

            def tt(o, a, b, op, sem_=None):
                v(dve.tensor_tensor(o, a, b, op), sem_)

            def ts(o, a, s1, s2, op0, op1=None, sem_=None):
                v(dve.tensor_scalar(o, a, s1, s2, op0, op1) if op1 is not None else dve.tensor_scalar(o, a, s1, s2, op0), sem_)

            def stt(o, a, s, b, op0, op1, sem_=None):
                v(dve.scalar_tensor_tensor(out=o, in0=a, scalar=s, in1=b, op0=op0, op1=op1), sem_)

            def norm(name):
                t.take(norm_root)
                v(dve.reciprocal(pg(YT + 8), pg(YT + 8)))
                for k in range(KC):
                    stt(pg(HT + k), pg(XT + k), par(name, k), pg(YT + 8), mul, mul, h_ready if k == KC - 1 else None)

            def conv(src, w, dst, bias, sem_):
                if bias is None:
                    ts(dst, src[:, 0:T], w(0), None, mul)
                else:
                    ts(dst, src[:, 0:T], w(0), bias, mul, add)
                for k in range(1, 4):
                    stt(dst, src[:, k:k + T], w(k), dst, mul, add, sem_ if k == 3 else None)

            def params(l):
                dve.wait_ge(p_loaded, 32 * (l + 1))
                lb = [par("lb", 4 * k, 4) for k in range(L)]
                tt(lbt[:, 8:12], lb[0], lb[1], ALU.max)
                tt(lbt[:, 0:4], lb[0], lbt[:, 8:12], sub)
                tt(lbt[:, 4:8], lb[1], lbt[:, 8:12], sub, par_dve)
                t.take(par_act)
                ts(lamc, par("lam", 0, 4), -1.0, 0.0, mul, ALU.max)
                tt(lamc, lamc, tmpc, add)
                ts(lamc, lamc, -8.0, None, mul)
                t.take(par_act)
                tt(lbt[:, 8:12], lbt[:, 0:4], lbt[:, 4:8], add)
                v(dve.reciprocal(lbt[:, 8:12], lbt[:, 8:12]))
                ts(lbc, lbt[:, 4:8], float(l), None, mul)
                tt(lbc, lbc, lbt[:, 8:12], mul)
                ts(lb1, lbc, -1.0, 1.0, mul, add)

            def heads(a, n=NH):
                return pg3(a, n)

            def chunks(a):
                return pg(a, 4).rearrange("p (s t) -> p s t", t=C)

            def head_norm(o, y, wname):
                for h in range(NH):
                    t.take(oroot_ready)
                    v(dve.reciprocal(pg(L_QS + h), pg(L_QS + h)))
                    stt(pg(o + h), pg(o + h), par(wname), pg(L_QS + h), mul, mul)
                    tt(pg(YT + y + h), pg(YT + y + h), pg(o + h), mul, y_ready if h == NH - 1 else None)

            def state_update(S, col, c):
                t.take(s_done)
                for h in range(NH):
                    stt(S[:, h, :], S[:, h, :], col(h, c), ps[:, 5, h * C:(h + 1) * C], mul, add, s_ready if h == NH - 1 else None)

            def linear(q, k, v_):
                tt_mask = ident.unsqueeze(1).broadcast_to([P, NC, C])
                v(dve.memset(pg(L_S), 0.0), la_ready)
                for n in range(9):
                    if n:
                        s2 = 2 * LEVELS[min(n, 7) - 1]
                        at = s2 // 2 - 1 if n < 8 else C - 1
                        bv = pg(L_B, 4).rearrange("p (s t) -> p s t", t=s2)
                        ev = pg(L_E, 4).rearrange("p (s t) -> p s t", t=s2)
                        if n > 1:
                            t.take(la_k)
                        tt(ev, bv, bv[:, :, at:at + 1].broadcast_to([P, 4 * T // s2, s2]), sub, la_diff)
                        t.take(la_e)
                        tt(pg(L_QS, 4), pg(q, 4), pg(L_E if n < 8 else L_B, 4), mul, la_q)
                    if n == 8:
                        break
                    for h in range(NH):
                        t.take(la_att)
                        dst = pg3(L_ATT, NH)[:, h, :].rearrange("p (c t) -> p c t", t=C)
                        src = ps[:, 2 + h, :].rearrange("p (c t) -> p c t", t=C)
                        if n == 0:
                            tt(dst, src, tt_mask, mul, la_used)
                        else:
                            v(dve.copy_predicated(dst, m_level(n - 1).bitcast(U16).unsqueeze(1).broadcast_to([P, NC, C]), src), la_used)
                t.take(la_k)
                v(dve.memset(pg(L_S), 0.0), s_ready)
                for c in range(NC):
                    state_update(pg3(L_S, NH, C), lambda h, c: pg3(L_B, NH)[:, h, (c + 1) * C - 1:(c + 1) * C], c)

            def scan_chunks(dst, src, data0):
                for c in range(NC):
                    q = slice(c * C, (c + 1) * C)
                    v(dve.tensor_tensor_scan(dst[:, q], data0, src[:, q], 0.0, mul, add))

            def router(l):
                sc, cand, eq = pg3(R_SC, 16, P), pg3(R_CAND, 8, 256), pg(R_EQ, 4)
                tmp, tmp2 = pg3(R_TMP, 4, P), pg3(R_TMP + 1, 4, 256)
                m0, m1, m2, m3 = (pg(R_SM + k) for k in range(4))
                top_s = m0[:, 0:256].rearrange("p (h k) -> p h k", k=TK)
                top_i = m0[:, 256:512].bitcast(U32).rearrange("p (h k) -> p h k", k=TK)
                top_f = m1[:, 0:256]
                best_s = m1[:, 256:384].rearrange("p (h k) -> p h k", k=TK)
                best_u = m1[:, 384:512].bitcast(U32)
                rank_f = [m2[:, 0:P], m2[:, P:2 * P]]
                rank_u = [m2[:, 2 * P:3 * P].bitcast(U32), m2[:, 3 * P:4 * P].bitcast(U32)]
                e, total = m3[:, 0:P], m3[:, P:P + 8]

                def top16(lots):
                    at = [0] * len(lots)
                    steps = (lambda x, w, s, i: dve.max(s[:, 0:8], x),
                             lambda x, w, s, i: dve.max_index(i[:, 0:8], s[:, 0:8], x),
                             lambda x, w, s, i: dve.match_replace(w, s[:, 0:8], x, BIG),
                             lambda x, w, s, i: dve.max(s[:, 8:16], w),
                             lambda x, w, s, i: dve.max_index(i[:, 8:16], s[:, 8:16], w))
                    for n, step in enumerate(steps):
                        for k, lot in enumerate(lots):
                            if n:
                                dve.wait_ge(dve_step, at[k])
                            t.tell(step(*lot), dve_step)
                            at[k] = t.put[dve_step]

                def settle():
                    dve.wait_ge(dve_step, t.put[dve_step])

                for tile in range(NC):
                    t.take(sc_evac)
                    sel = pg(R_SEL + tile)
                    for q in range(0, 16, 4):
                        top16([(sc[:, q + k, :], tmp[:, k, :], top_s[:, q + k, :], top_i[:, q + k, :]) for k in range(4)])
                        settle()
                    v(dve.tensor_copy(top_f, m0[:, 256:512].bitcast(U32)), sc_used)
                    ts4 = m0[:, 0:256].rearrange("p (h s k) -> p h s k", s=2, k=TK)
                    tf4 = top_f.rearrange("p (h s k) -> p h s k", s=2, k=TK)
                    tt(pg(R_CAND, 4).rearrange("p (h a b) -> p h a b", a=TK, b=TK),
                       ts4[:, :, 0, :].unsqueeze(3).broadcast_to([P, PH, TK, TK]),
                       ts4[:, :, 1, :].unsqueeze(2).broadcast_to([P, PH, TK, TK]), add)
                    bu = best_u.rearrange("p (h k) -> p h k", k=TK)
                    for q in range(0, PH, 4):
                        top16([(cand[:, q + k, :], tmp2[:, k, :], best_s[:, q + k, :], bu[:, q + k, :]) for k in range(4)])
                        settle()
                    tt(e.rearrange("p (h k) -> p h k", k=TK), best_s, best_s[:, :, 0:1].broadcast_to([P, PH, TK]), sub, best_ready)
                    v(dve.tensor_scalar(rank_u[0], best_u, 4, None, ALU.logical_shift_right))
                    v(dve.tensor_scalar(rank_u[1], best_u, 15, None, ALU.bitwise_and))
                    for k in range(2):
                        v(dve.tensor_copy(rank_f[k], rank_u[k]))
                        eq3 = eq.rearrange("p (r a) -> p r a", a=TK)
                        eq4 = eq.rearrange("p (h r a) -> p h r a", r=TK, a=TK)
                        tt(eq3, iota[:, 0:TK].unsqueeze(1).broadcast_to([P, P, TK]), rank_f[k].unsqueeze(2).broadcast_to([P, P, TK]), ALU.is_equal)
                        tt(eq4, eq4, tf4[:, :, k, :].unsqueeze(2).broadcast_to([P, PH, TK, TK]), mul)
                        v(dve.tensor_reduce(sel[:, k * P:(k + 1) * P], eq3, AX.X, add))
                    t.take(best_exp)
                    e3 = e.rearrange("p (h k) -> p h k", k=TK)
                    v(dve.tensor_reduce(total, e3, AX.X, add))
                    v(dve.reciprocal(total, total))
                    tt(sel[:, 2 * P:3 * P].rearrange("p (h k) -> p h k", k=TK), e3, total.unsqueeze(2).broadcast_to([P, PH, TK]), mul, sel_ready)

            def experts(l):
                hb, ha = pg3(OH_B, 16, P), pg3(OH_A, 16, P)
                it, jt, wt = (pg(IJW + k) for k in range(3))
                dve.wait_ge(selt_evac, NC * (l + 1))
                with dve.Fori(0, T // 16) as i:
                    for u in range(4):
                        dve.wait_ge(outer_done, i * 4 + (l * n_unit + u + 1))
                        for k in range(UNIT):
                            s = UNIT * u + k
                            n = i * 16 + s
                            dve.tensor_scalar(hb[:, s, :], iota, jt[:, bass.ds(n, 1)], wt[:, bass.ds(n, 1)], ALU.is_equal, mul)
                            ins = dve.tensor_scalar(ha[:, s, :], iota, it[:, bass.ds(n, 1)], None, ALU.is_equal)
                        ins.then_inc(hot_ready, 1)
                n0, g0 = l * NK, l * n_grp

                def split_keys(g):
                    for s in range(GRP):
                        dve.wait_ge(u_hi, g * GRP + (n0 + s + 1))
                        dve.tensor_tensor(hf(S_ULO + 2 * s, 2), pg(RING + 2 * s, 2), hf(S_UHI + 2 * s, 2).bitcast(F32), sub).then_inc(u_split, 1)

                def group(g, last):
                    for b in range(GRP):
                        dve.wait_ge(v_hi, g * GRP + (n0 + b + 1))
                        dve.tensor_tensor(hf(S_VLO + 2 * b, 2), pg(V_RAW + 2 * b, 2), hf(S_VHI + 2 * b, 2).bitcast(F32), sub).then_inc(v_split, 1)
                        if b == 0:
                            dve.wait_ge(gate_loaded, g * 64 + 64 * (g0 + 1))
                        dve.wait_ge(gelu_ready, g * GRP + (n0 + b + 3))
                        dve.tensor_tensor(pg(G_RING + b), pg(G_RING + b), pg(GELU + b % 2), mul).then_inc(c_ready, 1)
                        dve.wait_ge(c_hi, g * GRP + (n0 + b + 1))
                        dve.tensor_tensor(hf(S_CLO + b), pg(G_RING + b), hf(S_CHI + b).bitcast(F32), sub).then_inc(coef_ready, 1)
                    if not last:
                        split_keys(g + 1)
                    for m in range(8):
                        dve.wait_ge(mix_done, g * 8 + (g0 * 8 + m + 2))
                        if m == 0:
                            dve.wait_ge(acc_done, g * 8 + (g0 * 8 + 4))
                        dve.tensor_tensor(pg(XT + m), pg(XT + m), ps[:, 2 + m % 4, :], add).then_inc(acc_done, 1)

                split_keys(0)
                with dve.Fori(0, n_grp - 1) as g:
                    group(g, False)
                group(n_grp - 1, True)
                dve.wait_ge(acc_done, (g0 + n_grp) * 8 + 4)

            v(dve.memset(cols[:, :], 0.0))
            v(dve.memset(eps_c, EPS))
            v(dve.memset(ones[:, :], 1.0), ones_ready)
            for k in range(4):
                v(dve.memset(ps[:, 2 + k, 0:1], 0.0), acc_done)
            for k in range(2):
                v(dve.memset(ps[:, 2, 0:1], 0.0), c_ready)
            dve.wait_ge(c_loaded, 32)
            for l in range(L):
                j0 = l * JOBS
                a_in, c_in = pg3(A_IN, 12, T + 3), pg3(C_IN, 4, T + 3)
                t.take(norm_root)
                t.got[norm_root] -= 1
                v(dve.memset(a_in[:, :, 0:3], 0.0))
                v(dve.memset(c_in[:, :, 0:3], 0.0))
                params(l)
                norm("norm_mix")
                for m in range(4):
                    dve.wait_ge(evac_done, j0 + m + 1)
                    conv(c_in[:, m, :], lambda k: par("conv_c", 4 * m + k), pg(C_X + m), par("conv_cb", m), xc_ready)
                for m in range(12):
                    if m == 4:
                        dve.wait_ge(cgate_evac, 4 * (l + 1))
                        for g in range(4):
                            ts(pg(C_R + g), pg(C_R + g), lamc[:, g:g + 1], None, mul, None, loga_ready if g == 3 else None)
                        t.take(cexp_ready)
                        tt(pg(C_R, 4), pg(C_A, 4), pg(C_A, 4), mul)
                        stt(pg(C_R, 4), pg(C_R, 4), 1.0, pg(YT + 12, 4), add, mul, cm_ready)
                        tt(pg(C_I, 4), pg(C_I, 4), pg(C_X, 4), mul)
                        t.take(csqrt_ready)
                        tt(pg(C_I, 4), pg(C_I, 4), pg(C_R, 4), mul)
                        for g in range(4):
                            v(dve.tensor_tensor_scan(pg(C_X + g), pg(C_A + g), pg(C_I + g), 0.0, mul, add))
                        tt(pg(YT + 8, 4), pg(YT + 8, 4), pg(C_X, 4), mul, y_ready)
                        v(dve.memset(pg(D_K, 4), 0.0), c_done)
                    dve.wait_ge(evac_done, j0 + 8 + m + 1)
                    conv(a_in[:, m, :], lambda k: par("conv_a", 4 * m + k), pg(A_Q + m), None, aconv_ready)
                row_g, row_t = (mem(a * T, (a + 1) * T, slice(0, 4)) for a in (A_ROWG, A_S))
                t.take(sp_ln)
                stt(row_g, row_g, 0.0, row_t, ALU.max, add)
                ts(row_t, row_g, alog_e[0:4], -1.0, mul, mul)
                for c in range(NC):
                    q = slice(c * C, (c + 1) * C)
                    v(dve.tensor_tensor_scan(row_g[:, q], ones[0:4, :], row_t[:, q], 0.0, mul, add), rows_done if c == NC - 1 else None)
                for m in range(8):
                    t.take(aroot_ready)
                    v(dve.reciprocal(pg(A_MS + m % 4), pg(A_MS + m % 4)))
                    stt(pg(A_Q + m), pg(A_Q + m), P ** -0.5 if m < 4 else 1.0, pg(A_MS + m % 4), mul, mul, qk_ready if m in (3, 7) else None)
                t.take(col_done)
                v(dve.tensor_copy(cols[:, 20:52], ps[:, 6, 0:32]))
                t.take(bc_done)
                t.take(expg_ready)
                for h in range(NH):
                    for c in range(NC):
                        ts(chunks(A_DEC)[:, h * NC + c, :], ps[:, 2 + h, c * C:(c + 1) * C], gct[:, c * NH + h:c * NH + h + 1], 0.0, sub, ALU.min)
                last = ps[:, 2:6, C - 1:T:C]
                tt(kdc.rearrange("p (h c) -> p h c", h=NH), last, gct.rearrange("p (c h) -> p h c", h=NH), sub)
                v(dve.tensor_copy(glc.rearrange("p (h c) -> p h c", h=NH), last), dec_in)
                v(dve.memset(tmpc, 0.0), bc_used)
                t.take(dec_exp)
                tt(chunks(A_DEC), chunks(A_DEC), m_ge.unsqueeze(1).broadcast_to([P, 16, C]), mul)
                for h in range(NH):
                    t.take(prod_done)
                    tt(pg(A_ATT + h), ps[:, 2 + h, :], pg(A_DEC + h), mul, prod_used)
                for h in range(NH):
                    t.take(prod_done)
                    tt(pg(A_DEC + h), ps[:, 2 + h, :], pg(A_DEC + h), mul, prod_used)
                t.take(bc_done)
                tt(pg(A_DEC, 4), pg(A_DEC, 4), ps[:, 2:6, :], mul)
                tt(pg(A_Q, 4), pg(A_Q, 4), pg(A_EXPG, 4), mul)
                tt(pg(A_K, 4), pg(A_K, 4), pg(A_EXPG, 4), mul)
                tt(pg(A_K, 4), pg(A_K, 4), ps[:, 2:6, :], mul)
                for a in (A_X, A_XT):
                    v(dve.tensor_copy(chunks(a), ident.unsqueeze(1).broadcast_to([P, 16, C])), amat_ready if a == A_XT else None)
                for n in range(7):
                    for b in range(NH):
                        t.take(lev_d)
                        tt(pg(A_X + b), pg(A_X + b), ps[:, 6, :], sub)
                        tt(pg(A_XT + b), pg(A_XT + b), ps[:, 7, :], sub, lev_x)
                v(dve.memset(pg(A_S), 0.0), s_ready)
                for c in range(NC):
                    t.take(rs_done)
                    tt(pg3(A_R, NH, C), pg3(A_BV, NH)[:, :, c * C:(c + 1) * C], ps[:, 2, :].rearrange("p (h t) -> p h t", h=NH), sub, r_ready)
                    state_update(pg3(A_S, NH, C), lambda h, c: glc[:, h * NC + c:h * NC + c + 1], c)
                head_norm(A_V, 0, "gdn_norm")
                v(dve.memset(pg(D_K, 4), 0.0), dk_clear)
                t.take(dgate_done)
                for m in range(2):
                    ts(pg(D_F + m), ps[:, 2 + m, :], par("gla_b", m), -1.0, add, mul, sp_in if m else None)
                t.take(sp_ln)
                stt(pg(D_F, 2), pg(D_F, 2), 0.0, pg(L_E, 2), ALU.max, add)
                ts(pg(D_F, 2), pg(D_F, 2), -1.0 / 16, None, mul)
                ts(pg(B_Q, 4), pg(B_Q, 4), P ** -0.5, None, mul)
                t.take(la_sig)
                for h in range(NH):
                    ts(pg(LB_K + h), pg(LB_K + h), lb1[:, h:h + 1], None, mul)
                    ts(pg(B_F + h), pg(B_F + h), lb1[:, h:h + 1], lbc[:, h:h + 1], mul, add)
                ts(pg(B_F, 4), pg(B_F, 4), LN_FLOOR, None, ALU.max, None, la_lnin)
                t.take(la_ln)
                for h in range(NH):
                    scan_chunks(pg(L_B + h), pg(B_F + h), ones[:, :])
                linear(B_Q, LB_K, B_V)
                head_norm(L_O, 4, "hgrn_norm")
                for h in range(NH):
                    scan_chunks(pg(L_B + h), pg(D_F + h // 2), ones[:, :])
                linear(D_Q, D_K, D_V)
                head_norm(L_O, 12, "gla_norm")
                for m in range(8):
                    dve.wait_ge(block_done, l * N_STREAM + N_IN + 2 * m + 2)
                    tt(pg(XT + m), pg(XT + m), ps[:, 6 + m % 2, :], add, op_used)
                v(dve.memset(tmpc, 0.0), x_ready)
                norm("norm_ffn")
                router(l)
                experts(l)
            norm("norm_final")

        @block.gpsimd
        def _(pool):
            t = Tally(pool)
            pool.wait_ge(c_loaded, 32)

            def linear(k):
                for n in range(1, 9):
                    t.take(la_e)
                    t.take(la_att, NH)
                    t.done(pool.tensor_tensor(pg(L_KS, 4), pg(k, 4), pg(L_E, 4), ALU.mult), la_k)

            for l in range(L):
                t.take(amat_ready)
                for n in range(7):
                    for b in range(NH):
                        if n:
                            t.take(lev_p)
                        t.done(pool.tensor_tensor(pg(A_MS + b).rearrange("p (c t) -> p c t", t=C),
                                                  pg(A_DEC + b).rearrange("p (c t) -> p c t", t=C),
                                                  m_level(n).unsqueeze(1).broadcast_to([P, NC, C]), ALU.mult), lev_masked)
                t.take(lev_p, NH)
                linear(LB_K)
                linear(D_K)
                t.take(h_hi)
                t.done(pool.tensor_tensor(hf(S_HLO, KC), pg(HT, KC), hf(S_HHI, KC).bitcast(F32), ALU.subtract), h_split)


def constants():
    j, i = np.arange(P)[:, None], np.arange(P)[None, :]
    f = np.concatenate([np.eye(P), np.broadcast_to(i, (P, P))], 1).astype(np.float32)
    masks = [(j // (2 * s) == i // (2 * s)) & (j // s % 2 == 0) & (i // s % 2 == 1) for s in LEVELS] + [i >= j]
    return f, np.concatenate(masks, 1).astype(mybir.dt.np(BF16))


def lay_out(a):
    def blocks(w):
        r, c = w.shape
        return w.reshape(r // P, P, c // P, P).transpose(2, 1, 0, 3).reshape(c // P, P, -1)

    def columns(p):
        return p.reshape(-1, P).T

    stream, pcol, small, wgate = [], [], [], []
    for l in range(L):
        w = a["w_in"][l]
        o = np.cumsum([0, 512, 512, 512, 512, 4, 4, 512, 512, 512, 512, 512, 512, 256, 256, 512, 512, 16])
        aq, ak, av, az, aa, ab, bq, bf, bi, bg, cx, cg, dq, dk, dv, dg, dlr = (w[:, o[k]:o[k + 1]] for k in range(17))

        def tokens(v):
            return v.reshape(4, 2, P, T).transpose(0, 2, 1, 3).reshape(4, P, -1)

        stream += [blocks(m) for m in (cx, cg, aq, ak, av, az, bq, bg, bf)] + [tokens(bi)]
        stream += [blocks(m) for m in (dq, dk, dg)] + [tokens(dv)]
        wo = blocks(a["w_out"][l]).reshape(8, P, 2, D).transpose(0, 2, 1, 3).reshape(16, P, D)
        stream += [wo, blocks(a["peer_w_q"][l])]
        stream.append(a["peer_u"][l].reshape(NK, P, KC, P).transpose(0, 3, 2, 1).reshape(NK, P, D))
        rows = np.zeros((D, 96), np.float32)
        rows[:, 0:4], rows[:, 32:36], rows[:, 64:80] = aa, ab, dlr
        small.append(np.concatenate([rows.reshape(KC, P, 96).transpose(1, 0, 2).reshape(P, -1)] +
                                    [a[k][l].transpose(1, 0, 2).reshape(P, -1) for k in ("lru_w_a", "lru_w_x")], 1))
        wgate.append(a["gla_w_gate"][l])
        c = np.zeros((P, NPC), np.float32)
        for name, val in (("norm_mix", columns(a["norm_mix"][l])), ("norm_ffn", columns(a["norm_ffn"][l])),
                          ("conv_a", a["gdn_conv_w"][l].reshape(4, 12, P).transpose(2, 1, 0).reshape(P, 48)),
                          ("gdn_norm", columns(a["gdn_norm"][l])), ("hgrn_norm", columns(a["hgrn_norm"][l])),
                          ("gla_norm", columns(a["gla_norm"][l])),
                          ("conv_c", a["lru_conv_w"][l].reshape(4, 4, P).transpose(2, 1, 0).reshape(P, 16)),
                          ("conv_cb", columns(a["lru_conv_b"][l])), ("b_a", columns(a["lru_b_a"][l])),
                          ("b_x", columns(a["lru_b_x"][l])), ("lam", columns(a["lru_lambda"][l])),
                          ("gla_b", columns(a["gla_b_gate"][l])), ("norm_final", columns(a["norm_final"]))):
            c[:, PC[name][0]:PC[name][0] + PC[name][1]] = val
        for k in range(L):
            at = PC["lb"][0] + 4 * k
            c[:, at:at + 4] = columns(a["hgrn_lb_logits"][k])
        c[0:4, PC["a_log"][0]], c[0:4, PC["dt"][0]] = a["gdn_a_log"][l], a["gdn_dt_bias"][l]
        pcol.append(c)
    const_f, const_m = constants()
    sk = a["peer_sub_keys"].reshape(L, 16, NK, P).transpose(0, 3, 1, 2).reshape(L, P, 16 * NK)
    return {
        "x": a["x"][0].T.reshape(KC, P, T).transpose(1, 0, 2).reshape(P, KC * T),
        "wstream": np.concatenate(stream, 0), "pcol": np.stack(pcol), "small": np.stack(small),
        "wgate": np.stack(wgate), "skeys": sk, "vexp": a["peer_v"].reshape(L * NK // GRP, GRP, P, D),
        "const_f": const_f, "const_m": const_m,
    }


def kernel(**inputs):
    import concourse.bacc as bacc
    from concourse.bass_utils import run_bass_kernel_spmd

    arrays = {k: np.ascontiguousarray(v) for k, v in lay_out({k: np.asarray(v) for k, v in inputs.items()}).items()}
    nc = bacc.Bacc("TRN2", target_bir_lowering=False, num_devices=1)
    aps = {k: nc.dram_tensor(f"in_{k}", v.shape, mybir.dt.from_np(v.dtype), kind="ExternalInput").ap() for k, v in arrays.items()}
    out = nc.dram_tensor("out_0", (P, KC * T), F32, kind="ExternalOutput").ap()
    build_program(nc, out=out, **aps)
    r = run_bass_kernel_spmd(nc, [{f"in_{k}": v for k, v in arrays.items()}], core_ids=[0])
    y = np.asarray(r.results[0]["out_0"])
    return y.reshape(P, KC, T).transpose(2, 1, 0).reshape(1, T, D)
```

```python
from contextlib import ExitStack

import numpy as np

import concourse.bass as bass
from concourse import mybir

F32 = mybir.dt.float32
F32R = mybir.dt.float32r
BF16 = mybir.dt.bfloat16
U16 = mybir.dt.uint16
U32 = mybir.dt.uint32
ALU = mybir.AluOpType
ACT = mybir.ActivationFunctionType
AX = mybir.AxisListType

P = 128
T = 512
D = 1024
L = 2
KC = D // P
C = P
NC = T // C
NH = 4
NM = 2 * D // P
EPS = 1e-6
PH, NK, TK = 8, 128, 16
LEVELS = [1 << n for n in range(7)]
BIG = -3.0e38
LN_FLOOR = 2.0 ** -63

XT, HT, RING, YT = 0, 8, 16, 24
NPAGES = 101
RING_SLOTS = 4
C_IN, C_X, C_R, C_I, C_A, SMALL = 89, 67, 71, 75, 79, 83
A_IN, A_Q, A_K, A_V, A_ROWG, A_ROWB, A_EXPG = 40, 53, 57, 61, 65, 66, 67
A_DEC, A_ATT, A_X, A_XT, A_MS, A_R, A_P, A_KD, A_BV, A_S, A_VN = 71, 75, 40, 44, 48, 52, 67, 79, 83, 87, 88
LB_K, L_B, L_E, L_QS, L_KS, L_ATT, L_KD, L_O, L_S = 40, 44, 48, 53, 57, 61, 67, 71, 66
L_E2, L_QS2, L_KS2 = (L_E, L_KD), (L_QS, L_O), (L_KS, 93)
D_QS2 = (L_QS, 97)
B_SQ, B_ROOT = 89, 40
B_Q, B_F, B_V = 89, 93, 97
D_Q, D_K, D_F, D_V = 75, 79, 83, 85
R_Q, R_SK, R_SC, R_CAND, R_EQ, R_SM, R_SEL, R_TMP = 24, 40, 44, 48, 52, 56, 60, 64
G_RING, V_RAW, GELU, IJW = 8, 24, 32, 12
OH_B, OH_A, STAGE = 40, 44, (24, 48)
EARLY_OUT, EARLY_IN = 8, 12
SPLIT = 40
S_EARLY = 27
S_UHI, S_ULO, S_VHI, S_VLO, S_CHI, S_CLO, S_HHI, S_HLO = 27, 31, 0, 8, 16, 20, 43, 51
UNIT = 4
GRP = 4
N_EARLY = NK // 2
TILE_EARLY = N_EARLY // 2 // (T // 128)
NG = 64

PC = {}
_at = 0
for _name, _n in (("norm_mix", 8), ("norm_ffn", 8), ("conv_a", 48), ("gdn_norm", 1), ("hgrn_norm", 1), ("gla_norm", 1),
                  ("conv_c", 16), ("conv_cb", 4), ("b_a", 4), ("b_x", 4), ("lam", 4), ("gla_b", 2), ("lb", 8),
                  ("a_log", 1), ("dt", 1), ("norm_final", 8)):
    PC[_name] = (_at, _n)
    _at += _n
NPC = _at
OUT_BANKS = (7, 6, 0, 1, 2, 3, 4, 5)
LEV_BANKS = ((6, 7), (0, 1))
N_IN = 44 + 8
N_STREAM = N_IN + 16 + 16 + NK


class Tally:

    def __init__(self, eng):
        self.eng, self.put, self.got = eng, {}, {}

    def tell(self, ins, sem):
        ins.then_inc(sem, 1)
        self.put[sem] = self.put.get(sem, 0) + 1

    def done(self, ins, sem):
        self.tell(ins, sem)
        self.eng.wait_ge(sem, self.put[sem])

    def take(self, sem, n=1):
        self.got[sem] = self.got.get(sem, 0) + n
        self.eng.wait_ge(sem, self.got[sem])


def build_program(nc, x, wstream, pcol, small, wgate, skeys, vexp, const_f, const_m, out):
    with ExitStack() as ctx:
        def sb(name, shape, dt=F32):
            return ctx.enter_context(nc.sbuf_tensor(name, shape, dt))

        sems = {}

        def sem(name):
            sems[name] = ctx.enter_context(nc.semaphore(name))
            return sems[name]

        front = sb("front", [P, SPLIT * T])
        with nc.sbuf_tensor("back", [P, (NPAGES - SPLIT) * T], F32) as back:
            pass
        halves = sb("halves", [P, (NPAGES - SPLIT) * T], F32R)
        cf = sb("cf", [P, 2 * P])
        cm = sb("cm", [P, 8 * P], BF16)
        ones = sb("ones", [P, P])
        pc = sb("pc", [P, NPC])
        wg = sb("wg", [80, 2 * P])
        cols = sb("cols", [P, 96])
        ps = ctx.enter_context(nc.psum_tensor("ps", [P, 8, T], F32))

        def mem(lo, hi, parts=slice(0, P)):
            at = SPLIT * T
            assert hi <= at or lo >= at
            return front[parts, lo:hi] if hi <= at else back[parts, lo - at:hi - at]

        def pg(a, n=1):
            return mem(a * T, (a + n) * T)

        def pg3(a, n, w=T):
            return mem(a * T, a * T + n * w).rearrange("p (n t) -> p n t", t=w)

        def hf(a, n=1):
            return halves[:, a * T:(a + n) * T]

        def pairs(a, n, half):
            if n > len(LEVELS):
                return pg(a, 4)
            w = LEVELS[n - 1]
            return pg(a, 4).rearrange("p (s h t) -> p s h t", h=2, t=w)[:, :, half, :]

        def par(name, k=0, n=1):
            o = PC[name][0] + k
            return pc[:, o:o + n]

        ident = cf[:, 0:P]
        iota = cf[:, P:2 * P]
        m_ge = cm[:, 7 * P:8 * P]

        def m_level(n):
            return cm[:, n * P:(n + 1) * P]

        eps_c, lamc, lbc, lb1, tmpc = cols[:, 0:1], cols[:, 1:5], cols[:, 5:9], cols[:, 9:13], cols[:, 13:17]
        alog_e, one_c = cols[:, 17:18], cols[:, 18:19]
        gct, bct, kdc, glc = cols[:, 20:36], cols[:, 36:52], cols[:, 52:68], cols[:, 68:84]
        lbt = cols[:, 84:96]

        x_loaded, c_loaded, p_loaded, small_loaded, sk_loaded = map(sem, ("x_loaded", "c_loaded", "p_loaded", "small_loaded", "sk_loaded"))
        ring_loaded = [sem(f"ring_loaded{s}") for s in range(RING_SLOTS)]
        out_stored = sem("out_stored")
        act_step, dve_step = sem("act_step"), sem("dve_step")
        x_ready, sq_ready, norm_sum, norm_root, h_ready = map(sem, ("x_ready", "sq_ready", "norm_sum", "norm_root", "h_ready"))
        block_done, evac_done = sem("block_done"), sem("evac_done")
        par_act, par_dve, ones_ready = sem("par_act"), sem("par_dve"), sem("ones_ready")
        tm_evac = sem("tm_evac")
        xc_ready, cgate_done, cgate_evac, loga_ready, cexp_ready, cm_ready, csqrt_ready, c_done = map(
            sem, ("xc_ready", "cgate_done", "cgate_evac", "loga_ready", "cexp_ready", "cm_ready", "csqrt_ready", "c_done"))
        aconv_ready, rows_raw, rows_done = map(sem, ("aconv_ready", "rows_raw", "rows_done"))
        asq_ready, asum_done, aroot_ready, qk_ready = map(sem, ("asq_ready", "asum_done", "aroot_ready", "qk_ready"))
        sp_in, sp_ln = sem("sp_in"), sem("sp_ln")
        bc_done, bc_used, expg_ready, col_done, dec_in, dec_exp = map(
            sem, ("bc_done", "bc_used", "expg_ready", "col_done", "dec_in", "dec_exp"))
        prod_done, prod_used, tr_done, tr_used = map(sem, ("prod_done", "prod_used", "tr_done", "tr_used"))
        amat_ready, lev_masked, lev_p, lev_pc, lev_d, lev_x = map(sem, ("amat_ready", "lev_masked", "lev_p", "lev_pc", "lev_d", "lev_x"))
        rs_done, r_ready, vn_done, vn_ready, o_done, o_used, s_done, s_ready = map(
            sem, ("rs_done", "r_ready", "vn_done", "vn_ready", "o_done", "o_used", "s_done", "s_ready"))
        osq_ready, osum_done, oroot_ready, y_ready = map(sem, ("osq_ready", "osum_done", "oroot_ready", "y_ready"))
        la_sig, la_lnin, la_ln, la_diff, la_e, la_q, la_k, la_att, la_used = map(
            sem, ("la_sig", "la_lnin", "la_ln", "la_diff", "la_e", "la_q", "la_k", "la_att", "la_used"))
        la_ready, dk_clear, dgate_done = sem("la_ready"), sem("dk_clear"), sem("dgate_done")
        sc_done, sc_evac, sc_used, best_ready, best_exp, sel_ready, selt_done, selt_evac = map(
            sem, ("sc_done", "sc_evac", "sc_used", "best_ready", "best_exp", "sel_ready", "selt_done", "selt_evac"))
        hot_ready, outer_done, gate_staged = sem("hot_ready"), sem("outer_done"), sem("gate_staged")
        gate_stored = [sem(f"gate_stored{k}") for k in range(2)]
        gate_loaded, h_hi, h_split = sem("gate_loaded"), sem("h_hi"), sem("h_split")
        early_hi, early_split, early_gelu, early_loaded = map(sem, ("early_hi", "early_split", "early_gelu", "early_loaded"))
        early_stored = [sem(f"early_stored{k}") for k in range(4)]
        keys_loaded = [sem(f"keys_loaded{k}") for k in range(2)]
        values_loaded = [sem(f"values_loaded{k}") for k in range(GRP)]
        v_used = sem("v_used")
        u_hi, u_split, v_hi, v_split, c_ready, c_hi = map(sem, ("u_hi", "u_split", "v_hi", "v_split", "c_ready", "c_hi"))
        gelu_ready, coef_ready, mix_done, acc_done = map(sem, ("gelu_ready", "coef_ready", "mix_done", "acc_done"))
        gates_dram = nc.dram_tensor("gates_dram", (L * T // NG, P, NK * NG), F32, kind="Internal").ap()
        early_dram = nc.dram_tensor("early_dram", (L * N_EARLY, P, T), F32, kind="Internal").ap()

        lowrank = mem(A_ROWG * T, (A_ROWG + 1) * T, slice(64, 80))
        block = ctx.enter_context(nc.Block())

        yT = pg3(YT, NM)
        hT = pg3(HT, KC)
        n_grp = NK // GRP
        n_gran = T // NG
        n_unit = T // UNIT

        def slot(s, w=P):
            return mem((RING + 2 * s) * T, (RING + 2 * s + 2) * T).rearrange("p (k m) -> p k m", m=w)

        def stage(k):
            return pg(STAGE[k], 16).rearrange("p (i n) -> p i n", n=NG)

        @block.sync
        def _(sp):
            t = Tally(sp)
            sp.dma_start(pg(XT, KC), x).then_inc(x_loaded, 16)
            sp.dma_start(cf[:, :], const_f).then_inc(c_loaded, 16)
            sp.dma_start(cm[:, :], const_m).then_inc(c_loaded, 16)
            for l in range(L):
                if l:
                    sp.wait_ge(acc_done, 4 + l * NK // GRP * 8)
                sp.dma_start(pc[:, :], pcol[l]).then_inc(p_loaded, 16)
                sp.dma_start(wg[64:80, :], wgate[l]).then_inc(p_loaded, 16)
                sp.dma_start(pg(SMALL, 4)[:, 0:1792], small[l]).then_inc(small_loaded, 16)
                base = l * N_STREAM
                for n in range(N_IN + 32):
                    k = base + n
                    if k >= RING_SLOTS:
                        sp.wait_ge(block_done, k - RING_SLOTS + 1)
                    sp.dma_start(mem((RING + 2 * (n % 4)) * T, (RING + 2 * (n % 4) + 2) * T), wstream[k]).then_inc(ring_loaded[n % 4], 16)
                    if n == N_IN + 16:
                        t.take(y_ready, 4)
                        sp.dma_start(pg(R_SK, 4), skeys[l]).then_inc(sk_loaded, 16)
                e0 = l * N_EARLY

                def raw_slot(s):
                    return mem((RING + 2 * s) * T, (RING + 2 * s + 2) * T)

                def key_block(at):
                    return wstream[bass.ds(at, 1)].rearrange("a p n -> p (a n)")

                def early(i, at, last=False):
                    for s in range(4):
                        if not last:
                            sp.wait_ge(early_split, i * 4 + (e0 + at + s + 1))
                            sp.dma_start(raw_slot(s), key_block(i * 4 + (base + N_IN + 32 + at + s + 4))).then_inc(ring_loaded[s], 16)
                        sp.wait_ge(early_gelu, i * 4 + (2 + e0 + at + s + 1))
                        sp.dma_start(early_dram[bass.ds(i * 4 + (e0 + at + s), 1)].rearrange("a p n -> p (a n)"), pg(EARLY_OUT + s)).then_inc(early_stored[s], 16)

                def load_keys(g):
                    for s in range(2):
                        sp.dma_start(raw_slot(2 + s), key_block(g * 2 + (base + N_IN + 32 + N_EARLY + s))).then_inc(keys_loaded[s], 16)

                def gate_pair(i, last=False):
                    for k in range(2):
                        if last and k == 1:
                            sp.wait_ge(early_split, e0 + N_EARLY)
                            load_keys(0)
                        early(i * 2, N_EARLY // 2 + 4 * k, last and k == 1)
                        sp.wait_ge(gate_staged, i * (2 * NG // UNIT) + (UNIT + l * n_unit + (k + 1) * NG // UNIT))
                        sp.dma_start(gates_dram[bass.ds(i * 2 + (l * n_gran + k), 1)].rearrange("a p n -> p (a n)"), pg(STAGE[k], 16)).then_inc(gate_stored[k], 16)

                for s in range(4):
                    sp.wait_ge(block_done, base + N_IN + 32 + s - RING_SLOTS + 1)
                    sp.dma_start(raw_slot(s), wstream[base + N_IN + 32 + s]).then_inc(ring_loaded[s], 16)
                with sp.Fori(0, N_EARLY // 8) as i:
                    early(i, 0)
                with sp.Fori(0, n_gran // 2 - 1) as i:
                    gate_pair(i)
                gate_pair(n_gran // 2 - 1, True)

                def load_values(g, b):
                    sp.dma_start(pg(V_RAW + 2 * b, 2), vexp[bass.ds(g * GRP + (l * NK + b), 1)].rearrange("a p d -> p (a d)")).then_inc(values_loaded[b], 16)

                def load_gates(g):
                    src = gates_dram[l * n_gran:(l + 1) * n_gran].rearrange("q j (i n) -> j i q n", n=NG)
                    for b in range(GRP):
                        sp.dma_start(pg(G_RING + b).rearrange("p (q n) -> p q n", n=NG),
                                     src[:, bass.ds(g * GRP + b, 1)].rearrange("j a q n -> j (a q) n")).then_inc(gate_loaded, 16)
                    for b in range(2):
                        sp.dma_start(pg(EARLY_IN + b), early_dram[bass.ds(g * 2 + (e0 + b), 1)].rearrange("a p n -> p (a n)")).then_inc(early_loaded, 16)

                sp.wait_ge(gate_stored[0], 16 * (n_gran // 2) * (l + 1))
                for b in range(GRP):
                    load_values(0, b)
                sp.wait_ge(gate_stored[1], 16 * (n_gran // 2) * (l + 1))
                for k in range(4):
                    sp.wait_ge(early_stored[k], 16 * (N_EARLY // 4) * (l + 1))
                load_gates(0)
                with sp.Fori(0, n_grp - 1) as g:
                    sp.wait_ge(u_split, g * 2 + (e0 + 2))
                    load_keys(g + 1)
                    for b in range(GRP):
                        sp.wait_ge(v_split, g * GRP + (l * NK + b + 1))
                        load_values(g + 1, b)
                    sp.wait_ge(coef_ready, g * GRP + (l * NK + GRP))
                    load_gates(g + 1)
            sp.wait_ge(h_ready, (2 * L + 1) * KC)
            sp.dma_start(out, pg(HT, KC)).then_inc(out_stored, 16)
            sp.wait_ge(out_stored, 16)

        JOBS = 45 + 16

        @block.tensor
        def _(pe):
            t = Tally(pe)
            nblk = [0]
            jobs = [0]
            fresh = [0]

            def norm():
                for k in range(KC):
                    t.take(sq_ready)
                    ins = pe.matmul(ps[:, 7, :], ones[:, :], pg(YT + k), start=k == 0, stop=k == KC - 1)
                t.tell(ins, norm_sum)
                fresh[0] = KC

            def bank():
                if jobs[0] >= 2:
                    t.take(evac_done)
                jobs[0] += 1
                return (jobs[0] - 1) % 2

            def next_slot():
                s = nblk[0] % RING_SLOTS
                pe.wait_ge(ring_loaded[s], 16 * (nblk[0] // RING_SLOTS + 1))
                nblk[0] += 1
                return s

            def project(n):
                for _ in range(n):
                    b, s = bank(), next_slot()
                    for k in range(KC):
                        if fresh[0]:
                            t.take(h_ready)
                            fresh[0] -= 1
                        ins = pe.matmul(ps[:, b, :], slot(s)[:, k, :], hT[:, k, :], start=k == 0, stop=k == KC - 1)
                    ins.then_inc(block_done, 1)

            def project_small():
                b = bank()
                sw = mem(SMALL * T, SMALL * T + 768).rearrange("p (k m) -> p k m", m=96)
                for k in range(KC):
                    ins = pe.matmul(ps[0:96, b, :], sw[:, k, :], hT[:, k, :], start=k == 0, stop=k == KC - 1)
                t.tell(ins, rows_raw)

            def project_tokens():
                for q in range(4):
                    s = next_slot()
                    for k in range(2):
                        for c in range(NC):
                            ins = pe.matmul(ps[:, 2 + c, :], hT[:, 2 * q + k, c * C:(c + 1) * C], slot(s, T)[:, k, :],
                                            start=q == 0 and k == 0, stop=q == 3 and k == 1)
                    ins.then_inc(block_done, 1)
                t.take(tm_evac)

            def group_c():
                sw = mem(SMALL * T + 768, SMALL * T + 1792).rearrange("p (g m) -> p g m", m=P)
                for g in range(4):
                    t.take(xc_ready)
                    if g:
                        t.take(cgate_evac)
                    pe.matmul(ps[:, 6, :], sw[:, g, :], pg(C_X + g), start=True, stop=True)
                    t.tell(pe.matmul(ps[:, 7, :], sw[:, 4 + g, :], pg(C_X + g), start=True, stop=True), cgate_done)
                t.take(cgate_evac)

            def transposes(src):
                for b in range(NH):
                    for c in range(NC):
                        ins = pe.transpose(ps[:, 2 + b, c * C:(c + 1) * C], src[:, b, c * C:(c + 1) * C], ident)
                    t.tell(ins, tr_done)
                t.take(tr_used, 4)

            def group_a():
                qT, kT, vT = pg3(A_Q, NH), pg3(A_K, NH), pg3(A_V, NH)
                for m in range(8):
                    t.take(asq_ready)
                    ins = pe.matmul(ps[:, 6 + m % 2, :], ones[:, :], pg(A_X + m), start=True, stop=True)
                    t.tell(ins, asum_done)
                    if m >= 1:
                        t.take(aroot_ready)
                    if m % 2:
                        project(1)
                t.take(aroot_ready)
                t.take(rows_done)
                for c in range(NC):
                    pe.transpose(ps[:, 6, c * 4:c * 4 + 4], mem(A_ROWG * T + c * C, A_ROWG * T + (c + 1) * C, slice(0, 4)), ident[0:4, 0:4])
                    ins = pe.transpose(ps[:, 6, 16 + c * 4:20 + c * 4], mem(A_ROWB * T + c * C, A_ROWB * T + (c + 1) * C, slice(0, 4)), ident[0:4, 0:4])
                t.tell(ins, col_done)
                for h in range(NH):
                    ins = pe.matmul(ps[:, 2 + h, :], ident[0:4, h:h + 1].broadcast_to([4, P]), mem(A_ROWG * T, (A_ROWG + 1) * T, slice(0, 4)), start=True, stop=True)
                t.tell(ins, bc_done)
                t.take(bc_used)
                t.take(qk_ready, 2)
                for rhs in (qT, kT):
                    for h in range(NH):
                        for c in range(NC):
                            ins = pe.matmul(ps[:, 2 + h, c * C:(c + 1) * C], kT[:, h, c * C:(c + 1) * C], rhs[:, h, c * C:(c + 1) * C], start=True, stop=True)
                        t.tell(ins, prod_done)
                    t.take(prod_used, 4)
                transposes(kT)
                transposes(vT)
                for h in range(NH):
                    ins = pe.matmul(ps[:, 2 + h, :], ident[0:4, h:h + 1].broadcast_to([4, P]), mem(A_ROWB * T, (A_ROWB + 1) * T, slice(0, 4)), start=True, stop=True)
                t.tell(ins, bc_done)
                X, XTr, MS, PP = pg3(A_X, NH), pg3(A_XT, NH), pg3(A_MS, NH), pg3(A_P, NH)
                t.take(amat_ready)
                pe.wait_ge(evac_done, jobs[0])
                x0 = t.got.get(lev_x, 0)
                for n in range(7):
                    for b in range(NH):
                        t.take(lev_masked)
                        if n:
                            pe.wait_ge(lev_x, x0 + NH * (n - 1) + b + 1)
                        for c in range(NC):
                            q = slice(c * C, (c + 1) * C)
                            ins = pe.matmul(ps[:, 2 + b, q], MS[:, b, q], X[:, b, q], start=True, stop=True)
                        t.tell(ins, lev_p)
                    for b in range(NH):
                        t.take(lev_pc)
                        if NH * n + b >= 2:
                            pe.wait_ge(lev_x, x0 + NH * n + b - 1)
                        for c in range(NC):
                            q = slice(c * C, (c + 1) * C)
                            pe.matmul(ps[:, LEV_BANKS[b % 2][0], q], XTr[:, b, q], PP[:, b, q], start=True, stop=True)
                        for c in range(NC):
                            q = slice(c * C, (c + 1) * C)
                            ins = pe.matmul(ps[:, LEV_BANKS[b % 2][1], q], PP[:, b, q], XTr[:, b, q], start=True, stop=True)
                        t.tell(ins, lev_d)
                t.take(lev_x, 7 * NH)
                S, VN, R, ATT, KD = pg3(A_S, NH, C), pg3(A_VN, NH, C), pg3(A_R, NH, C), pg3(A_ATT, NH), pg3(A_KD, NH)
                t.take(s_ready)
                for c in range(NC):
                    q = slice(c * C, (c + 1) * C)
                    for h in range(NH):
                        ins = pe.matmul(ps[:, 2, h * C:(h + 1) * C], kT[:, h, q], S[:, h, :], start=True, stop=True)
                    t.tell(ins, rs_done)
                    t.take(r_ready)
                    for h in range(NH):
                        ins = pe.matmul(ps[:, 3, h * C:(h + 1) * C], XTr[:, h, q], R[:, h, :], start=True, stop=True)
                    t.tell(ins, vn_done)
                    t.take(vn_ready)
                    for h in range(NH):
                        pe.matmul(ps[:, 4, h * C:(h + 1) * C], S[:, h, :], qT[:, h, q], start=True, stop=False)
                        ins = pe.matmul(ps[:, 4, h * C:(h + 1) * C], VN[:, h, :], ATT[:, h, q], start=False, stop=True)
                    t.tell(ins, o_done)
                    for h in range(NH):
                        ins = pe.matmul(ps[:, 5, h * C:(h + 1) * C], KD[:, h, q], VN[:, h, :], start=True, stop=True)
                    t.tell(ins, s_done)
                    t.take(s_ready)
                    t.take(o_used)

            def head_norm(sq=L_E, last=False):
                for h in range(NH):
                    t.take(osq_ready)
                    t.tell(pe.matmul(ps[:, 2 + h, :], ones[:, :], pg(sq + h), start=True, stop=True), osum_done)
                if not last:
                    t.take(oroot_ready, 4)

            def gate_d():
                for m in range(2):
                    ins = pe.matmul(ps[:, 6 + m, :], wg[64:80, m * P:(m + 1) * P], lowrank, start=True, stop=True)
                t.tell(ins, dgate_done)

            def linear(qa, ka, va, qs2):
                qT, kT, QS, KS = pg3(qa, NH), pg3(ka, NH), pg3(L_QS, NH), pg3(L_KS, NH)
                ATT, KD, S, V = pg3(L_ATT, NH), pg3(L_KD, NH), pg3(L_S, NH, C), pg3(va, NC)
                t.take(la_ready)
                for n in range(8):
                    a, b = (kT, qT) if n == 0 else (pg3(L_KS2[n % 2], NH), pg3(qs2[n % 2], NH))
                    if n:
                        t.take(la_q)
                        t.take(la_k)
                    for h in range(NH):
                        if n:
                            t.take(la_used)
                        for c in range(NC):
                            q = slice(c * C, (c + 1) * C)
                            ins = pe.matmul(ps[:, 2 + h, q], a[:, h, q], b[:, h, q], start=True, stop=True)
                        t.tell(ins, la_att)
                t.take(la_used, 4)
                t.take(la_q)
                t.take(la_k)
                transposes(KS)
                t.take(s_ready)
                for c in range(NC):
                    q = slice(c * C, (c + 1) * C)
                    for h in range(NH):
                        pe.matmul(ps[:, 4, h * C:(h + 1) * C], S[:, h, :], QS[:, h, q], start=True, stop=False)
                        ins = pe.matmul(ps[:, 4, h * C:(h + 1) * C], V[:, c, h * C:(h + 1) * C], ATT[:, h, q], start=False, stop=True)
                    t.tell(ins, o_done)
                    for h in range(NH):
                        ins = pe.matmul(ps[:, 5, h * C:(h + 1) * C], KD[:, h, q], V[:, c, h * C:(h + 1) * C], start=True, stop=True)
                    t.tell(ins, s_done)
                    t.take(s_ready)
                    t.take(o_used)

            def out_projection():
                t.take(y_ready, 3)
                pe.wait_ge(evac_done, jobs[0])
                for half in range(2):
                    for m in range(8):
                        if half == 0 and m == 4:
                            t.take(oroot_ready, 4)
                        s = next_slot()
                        for k in range(8):
                            ins = pe.matmul(ps[:, OUT_BANKS[m], :], slot(s)[:, k, :], yT[:, 8 * half + k, :],
                                            start=half == 0 and k == 0, stop=half == 1 and k == 7)
                        ins.then_inc(block_done, 1)
                    if half == 0:
                        t.take(y_ready)

            def halves3(w_hi, w_lo, m_hi, m_lo):
                return (w_hi, m_hi), (w_hi, m_lo), (w_lo, m_hi)

            def keys_times_tokens(bank, hi, lo):
                for k in range(KC):
                    q = slice(k * P, (k + 1) * P)
                    for n, (w, m) in enumerate(halves3(hi[:, q], lo[:, q], hf(S_HHI + k), hf(S_HLO + k))):
                        ins = pe.matmul(ps[:, bank, :], w, m, start=k == 0 and n == 0, stop=k == KC - 1 and n == 2)
                ins.then_inc(block_done, 1)

            def early(l, i, at, s):
                pe.wait_ge(early_split, i * 4 + (l * N_EARLY + at + s + 1))
                pe.wait_ge(early_gelu, i * 4 + (l * N_EARLY + at + s + 1))
                keys_times_tokens(s % 2, hf(S_EARLY + 4 * s, 2), hf(S_EARLY + 4 * s + 2, 2))

            def router(l):
                qT = pg3(R_Q, 16)
                sk = pg3(R_SK, 16, P)
                pe.wait_ge(sk_loaded, 16 * (l + 1))
                pe.wait_ge(evac_done, jobs[0])
                pe.wait_ge(h_split, l + 1)
                for tile in range(NC):
                    if tile:
                        t.take(sc_evac)
                    for hp in range(16):
                        ins = pe.matmul(ps[:, 2 + hp // 4, (hp % 4) * P:(hp % 4 + 1) * P], qT[:, hp, tile * C:(tile + 1) * C], sk[:, hp, :], start=True, stop=True)
                    t.tell(ins, sc_done)
                    with pe.Fori(0, TILE_EARLY // 4) as i:
                        for s in range(4):
                            early(l, i, tile * TILE_EARLY, s)
                t.take(sc_evac)
                for tile in range(NC):
                    t.take(sel_ready)
                    if tile:
                        t.take(selt_evac)
                    for k in range(3):
                        ins = pe.transpose(ps[:, 6, k * P:(k + 1) * P], pg(R_SEL + tile)[:, k * P:(k + 1) * P], ident)
                    t.tell(ins, selt_done)
                t.take(selt_evac)

            def build_gates(l):
                hb, ha = pg3(OH_B, 16, P), pg3(OH_A, 16, P)
                with pe.Fori(0, n_gran) as i:
                    for s in range(4):
                        for u in range(4):
                            pe.wait_ge(hot_ready, i * 16 + (l * n_unit + 4 * s + u + 1))
                            pe.wait_ge(gate_staged, i * 16 + (l * n_unit + 4 * s + u + 1))
                            for k in range(UNIT):
                                ins = pe.matmul(ps[:, 2 + u, k * P:(k + 1) * P], hb[:, UNIT * u + k, :], ha[:, UNIT * u + k, :], start=True, stop=True)
                            ins.then_inc(outer_done, 1)
                        early(l, i, N_EARLY // 2, s)

            def experts(l):
                n0, g0 = l * NK, l * n_grp
                pe.wait_ge(gate_staged, UNIT + (l + 1) * n_unit)
                e0 = l * N_EARLY
                pe.wait_ge(early_gelu, e0 + N_EARLY + 2)
                with pe.Fori(0, n_grp) as g:
                    for s in range(2):
                        pe.wait_ge(u_split, g * 2 + (e0 + s + 1))
                        pe.wait_ge(gelu_ready, g * 2 + (e0 + s + 1))
                        keys_times_tokens(s, hf(S_UHI + 2 * s, 2), hf(S_ULO + 2 * s, 2))

                    def values(m, b):
                        q = slice(m * P, (m + 1) * P)
                        for n, (w, c) in enumerate(halves3(hf(S_VHI + 2 * b, 2)[:, q], hf(S_VLO + 2 * b, 2)[:, q], hf(S_CHI + b), hf(S_CLO + b))):
                            ins = pe.matmul(ps[:, 2 + m % 4, :], w, c, start=b == 0 and n == 0, stop=b == GRP - 1 and n == 2)
                        return ins

                    for m in range(4):
                        if m == 0:
                            pe.wait_ge(v_split, g * GRP + (n0 + GRP - 1))
                            pe.wait_ge(coef_ready, g * GRP + (n0 + GRP - 1))
                        pe.wait_ge(acc_done, g * 8 + (g0 * 8 + m + 1))
                        for b in range(GRP - 1):
                            values(m, b)
                    pe.wait_ge(v_split, g * GRP + (n0 + GRP))
                    pe.wait_ge(coef_ready, g * GRP + (n0 + GRP))
                    for m in range(4):
                        values(m, GRP - 1).then_inc(mix_done, 1)
                    for b in range(GRP):
                        for m in range(4, 8):
                            if b == 0:
                                pe.wait_ge(acc_done, g * 8 + (g0 * 8 + m + 1))
                            ins = values(m, b)
                            if b == GRP - 1:
                                ins.then_inc(mix_done, 1)
                        if b < GRP - 1:
                            ins.then_inc(v_used, 1)
                pe.wait_ge(acc_done, (g0 + n_grp) * 8 + 4)

            pe.wait_ge(c_loaded, 32)
            t.take(ones_ready)
            for k in range(4):
                pe.matmul(ps[:, 6, 0:P], ones[:, :], ones[:, :], start=True, stop=True).then_inc(outer_done, 1)
            for l in range(L):
                norm()
                project(8)
                project(16)
                pe.wait_ge(small_loaded, 16 * (l + 1))
                project_small()
                group_c()
                project(12)
                project_tokens()
                group_a()
                head_norm()
                project(4)
                project_tokens()
                gate_d()
                linear(B_Q, LB_K, B_V, L_QS2)
                head_norm(B_SQ)
                linear(D_Q, D_K, D_V, D_QS2)
                head_norm(last=True)
                out_projection()
                norm()
                project(16)
                router(l)
                build_gates(l)
                experts(l)
                nblk[0] += N_EARLY
            norm()

        @block.scalar
        def _(act):
            t = Tally(act)

            def f(out_, in_, func, sem_=None, **kw):
                t.done(act.activation(out_, in_, func, **kw), sem_ or act_step)

            def norm(l, first, scale=1.0 / D):
                if first and l == 0:
                    act.wait_ge(x_loaded, 16)
                for k in range(KC):
                    if not first:
                        t.take(x_ready)
                    elif l:
                        act.wait_ge(acc_done, 4 + l * n_grp * 8 - KC + k + 1)
                    f(pg(YT + k), pg(XT + k), ACT.Square, sq_ready)
                t.take(norm_sum)
                f(pg(YT + 8), ps[:, 7, :], ACT.Sqrt, norm_root, scale=scale, bias=eps_c)

            jobs = [0]

            def evacs(n, write):
                for m in range(n):
                    t.take(block_done)
                    write(m, ps[:, jobs[0] % 2, :])
                    jobs[0] += 1

            def softplus_tail(z, tmp, sig_):
                f(tmp, z, ACT.Abs)
                f(tmp, tmp, ACT.Exp, scale=-1.0)
                f(tmp, tmp, ACT.Ln, sig_, bias=1.0)

            def params(l):
                act.wait_ge(p_loaded, 32 * (l + 1))
                f(alog_e[0:4], par("a_log")[0:4], ACT.Exp)
                softplus_tail(par("lam", 0, 4), tmpc, par_act)
                t.take(par_dve)
                f(lbt[:, 0:8], lbt[:, 0:8], ACT.Exp, par_act)

            def tokens(dst):
                t.take(block_done, 4)
                f(pg(dst, 4), ps[:, 2:6, :], ACT.Copy, tm_evac)

            def store(dst):
                return lambda m, src: f(pg(dst + m), src, ACT.Copy, evac_done)

            def head_norm(o, sq=L_E, root=L_QS):
                for h in range(NH):
                    f(pg(sq + h), pg(o + h), ACT.Square, osq_ready)
                for h in range(NH):
                    t.take(osum_done)
                    f(pg(root + h), ps[:, 2 + h, :], ACT.Sqrt, oroot_ready, scale=1.0 / P, bias=eps_c)

            def recurrence(o, delta):
                for c in range(NC):
                    q = slice(c * C, (c + 1) * C)
                    if delta:
                        t.take(vn_done)
                        f(pg(A_VN), ps[:, 3, :], ACT.Copy, vn_ready)
                    t.take(o_done)
                    f(pg3(o, NH)[:, :, q], ps[:, 4, :].rearrange("p (h t) -> p h t", h=NH), ACT.Copy, o_used)

            def linear(between=None, sq=L_E, root=L_QS):
                for n in range(1, 9):
                    t.take(la_diff)
                    e = pg(L_E2[n % 2], 4)
                    f(e, e, ACT.Abs)
                    if n == 8:
                        f(pg(L_B, 4), pg(L_B, 4), ACT.Exp)
                    f(e, e, ACT.Exp, la_e, scale=-1.0)
                    if n == 2 and between:
                        between()
                for h in range(NH):
                    t.take(tr_done)
                    f(pg(L_KD + h), ps[:, 2 + h, :], ACT.Copy, tr_used)
                recurrence(L_O, False)
                head_norm(L_O, sq, root)

            t.take(ones_ready)
            for k in range(8):
                f(ps[:, k % 2, k:k + 1], ones[:, 0:1], ACT.Copy, gate_staged if k < 4 else gelu_ready if k < 6 else early_gelu)
            for l in range(L):
                norm(l, True)
                params(l)
                c_in = pg3(C_IN, 4, T + 3)
                evacs(4, lambda m, src: f(c_in[:, m, 3:T + 3], src, ACT.Copy, evac_done))
                evacs(4, lambda m, src: f(pg(YT + 8 + m), src, ACT.Gelu_apprx_tanh, evac_done))
                a_in = pg3(A_IN, 12, T + 3)
                evacs(12, lambda m, src: f(a_in[:, m, 3:T + 3], src, ACT.Copy, evac_done))
                evacs(4, lambda m, src: f(pg(YT + m), src, ACT.Silu, evac_done))
                t.take(rows_raw)
                src = ps[:, jobs[0] % 2, :]
                jobs[0] += 1
                row_g, row_b, row_t = (mem(a * T, (a + 1) * T, slice(0, 4)) for a in (A_ROWG, A_ROWB, A_S))
                f(row_g, src[0:4], ACT.Identity, bias=par("dt")[0:4])
                f(lowrank, src[64:80], ACT.Copy)
                f(row_b, src[32:36], ACT.Sigmoid, evac_done)
                for g in range(4):
                    t.take(cgate_done)
                    f(pg(C_R + g), ps[:, 6, :], ACT.Sigmoid, bias=par("b_a", g))
                    f(pg(C_I + g), ps[:, 7, :], ACT.Sigmoid, cgate_evac, bias=par("b_x", g))
                t.take(loga_ready)
                f(pg(C_A, 4), pg(C_R, 4), ACT.Exp)
                f(pg(YT + 12, 4), pg(C_R, 4), ACT.Tanh, cexp_ready, scale=-1.0)
                t.take(cm_ready)
                f(pg(C_R, 4), pg(C_R, 4), ACT.Sqrt, csqrt_ready)
                softplus_tail(row_g, row_t, sp_ln)
                t.take(c_done)
                for m in range(12):
                    t.take(aconv_ready)
                    f(pg(A_Q + m), pg(A_Q + m), ACT.Silu)
                    t.take(block_done)
                    src = ps[:, jobs[0] % 2, :]
                    jobs[0] += 1
                    if m < 4:
                        f(pg(B_Q + m), src, ACT.Silu, evac_done)
                    elif m < 8:
                        f(pg(YT + m), src, ACT.Silu, evac_done)
                    else:
                        f(pg(B_F + m - 8), src, ACT.Copy, evac_done)
                tokens(B_V)

                def d_gate(m):
                    evacs(1, lambda _, src: f(pg(YT + 12 + m), src, ACT.Silu, evac_done))

                for m in range(8):
                    f(pg(A_X + m), pg(A_Q + m), ACT.Square, asq_ready)
                for m in range(8):
                    t.take(asum_done)
                    if m == 4:
                        t.take(qk_ready)
                    f(pg(A_MS + m % 4), ps[:, 6 + m % 2, :], ACT.Sqrt, aroot_ready, bias=eps_c)
                    if m in (3, 5, 7):
                        d_gate(m // 2 - 1)
                d_gate(3)
                t.take(qk_ready)
                t.take(bc_done)
                f(pg(A_EXPG, 4), ps[:, 2:6, :], ACT.Exp, expg_ready)
                t.take(dec_in)
                f(pg(A_DEC, 4), pg(A_DEC, 4), ACT.Exp)
                f(cols[:, 52:84], cols[:, 52:84], ACT.Exp, dec_exp)
                for dst, scale in ((A_KD, kdc), (A_BV, bct)):
                    for h in range(NH):
                        t.take(tr_done)
                        for c in range(NC):
                            col = scale[:, h * NC + c:h * NC + c + 1] if dst == A_KD else scale[:, c * NH + h:c * NH + h + 1]
                            f(pg3(dst, NH)[:, h, c * C:(c + 1) * C], ps[:, 2 + h, c * C:(c + 1) * C], ACT.Copy,
                              tr_used if c == NC - 1 else None, scale=col)
                t.take(bc_done)
                for n in range(7):
                    for b in range(NH):
                        t.take(lev_p)
                        f(pg(A_P + b), ps[:, 2 + b, :], ACT.Copy, lev_pc)
                recurrence(A_V, True)
                head_norm(A_V)
                f(pg(LB_K, 4), pg(B_F, 4), ACT.Sigmoid, scale=-1.0)
                f(pg(B_F, 4), pg(B_F, 4), ACT.Sigmoid, la_sig)
                t.take(dk_clear)
                for m in range(2):
                    t.take(block_done)
                    src = ps[:, jobs[0] % 2, :]
                    jobs[0] += 1
                    f(pg(D_Q + 2 * m), src, ACT.Copy, scale=64 ** -0.5)
                    f(pg(D_Q + 2 * m + 1), src, ACT.Copy, evac_done, scale=64 ** -0.5)
                for m in range(2):
                    t.take(block_done)
                    src = ps[:, jobs[0] % 2, :]
                    jobs[0] += 1
                    f(pg(D_K + 2 * m)[0:64], src[0:64], ACT.Copy)
                    f(pg(D_K + 2 * m + 1)[64:128], src[64:128], ACT.Copy, evac_done)
                t.take(la_lnin)
                f(pg(B_F, 4), pg(B_F, 4), ACT.Ln, la_ln)
                tokens(D_V)

                def d_decay():
                    t.take(sp_in)
                    softplus_tail(pg(D_F, 2), pg(L_QS, 2), sp_ln)

                linear(d_decay, B_SQ, B_ROOT)
                linear()
                norm(l, False)
                act.wait_ge(h_ready, (2 * l + 2) * KC)
                f(hf(S_HHI, KC), pg(HT, KC), ACT.Copy, h_hi)
                t.got[block_done] += 16
                evacs(16, store(R_Q))

                def scores(tile):
                    t.take(sc_done)
                    if tile:
                        t.take(sc_used)
                    f(pg(R_SC, 4), ps[:, 2:6, :], ACT.Copy, sc_evac)

                n0, g0, k0, e0 = l * NK, l * n_grp, l * N_STREAM + N_IN + 32, l * N_EARLY
                r0 = l * (N_IN + 32 + N_EARLY) + N_IN + 32

                def split_early(s, i, at):
                    act.wait_ge(ring_loaded[s], i * 16 + 16 * ((r0 + at) // 4 + 1))
                    act.activation(hf(S_EARLY + 4 * s, 2), pg(RING + 2 * s, 2), ACT.Copy).then_inc(early_hi, 1)

                def early(i, at, s, first=False, last=False):
                    act.wait_ge(block_done, i * 4 + (k0 + at + s + 1))
                    if not last:
                        split_early(s, i, at + 4)
                    if not first:
                        act.wait_ge(early_stored[s], i * 16 + 16 * (e0 + at) // 4)
                    act.activation(pg(EARLY_OUT + s), ps[:, s % 2, :], ACT.Gelu_apprx_tanh).then_inc(early_gelu, 1)

                act.wait_ge(h_split, l + 1)
                for s in range(4):
                    split_early(s, 0, 0)
                scores(0)
                for tile in range(NC):
                    if tile == 0:
                        for i in range(TILE_EARLY // 4):
                            for s in range(4):
                                early(i, 0, s, first=l == 0 and i == 0)
                    else:
                        with act.Fori(0, TILE_EARLY // 4) as i:
                            for s in range(4):
                                early(i, tile * TILE_EARLY, s)
                    t.take(best_ready)
                    best = pg(R_SM + 3)[:, 0:P]
                    f(best, best, ACT.Exp, best_exp)
                    if tile + 1 < NC:
                        scores(tile + 1)
                t.take(sc_used)
                for tile in range(NC):
                    t.take(selt_done)
                    f(pg3(IJW, 3)[:, :, tile * C:(tile + 1) * C], ps[:, 6, 0:3 * P].rearrange("p (k t) -> p k t", k=3), ACT.Copy, selt_evac)

                def gate_pair(i, first=False, last=False):
                    for k in range(2):
                        if not first:
                            act.wait_ge(gate_stored[k], i * 16 + 16 * (l * n_gran // 2))
                        for s in range(4):
                            for u in range(4):
                                act.wait_ge(outer_done, i * 32 + (UNIT + l * n_unit + 16 * k + 4 * s + u + 1))
                                act.activation(stage(k)[:, :, 16 * s + UNIT * u:16 * s + UNIT * (u + 1)],
                                               ps[:, 2 + u, :].rearrange("p (n i) -> p i n", n=UNIT), ACT.Copy).then_inc(gate_staged, 1)
                            early(i * 2, N_EARLY // 2 + 4 * k, s, last=last and k == 1)

                gate_pair(0, first=l == 0)
                with act.Fori(0, n_gran // 2 - 2) as i:
                    gate_pair(i + 1)
                gate_pair(n_gran // 2 - 1, last=True)

                def split_keys(g):
                    for s in range(2):
                        act.wait_ge(keys_loaded[s], g * 16 + 16 * (g0 + 1))
                        act.wait_ge(block_done, g * 2 + (k0 + N_EARLY + s - 1))
                        act.activation(hf(S_UHI + 2 * s, 2), pg(RING + 2 * (2 + s), 2), ACT.Copy).then_inc(u_hi, 1)

                def split_values(g, b):
                    act.wait_ge(values_loaded[b], g * 16 + 16 * (g0 + 1))
                    act.activation(hf(S_VHI + 2 * b, 2), pg(V_RAW + 2 * b, 2), ACT.Copy).then_inc(v_hi, 1)

                def group(g, last):
                    for b in range(GRP):
                        if b >= 2:
                            act.wait_ge(block_done, g * 2 + (k0 + N_EARLY + b - 1))
                            act.wait_ge(c_ready, g * GRP + (n0 + b - 1))
                            act.activation(pg(GELU + b % 2), ps[:, b % 2, :], ACT.Gelu_apprx_tanh).then_inc(gelu_ready, 1)
                        act.wait_ge(c_ready, g * GRP + (n0 + b + 3))
                        act.activation(hf(S_CHI + b), pg(G_RING + b), ACT.Copy).then_inc(c_hi, 1)
                    if not last:
                        split_keys(g + 1)
                        for b in range(GRP):
                            if b < GRP - 1:
                                act.wait_ge(v_used, g * (GRP - 1) + (g0 * (GRP - 1) + b + 1))
                            else:
                                act.wait_ge(mix_done, g * 8 + (g0 * 8 + 8))
                            split_values(g + 1, b)

                split_keys(0)
                for k in range(2):
                    act.wait_ge(gate_stored[k], 16 * (n_gran // 2) * (l + 1))
                for b in range(GRP):
                    split_values(0, b)
                with act.Fori(0, n_grp - 1) as g:
                    group(g, False)
                group(n_grp - 1, True)
                act.wait_ge(mix_done, (g0 + n_grp) * 8)
                t.got[block_done] = (l + 1) * N_STREAM
            norm(L, True)

        @block.vector
        def _(dve):
            t = Tally(dve)
            mul, add, sub = ALU.mult, ALU.add, ALU.subtract

            def v(ins, sem_=None):
                t.done(ins, sem_ or dve_step)

            def tt(o, a, b, op, sem_=None):
                v(dve.tensor_tensor(o, a, b, op), sem_)

            def ts(o, a, s1, s2, op0, op1=None, sem_=None):
                v(dve.tensor_scalar(o, a, s1, s2, op0, op1) if op1 is not None else dve.tensor_scalar(o, a, s1, s2, op0), sem_)

            def stt(o, a, s, b, op0, op1, sem_=None):
                v(dve.scalar_tensor_tensor(out=o, in0=a, scalar=s, in1=b, op0=op0, op1=op1), sem_)

            def norm(name):
                t.take(norm_root)
                v(dve.reciprocal(pg(YT + 8), pg(YT + 8)))
                for k in range(KC):
                    stt(pg(HT + k), pg(XT + k), par(name, k), pg(YT + 8), mul, mul, h_ready)

            def conv(src, w, dst, bias, sem_):
                if bias is None:
                    ts(dst, src[:, 0:T], w(0), None, mul)
                else:
                    ts(dst, src[:, 0:T], w(0), bias, mul, add)
                for k in range(1, 4):
                    stt(dst, src[:, k:k + T], w(k), dst, mul, add, sem_ if k == 3 else None)

            def params(l):
                dve.wait_ge(p_loaded, 32 * (l + 1))
                lb = [par("lb", 4 * k, 4) for k in range(L)]
                tt(lbt[:, 8:12], lb[0], lb[1], ALU.max)
                tt(lbt[:, 0:4], lb[0], lbt[:, 8:12], sub)
                tt(lbt[:, 4:8], lb[1], lbt[:, 8:12], sub, par_dve)
                t.take(par_act)
                ts(lamc, par("lam", 0, 4), -1.0, 0.0, mul, ALU.max)
                tt(lamc, lamc, tmpc, add)
                ts(lamc, lamc, -8.0, None, mul)
                t.take(par_act)
                tt(lbt[:, 8:12], lbt[:, 0:4], lbt[:, 4:8], add)
                v(dve.reciprocal(lbt[:, 8:12], lbt[:, 8:12]))
                ts(lbc, lbt[:, 4:8], float(l), None, mul)
                tt(lbc, lbc, lbt[:, 8:12], mul)
                ts(lb1, lbc, -1.0, 1.0, mul, add)

            def heads(a, n=NH):
                return pg3(a, n)

            def chunks(a):
                return pg(a, 4).rearrange("p (s t) -> p s t", t=C)

            def norm_head(h, o, y, wname, root=L_QS):
                t.take(oroot_ready)
                v(dve.reciprocal(pg(root + h), pg(root + h)))
                stt(pg(o + h), pg(o + h), par(wname), pg(root + h), mul, mul)
                tt(pg(YT + y + h), pg(YT + y + h), pg(o + h), mul, y_ready if h == NH - 1 else None)

            def head_norm(o, y, wname):
                for h in range(NH):
                    norm_head(h, o, y, wname)

            def state_update(S, col, c):
                t.take(s_done)
                for h in range(NH):
                    stt(S[:, h, :], S[:, h, :], col(h, c), ps[:, 5, h * C:(h + 1) * C], mul, add, s_ready if h == NH - 1 else None)

            def linear(q, qs2, between=None, beside=None):
                tt_mask = ident.unsqueeze(1).broadcast_to([P, NC, C])
                v(dve.memset(pg(L_S), 0.0), la_ready)

                def diff(n):
                    s2 = 2 * LEVELS[min(n, 7) - 1]
                    at = s2 // 2 - 1 if n < 8 else C - 1
                    bv = pg(L_B, 4).rearrange("p (s t) -> p s t", t=s2)
                    ev = pg(L_E2[n % 2], 4).rearrange("p (s t) -> p s t", t=s2)
                    tt(ev, bv, bv[:, :, at:at + 1].broadcast_to([P, 4 * T // s2, s2]), sub, la_diff)

                def collect(n):
                    for h in range(NH):
                        t.take(la_att)
                        dst = pg3(L_ATT, NH)[:, h, :].rearrange("p (c t) -> p c t", t=C)
                        src = ps[:, 2 + h, :].rearrange("p (c t) -> p c t", t=C)
                        if n == 0:
                            tt(dst, src, tt_mask, mul, la_used)
                        else:
                            v(dve.copy_predicated(dst, m_level(n - 1).bitcast(U16).unsqueeze(1).broadcast_to([P, NC, C]), src), la_used)

                diff(1)
                diff(2)
                if between:
                    between()
                collect(0)
                for n in range(1, 9):
                    t.take(la_e)
                    tt(pairs(qs2[n % 2], n, 1), pairs(q, n, 1), pairs(L_E2[n % 2] if n < 8 else L_B, n, 1), mul, la_q)
                    if n > 1:
                        collect(n - 1)
                    if n + 2 < 9:
                        t.take(la_k)
                        diff(n + 2)
                    if beside and n % 2:
                        beside(n // 2)
                t.take(la_k, 2)
                v(dve.memset(pg(L_S), 0.0), s_ready)
                for c in range(NC):
                    state_update(pg3(L_S, NH, C), lambda h, c: pg3(L_B, NH)[:, h, (c + 1) * C - 1:(c + 1) * C], c)

            def scan_chunks(dst, src, data0):
                for c in range(NC):
                    q = slice(c * C, (c + 1) * C)
                    v(dve.tensor_tensor_scan(dst[:, q], data0, src[:, q], 0.0, mul, add))

            def router(l):
                sc, cand, eq = pg3(R_SC, 16, P), pg3(R_CAND, 8, 256), pg(R_EQ, 4)
                tmp, tmp2 = pg3(R_TMP, 4, P), pg3(R_TMP + 1, 4, 256)
                m0, m1, m2, m3 = (pg(R_SM + k) for k in range(4))
                top_s = m0[:, 0:256].rearrange("p (h k) -> p h k", k=TK)
                top_i = m0[:, 256:512].bitcast(U32).rearrange("p (h k) -> p h k", k=TK)
                top_f = m1[:, 0:256]
                best_s = m1[:, 256:384].rearrange("p (h k) -> p h k", k=TK)
                best_u = m1[:, 384:512].bitcast(U32)
                rank_f = [m2[:, 0:P], m2[:, P:2 * P]]
                rank_u = [m2[:, 2 * P:3 * P].bitcast(U32), m2[:, 3 * P:4 * P].bitcast(U32)]
                e, total = m3[:, 0:P], m3[:, P:P + 8]

                def top16(lots):
                    at = [0] * len(lots)
                    steps = (lambda x, w, s, i: dve.max(s[:, 0:8], x),
                             lambda x, w, s, i: dve.max_index(i[:, 0:8], s[:, 0:8], x),
                             lambda x, w, s, i: dve.match_replace(w, s[:, 0:8], x, BIG),
                             lambda x, w, s, i: dve.max(s[:, 8:16], w),
                             lambda x, w, s, i: dve.max_index(i[:, 8:16], s[:, 8:16], w))
                    for n, step in enumerate(steps):
                        for k, lot in enumerate(lots):
                            if n:
                                dve.wait_ge(dve_step, at[k])
                            t.tell(step(*lot), dve_step)
                            at[k] = t.put[dve_step]

                def settle():
                    dve.wait_ge(dve_step, t.put[dve_step])

                for tile in range(NC):
                    t.take(sc_evac)
                    sel = pg(R_SEL + tile)
                    for q in range(0, 16, 4):
                        top16([(sc[:, q + k, :], tmp[:, k, :], top_s[:, q + k, :], top_i[:, q + k, :]) for k in range(4)])
                        settle()
                    v(dve.tensor_copy(top_f, m0[:, 256:512].bitcast(U32)), sc_used)
                    ts4 = m0[:, 0:256].rearrange("p (h s k) -> p h s k", s=2, k=TK)
                    tf4 = top_f.rearrange("p (h s k) -> p h s k", s=2, k=TK)
                    tt(pg(R_CAND, 4).rearrange("p (h a b) -> p h a b", a=TK, b=TK),
                       ts4[:, :, 0, :].unsqueeze(3).broadcast_to([P, PH, TK, TK]),
                       ts4[:, :, 1, :].unsqueeze(2).broadcast_to([P, PH, TK, TK]), add)
                    bu = best_u.rearrange("p (h k) -> p h k", k=TK)
                    for q in range(0, PH, 4):
                        top16([(cand[:, q + k, :], tmp2[:, k, :], best_s[:, q + k, :], bu[:, q + k, :]) for k in range(4)])
                        settle()
                    tt(e.rearrange("p (h k) -> p h k", k=TK), best_s, best_s[:, :, 0:1].broadcast_to([P, PH, TK]), sub, best_ready)
                    v(dve.tensor_scalar(rank_u[0], best_u, 4, None, ALU.logical_shift_right))
                    v(dve.tensor_scalar(rank_u[1], best_u, 15, None, ALU.bitwise_and))
                    for k in range(2):
                        v(dve.tensor_copy(rank_f[k], rank_u[k]))
                        eq3 = eq.rearrange("p (r a) -> p r a", a=TK)
                        eq4 = eq.rearrange("p (h r a) -> p h r a", r=TK, a=TK)
                        tt(eq3, iota[:, 0:TK].unsqueeze(1).broadcast_to([P, P, TK]), rank_f[k].unsqueeze(2).broadcast_to([P, P, TK]), ALU.is_equal)
                        tt(eq4, eq4, tf4[:, :, k, :].unsqueeze(2).broadcast_to([P, PH, TK, TK]), mul)
                        v(dve.tensor_reduce(sel[:, k * P:(k + 1) * P], eq3, AX.X, add))
                    t.take(best_exp)
                    e3 = e.rearrange("p (h k) -> p h k", k=TK)
                    v(dve.tensor_reduce(total, e3, AX.X, add))
                    v(dve.reciprocal(total, total))
                    tt(sel[:, 2 * P:3 * P].rearrange("p (h k) -> p h k", k=TK), e3, total.unsqueeze(2).broadcast_to([P, PH, TK]), mul, sel_ready)

            def experts(l):
                hb, ha = pg3(OH_B, 16, P), pg3(OH_A, 16, P)
                it, jt, wt = (pg(IJW + k) for k in range(3))
                dve.wait_ge(selt_evac, NC * (l + 1))
                with dve.Fori(0, T // 16) as i:
                    for u in range(4):
                        dve.wait_ge(outer_done, i * 4 + (l * n_unit + u + 1))
                        for k in range(UNIT):
                            s = UNIT * u + k
                            n = i * 16 + s
                            dve.tensor_scalar(hb[:, s, :], iota, jt[:, bass.ds(n, 1)], wt[:, bass.ds(n, 1)], ALU.is_equal, mul)
                            ins = dve.tensor_scalar(ha[:, s, :], iota, it[:, bass.ds(n, 1)], None, ALU.is_equal)
                        ins.then_inc(hot_ready, 1)
                n0, g0 = l * NK, l * n_grp

                e0 = l * N_EARLY

                def split_keys(g):
                    for s in range(2):
                        dve.wait_ge(u_hi, g * 2 + (e0 + s + 1))
                        dve.tensor_tensor(hf(S_ULO + 2 * s, 2), pg(RING + 2 * (2 + s), 2), hf(S_UHI + 2 * s, 2).bitcast(F32), sub).then_inc(u_split, 1)

                def split_values(g, b):
                    dve.wait_ge(v_hi, g * GRP + (n0 + b + 1))
                    dve.tensor_tensor(hf(S_VLO + 2 * b, 2), pg(V_RAW + 2 * b, 2), hf(S_VHI + 2 * b, 2).bitcast(F32), sub).then_inc(v_split, 1)

                def group(g, last):
                    for b in range(GRP):
                        if b == 0:
                            dve.wait_ge(gate_loaded, g * 64 + 64 * (g0 + 1))
                            dve.wait_ge(early_loaded, g * 32 + 32 * (g0 + 1))
                        if b >= 2:
                            dve.wait_ge(gelu_ready, g * 2 + (e0 + b + 1))
                        gelu = pg(EARLY_IN + b) if b < 2 else pg(GELU + b % 2)
                        dve.tensor_tensor(pg(G_RING + b), pg(G_RING + b), gelu, mul).then_inc(c_ready, 1)
                        dve.wait_ge(c_hi, g * GRP + (n0 + b + 1))
                        dve.tensor_tensor(hf(S_CLO + b), pg(G_RING + b), hf(S_CHI + b).bitcast(F32), sub).then_inc(coef_ready, 1)
                    if not last:
                        split_keys(g + 1)
                    for m in range(8):
                        if m == 4 and not last:
                            for b in range(GRP - 1):
                                split_values(g + 1, b)
                        dve.wait_ge(mix_done, g * 8 + (g0 * 8 + m + 1))
                        if m == 0:
                            dve.wait_ge(acc_done, g * 8 + (g0 * 8 + 4))
                        dve.tensor_tensor(pg(XT + m), pg(XT + m), ps[:, 2 + m % 4, :], add).then_inc(acc_done, 1)
                    if not last:
                        split_values(g + 1, GRP - 1)

                split_keys(0)
                for b in range(GRP):
                    split_values(0, b)
                with dve.Fori(0, n_grp - 1) as g:
                    group(g, False)
                group(n_grp - 1, True)
                dve.wait_ge(acc_done, (g0 + n_grp) * 8 + 4)

            v(dve.memset(cols[:, :], 0.0))
            v(dve.memset(eps_c, EPS))
            v(dve.memset(ones[:, :], 1.0), ones_ready)
            for k in range(4):
                v(dve.memset(ps[:, 2 + k, 0:1], 0.0), acc_done)
            for k in range(2):
                v(dve.memset(ps[:, 2, 0:1], 0.0), c_ready)
            dve.wait_ge(c_loaded, 32)
            for l in range(L):
                j0 = l * JOBS
                a_in, c_in = pg3(A_IN, 12, T + 3), pg3(C_IN, 4, T + 3)
                t.take(norm_root)
                t.got[norm_root] -= 1
                v(dve.memset(a_in[:, :, 0:3], 0.0))
                v(dve.memset(c_in[:, :, 0:3], 0.0))
                params(l)
                norm("norm_mix")
                for m in range(4):
                    dve.wait_ge(evac_done, j0 + m + 1)
                    conv(c_in[:, m, :], lambda k: par("conv_c", 4 * m + k), pg(C_X + m), par("conv_cb", m), xc_ready)
                for m in range(12):
                    if m == 4:
                        dve.wait_ge(cgate_evac, 4 * (l + 1))
                        for g in range(4):
                            ts(pg(C_R + g), pg(C_R + g), lamc[:, g:g + 1], None, mul, None, loga_ready if g == 3 else None)
                        t.take(cexp_ready)
                        tt(pg(C_R, 4), pg(C_A, 4), pg(C_A, 4), mul)
                        stt(pg(C_R, 4), pg(C_R, 4), 1.0, pg(YT + 12, 4), add, mul, cm_ready)
                        tt(pg(C_I, 4), pg(C_I, 4), pg(C_X, 4), mul)
                        t.take(csqrt_ready)
                        tt(pg(C_I, 4), pg(C_I, 4), pg(C_R, 4), mul)
                        for g in range(4):
                            v(dve.tensor_tensor_scan(pg(C_X + g), pg(C_A + g), pg(C_I + g), 0.0, mul, add))
                        tt(pg(YT + 8, 4), pg(YT + 8, 4), pg(C_X, 4), mul, y_ready)
                        v(dve.memset(pg(D_K, 4), 0.0), c_done)
                    dve.wait_ge(evac_done, j0 + 8 + m + 1)
                    conv(a_in[:, m, :], lambda k: par("conv_a", 4 * m + k), pg(A_Q + m), None, aconv_ready)
                row_g, row_t = (mem(a * T, (a + 1) * T, slice(0, 4)) for a in (A_ROWG, A_S))
                t.take(sp_ln)
                stt(row_g, row_g, 0.0, row_t, ALU.max, add)
                ts(row_t, row_g, alog_e[0:4], -1.0, mul, mul)
                for c in range(NC):
                    q = slice(c * C, (c + 1) * C)
                    v(dve.tensor_tensor_scan(row_g[:, q], ones[0:4, :], row_t[:, q], 0.0, mul, add), rows_done if c == NC - 1 else None)
                for m in range(8):
                    t.take(aroot_ready)
                    v(dve.reciprocal(pg(A_MS + m % 4), pg(A_MS + m % 4)))
                    stt(pg(A_Q + m), pg(A_Q + m), P ** -0.5 if m < 4 else 1.0, pg(A_MS + m % 4), mul, mul, qk_ready if m in (3, 7) else None)
                t.take(col_done)
                v(dve.tensor_copy(cols[:, 20:52], ps[:, 6, 0:32]))
                t.take(bc_done)
                t.take(expg_ready)
                for h in range(NH):
                    for c in range(NC):
                        ts(chunks(A_DEC)[:, h * NC + c, :], ps[:, 2 + h, c * C:(c + 1) * C], gct[:, c * NH + h:c * NH + h + 1], 0.0, sub, ALU.min)
                last = ps[:, 2:6, C - 1:T:C]
                tt(kdc.rearrange("p (h c) -> p h c", h=NH), last, gct.rearrange("p (c h) -> p h c", h=NH), sub)
                v(dve.tensor_copy(glc.rearrange("p (h c) -> p h c", h=NH), last), dec_in)
                v(dve.memset(tmpc, 0.0), bc_used)
                t.take(dec_exp)
                tt(chunks(A_DEC), chunks(A_DEC), m_ge.unsqueeze(1).broadcast_to([P, 16, C]), mul)
                for h in range(NH):
                    t.take(prod_done)
                    tt(pg(A_ATT + h), ps[:, 2 + h, :], pg(A_DEC + h), mul, prod_used)
                for h in range(NH):
                    t.take(prod_done)
                    tt(pg(A_DEC + h), ps[:, 2 + h, :], pg(A_DEC + h), mul, prod_used)
                t.take(bc_done)
                tt(pg(A_DEC, 4), pg(A_DEC, 4), ps[:, 2:6, :], mul)
                tt(pg(A_Q, 4), pg(A_Q, 4), pg(A_EXPG, 4), mul)
                tt(pg(A_K, 4), pg(A_K, 4), pg(A_EXPG, 4), mul)
                tt(pg(A_K, 4), pg(A_K, 4), ps[:, 2:6, :], mul)
                for a in (A_X, A_XT):
                    v(dve.tensor_copy(chunks(a), ident.unsqueeze(1).broadcast_to([P, 16, C])), amat_ready if a == A_XT else None)
                for n in range(7):
                    for b in range(NH):
                        t.take(lev_d)
                        tt(pg(A_X + b), pg(A_X + b), ps[:, LEV_BANKS[b % 2][0], :], sub)
                        tt(pg(A_XT + b), pg(A_XT + b), ps[:, LEV_BANKS[b % 2][1], :], sub, lev_x)
                v(dve.memset(pg(A_S), 0.0), s_ready)
                for c in range(NC):
                    t.take(rs_done)
                    tt(pg3(A_R, NH, C), pg3(A_BV, NH)[:, :, c * C:(c + 1) * C], ps[:, 2, :].rearrange("p (h t) -> p h t", h=NH), sub, r_ready)
                    state_update(pg3(A_S, NH, C), lambda h, c: glc[:, h * NC + c:h * NC + c + 1], c)
                head_norm(A_V, 0, "gdn_norm")
                v(dve.memset(pg(D_K, 4), 0.0), dk_clear)
                ts(pg(B_Q, 4), pg(B_Q, 4), P ** -0.5, None, mul)
                t.take(la_sig)
                for h in range(NH):
                    ts(pg(LB_K + h), pg(LB_K + h), lb1[:, h:h + 1], None, mul)
                    ts(pg(B_F + h), pg(B_F + h), lb1[:, h:h + 1], lbc[:, h:h + 1], mul, add)
                ts(pg(B_F, 4), pg(B_F, 4), LN_FLOOR, None, ALU.max, None, la_lnin)
                t.take(la_ln)
                for h in range(NH):
                    scan_chunks(pg(L_B + h), pg(B_F + h), ones[:, :])

                def d_decay():
                    t.take(dgate_done)
                    for m in range(2):
                        ts(pg(D_F + m), ps[:, 6 + m, :], par("gla_b", m), -1.0, add, mul, sp_in if m else None)
                    t.take(sp_ln)
                    stt(pg(D_F, 2), pg(D_F, 2), 0.0, pg(L_QS, 2), ALU.max, add)
                    ts(pg(D_F, 2), pg(D_F, 2), -1.0 / 16, None, mul)

                linear(B_Q, L_QS2, between=d_decay)
                for h in range(NH):
                    scan_chunks(pg(L_B + h), pg(D_F + h // 2), ones[:, :])
                linear(D_Q, D_QS2, beside=lambda h: norm_head(h, L_O, 4, "hgrn_norm", B_ROOT))
                head_norm(L_O, 12, "gla_norm")
                for m in range(8):
                    dve.wait_ge(block_done, l * N_STREAM + N_IN + 8 + m + 1)
                    tt(pg(XT + m), pg(XT + m), ps[:, OUT_BANKS[m], :], add, x_ready)
                norm("norm_ffn")
                router(l)
                experts(l)
            norm("norm_final")

        @block.gpsimd
        def _(pool):
            t = Tally(pool)
            pool.wait_ge(c_loaded, 32)

            def linear(k):
                for n in range(1, 9):
                    t.take(la_e)
                    if n > 1:
                        t.take(la_att, NH)
                    t.done(pool.tensor_tensor(pairs(L_KS2[n % 2], n, 0), pairs(k, n, 0), pairs(L_E2[n % 2], n, 0), ALU.mult), la_k)
                t.take(la_att, NH)

            for l in range(L):
                t.take(amat_ready)
                for n in range(7):
                    for b in range(NH):
                        if n:
                            t.take(lev_p)
                        t.done(pool.tensor_tensor(pg(A_MS + b).rearrange("p (c t) -> p c t", t=C),
                                                  pg(A_DEC + b).rearrange("p (c t) -> p c t", t=C),
                                                  m_level(n).unsqueeze(1).broadcast_to([P, NC, C]), ALU.mult), lev_masked)
                t.take(lev_p, NH)
                linear(LB_K)
                linear(D_K)
                t.take(h_hi)
                t.done(pool.tensor_tensor(hf(S_HLO, KC), pg(HT, KC), hf(S_HHI, KC).bitcast(F32), ALU.subtract), h_split)
                with pool.Fori(0, N_EARLY // 4) as i:
                    for s in range(4):
                        pool.wait_ge(early_hi, i * 4 + (l * N_EARLY + s + 1))
                        pool.tensor_tensor(hf(S_EARLY + 4 * s + 2, 2), pg(RING + 2 * s, 2), hf(S_EARLY + 4 * s, 2).bitcast(F32),
                                           ALU.subtract).then_inc(early_split, 1)


def constants():
    j, i = np.arange(P)[:, None], np.arange(P)[None, :]
    f = np.concatenate([np.eye(P), np.broadcast_to(i, (P, P))], 1).astype(np.float32)
    masks = [(j // (2 * s) == i // (2 * s)) & (j // s % 2 == 0) & (i // s % 2 == 1) for s in LEVELS] + [i >= j]
    return f, np.concatenate(masks, 1).astype(mybir.dt.np(BF16))


def lay_out(a):
    def blocks(w):
        r, c = w.shape
        return w.reshape(r // P, P, c // P, P).transpose(2, 1, 0, 3).reshape(c // P, P, -1)

    def columns(p):
        return p.reshape(-1, P).T

    stream, pcol, small, wgate = [], [], [], []
    for l in range(L):
        w = a["w_in"][l]
        o = np.cumsum([0, 512, 512, 512, 512, 4, 4, 512, 512, 512, 512, 512, 512, 256, 256, 512, 512, 16])
        aq, ak, av, az, aa, ab, bq, bf, bi, bg, cx, cg, dq, dk, dv, dg, dlr = (w[:, o[k]:o[k + 1]] for k in range(17))

        def tokens(v):
            return v.reshape(4, 2, P, T).transpose(0, 2, 1, 3).reshape(4, P, -1)

        stream += [blocks(m) for m in (cx, cg, aq, ak, av, az, bq, bg, bf)] + [tokens(bi)]
        stream += [blocks(m) for m in (dg, dq, dk)] + [tokens(dv)]
        wo = blocks(a["w_out"][l]).reshape(8, P, 2, D).transpose(2, 0, 1, 3).reshape(16, P, D)
        stream += [wo, blocks(a["peer_w_q"][l])]
        u = a["peer_u"][l].reshape(NK // GRP, 2, GRP // 2, P, KC, P).transpose(1, 0, 2, 5, 4, 3)
        stream.append(u.reshape(NK, P, D))
        rows = np.zeros((D, 96), np.float32)
        rows[:, 0:4], rows[:, 32:36], rows[:, 64:80] = aa, ab, dlr
        small.append(np.concatenate([rows.reshape(KC, P, 96).transpose(1, 0, 2).reshape(P, -1)] +
                                    [a[k][l].transpose(1, 0, 2).reshape(P, -1) for k in ("lru_w_a", "lru_w_x")], 1))
        wgate.append(a["gla_w_gate"][l])
        c = np.zeros((P, NPC), np.float32)
        for name, val in (("norm_mix", columns(a["norm_mix"][l])), ("norm_ffn", columns(a["norm_ffn"][l])),
                          ("conv_a", a["gdn_conv_w"][l].reshape(4, 12, P).transpose(2, 1, 0).reshape(P, 48)),
                          ("gdn_norm", columns(a["gdn_norm"][l])), ("hgrn_norm", columns(a["hgrn_norm"][l])),
                          ("gla_norm", columns(a["gla_norm"][l])),
                          ("conv_c", a["lru_conv_w"][l].reshape(4, 4, P).transpose(2, 1, 0).reshape(P, 16)),
                          ("conv_cb", columns(a["lru_conv_b"][l])), ("b_a", columns(a["lru_b_a"][l])),
                          ("b_x", columns(a["lru_b_x"][l])), ("lam", columns(a["lru_lambda"][l])),
                          ("gla_b", columns(a["gla_b_gate"][l])), ("norm_final", columns(a["norm_final"]))):
            c[:, PC[name][0]:PC[name][0] + PC[name][1]] = val
        for k in range(L):
            at = PC["lb"][0] + 4 * k
            c[:, at:at + 4] = columns(a["hgrn_lb_logits"][k])
        c[0:4, PC["a_log"][0]], c[0:4, PC["dt"][0]] = a["gdn_a_log"][l], a["gdn_dt_bias"][l]
        pcol.append(c)
    const_f, const_m = constants()
    sk = a["peer_sub_keys"].reshape(L, 16, NK, P).transpose(0, 3, 1, 2).reshape(L, P, 16 * NK)
    return {
        "x": a["x"][0].T.reshape(KC, P, T).transpose(1, 0, 2).reshape(P, KC * T),
        "wstream": np.concatenate(stream, 0), "pcol": np.stack(pcol), "small": np.stack(small),
        "wgate": np.stack(wgate), "skeys": sk, "vexp": a["peer_v"].reshape(L * NK, P, D),
        "const_f": const_f, "const_m": const_m,
    }


def kernel(**inputs):
    import concourse.bacc as bacc
    from concourse.bass_utils import run_bass_kernel_spmd

    arrays = {k: np.ascontiguousarray(v) for k, v in lay_out({k: np.asarray(v) for k, v in inputs.items()}).items()}
    nc = bacc.Bacc("TRN2", target_bir_lowering=False, num_devices=1)
    aps = {k: nc.dram_tensor(f"in_{k}", v.shape, mybir.dt.from_np(v.dtype), kind="ExternalInput").ap() for k, v in arrays.items()}
    out = nc.dram_tensor("out_0", (P, KC * T), F32, kind="ExternalOutput").ap()
    build_program(nc, out=out, **aps)
    r = run_bass_kernel_spmd(nc, [{f"in_{k}": v for k, v in arrays.items()}], core_ids=[0])
    y = np.asarray(r.results[0]["out_0"])
    return y.reshape(P, KC, T).transpose(2, 1, 0).reshape(1, T, D)
```
